# Optimizing a Trainium2 kernel written in Bass

```python
import math
import jax, jax.numpy as jnp
from jax import lax
import numpy as np

D_MODEL = 1024
BATCH = 1
SEQ = 512
DEPTH = 1

GDN_HEADS = 4
GDN_HEAD_DIM = 128
GDN_WIDTH = GDN_HEADS * GDN_HEAD_DIM
GDN_CONV = 4
GDN_CHUNK = 64
S5_GROUP = 16
S5_GROUPS = 32
S5_WIDTH = S5_GROUPS * S5_GROUP
S5_STATE = 64
DIFF_HEADS = 4
DIFF_HEAD_DIM = 64
DIFF_V_DIM = 2 * DIFF_HEAD_DIM
DIFF_WIDTH = DIFF_HEADS * DIFF_V_DIM
Q_BLOCK = 128
MIX_WIDTH = GDN_WIDTH + S5_WIDTH + DIFF_WIDTH
IN_SIZES = (GDN_WIDTH, GDN_WIDTH, GDN_WIDTH, GDN_WIDTH, GDN_HEADS, GDN_HEADS,
            S5_WIDTH,
            DIFF_HEADS * 2 * DIFF_HEAD_DIM, DIFF_HEADS * 2 * DIFF_HEAD_DIM, DIFF_WIDTH)
IN_WIDTH = sum(IN_SIZES)
D_FF = 2816
FFN_CONV = 3
EPS = 1e-6


def rms_norm(x, w, eps=EPS):
    xf = x.astype(jnp.float32)
    y = xf * lax.rsqrt(jnp.mean(xf * xf, axis=-1, keepdims=True) + eps)
    return y.astype(x.dtype) * w

def l2norm(x, eps=1e-6):
    xf = x.astype(jnp.float32)
    return xf * lax.rsqrt(jnp.sum(xf * xf, axis=-1, keepdims=True) + eps)

def split_cols(t, sizes):
    offs = np.cumsum(sizes)[:-1].tolist()
    return jnp.split(t, offs, axis=-1)

def causal_dwconv(x, w):
    k = w.shape[0]
    return lax.conv_general_dilated(
        x, w[:, None, :].astype(x.dtype), window_strides=(1,), padding=[(k - 1, 0)],
        dimension_numbers=('NWC', 'WIO', 'NWC'), feature_group_count=x.shape[-1])

def _gdn_chunk_step(state, inp):
    q_n, k_n, u_n, w_n, g_n, attn_n = inp
    v_new = u_n - jnp.einsum('bhck,bhkv->bhcv', w_n, state)
    out = (jnp.einsum('bhck,bhkv->bhcv', q_n * jnp.exp(g_n)[..., None], state)
           + jnp.einsum('bhcs,bhsv->bhcv', attn_n, v_new))
    g_last = g_n[..., -1]
    state = (state * jnp.exp(g_last)[..., None, None]
             + jnp.einsum('bhck,bhcv->bhkv', k_n * jnp.exp(g_last[..., None] - g_n)[..., None], v_new))
    return state, out

def gated_delta_chunked(q, k, v, beta, g):
    b, l, h, dk = q.shape
    dv = v.shape[-1]
    c = GDN_CHUNK
    n = l // c

    def to_chunks(t):
        return t.reshape(b, n, c, h, -1).transpose(0, 3, 1, 2, 4)

    q = to_chunks(q * dk ** -0.5)
    k = to_chunks(k)
    v = to_chunks(v)
    beta = to_chunks(beta[..., None])[..., 0]
    gc = jnp.cumsum(to_chunks(g[..., None])[..., 0], axis=-1)
    incl = jnp.tril(jnp.ones((c, c), dtype=bool))
    strict = jnp.tril(jnp.ones((c, c), dtype=bool), -1)
    diff = gc[..., :, None] - gc[..., None, :]
    decay = jnp.where(incl, jnp.exp(jnp.where(incl, diff, 0.0)), 0.0)
    k_beta = k * beta[..., None]
    lower = jnp.where(strict, jnp.einsum('bhnck,bhnsk->bhncs', k_beta, k) * decay, 0.0)
    eye = jnp.eye(c, dtype=jnp.float32)
    t_inv = lax.linalg.triangular_solve(lower + eye, jnp.broadcast_to(eye, lower.shape),
                                        left_side=True, lower=True, unit_diagonal=True)
    u = t_inv @ (v * beta[..., None])
    w = t_inv @ (k_beta * jnp.exp(gc)[..., None])
    attn = jnp.where(incl, jnp.einsum('bhnck,bhnsk->bhncs', q, k) * decay, 0.0)
    xs = tuple(jnp.moveaxis(t, 2, 0) for t in (q, k, u, w, gc, attn))
    s0 = jnp.zeros((b, h, dk, dv), jnp.float32)
    _, out = lax.scan(_gdn_chunk_step, s0, xs)
    return out.transpose(1, 0, 3, 2, 4).reshape(b, l, h, dv)

def _linear_recurrence_combine(left, right):
    a_i, b_i = left
    a_j, b_j = right
    return a_j * a_i, a_j * b_i + b_j

def s5_mixer(u, lam_re, lam_im, log_dt, b_re, b_im, c_re, c_im, d_skip, w_glu, b_glu):
    f32 = jnp.float32
    b, l, _ = u.shape
    uf = u.astype(f32).reshape(b, l, S5_GROUPS, S5_GROUP)
    lam = lax.complex(jnp.minimum(lam_re.astype(f32), -1e-4), lam_im.astype(f32))
    dt = jnp.exp(log_dt.astype(f32))[:, None]
    lam_bar = jnp.exp(lam * dt)
    b_bar = ((lam_bar - 1.0) / lam)[..., None] * lax.complex(b_re.astype(f32), b_im.astype(f32))
    bu = jnp.einsum('gph,blgh->blgp', b_bar, uf.astype(jnp.complex64))
    a = jnp.broadcast_to(lam_bar, (1, l) + lam_bar.shape)
    _, states = lax.associative_scan(_linear_recurrence_combine, (a, bu), axis=1)
    c = lax.complex(c_re.astype(f32), c_im.astype(f32))
    y = (jnp.real(jnp.einsum('ghp,blgp->blgh', c, states))
         + d_skip.astype(f32).reshape(S5_GROUPS, S5_GROUP) * uf)
    y = jax.nn.gelu(y.reshape(b, l, S5_WIDTH))
    y = y * jax.nn.sigmoid(y @ w_glu.astype(f32) + b_glu.astype(f32))
    return y.astype(u.dtype)

def diff_attention(q, k, v, lam):
    b, l, h, _, dh = q.shape
    nb = l // Q_BLOCK
    qf = (q.astype(jnp.float32) * dh ** -0.5).reshape(b, nb, Q_BLOCK, h, 2, dh).swapaxes(0, 1)
    kf = k.astype(jnp.float32)
    vf = v.astype(jnp.float32)
    key_pos = jnp.arange(l)

    def block(args):
        q_blk, start = args
        s = jnp.einsum('bqhcd,bkhcd->bhcqk', q_blk, kf)
        causal = (start + jnp.arange(Q_BLOCK))[:, None] >= key_pos[None, :]
        p = jax.nn.softmax(jnp.where(causal, s, -jnp.inf), axis=-1)
        a = p[:, :, 0] - lam * p[:, :, 1]
        return jnp.einsum('bhqk,bkhe->bqhe', a, vf)

    starts = jnp.arange(nb, dtype=jnp.int32) * Q_BLOCK
    out = lax.map(block, (qf, starts))
    return out.swapaxes(0, 1).reshape(b, l, h, -1).astype(v.dtype)

def conv_glu_ffn(h, w_up, conv_w, conv_b, w_down):
    u = causal_dwconv(h @ w_up, conv_w) + conv_b
    gate, up = jnp.split(u, 2, axis=-1)
    return (jax.nn.silu(gate) * up) @ w_down

def first_inputs(seed: int = 0) -> dict:
    key = jax.random.key(seed)
    ks = iter(jax.random.split(key, 40))
    f32 = jnp.float32

    def nrm(shape, scale):
        return jax.random.normal(next(ks), shape, f32) * scale

    def gain(shape):
        return 1.0 + 0.01 * jax.random.normal(next(ks), shape, f32)

    x = nrm((BATCH, SEQ, D_MODEL), 1.0)
    attn_norm_w = gain((DEPTH, D_MODEL))
    w_in = nrm((DEPTH, D_MODEL, IN_WIDTH), D_MODEL ** -0.5)
    gdn_conv_w = nrm((DEPTH, GDN_CONV, 3 * GDN_WIDTH), GDN_CONV ** -0.5)
    gdn_a_log = jnp.log(jax.random.uniform(next(ks), (DEPTH, GDN_HEADS), f32, 1.0, 16.0))
    gdn_dt = jnp.exp(jax.random.uniform(next(ks), (DEPTH, GDN_HEADS), f32, math.log(1e-3), math.log(1e-1)))
    gdn_dt_bias = gdn_dt + jnp.log(-jnp.expm1(-gdn_dt))
    gdn_norm_w = gain((DEPTH, GDN_HEAD_DIM))
    s5_lambda_re = -0.5 + nrm((DEPTH, S5_GROUPS, S5_STATE), 0.01)
    s5_lambda_im = jnp.pi * jnp.arange(S5_STATE, dtype=f32) + nrm((DEPTH, S5_GROUPS, S5_STATE), 0.01)
    s5_log_dt = jax.random.uniform(next(ks), (DEPTH, S5_GROUPS), f32, math.log(1e-3), math.log(1e-1))
    s5_b_re = nrm((DEPTH, S5_GROUPS, S5_STATE, S5_GROUP), (2 * S5_GROUP) ** -0.5)
    s5_b_im = nrm((DEPTH, S5_GROUPS, S5_STATE, S5_GROUP), (2 * S5_GROUP) ** -0.5)
    s5_c_re = nrm((DEPTH, S5_GROUPS, S5_GROUP, S5_STATE), S5_STATE ** -0.5)
    s5_c_im = nrm((DEPTH, S5_GROUPS, S5_GROUP, S5_STATE), S5_STATE ** -0.5)
    s5_d = nrm((DEPTH, S5_WIDTH), 1.0)
    s5_w_glu = nrm((DEPTH, S5_WIDTH, S5_WIDTH), S5_WIDTH ** -0.5)
    s5_b_glu = nrm((DEPTH, S5_WIDTH), 0.01)
    s5_norm_w = gain((DEPTH, S5_WIDTH))
    diff_lambda_q1 = nrm((DEPTH, DIFF_HEAD_DIM), 0.1)
    diff_lambda_k1 = nrm((DEPTH, DIFF_HEAD_DIM), 0.1)
    diff_lambda_q2 = nrm((DEPTH, DIFF_HEAD_DIM), 0.1)
    diff_lambda_k2 = nrm((DEPTH, DIFF_HEAD_DIM), 0.1)
    diff_norm_w = gain((DEPTH, DIFF_V_DIM))
    w_out = nrm((DEPTH, MIX_WIDTH, D_MODEL), MIX_WIDTH ** -0.5)
    ffn_norm_w = gain((DEPTH, D_MODEL))
    ffn_w_up = nrm((DEPTH, D_MODEL, 2 * D_FF), D_MODEL ** -0.5)
    ffn_conv_w = nrm((DEPTH, FFN_CONV, 2 * D_FF), FFN_CONV ** -0.5)
    ffn_conv_b = nrm((DEPTH, 2 * D_FF), 0.01)
    ffn_w_down = nrm((DEPTH, D_FF, D_MODEL), D_FF ** -0.5)
    final_norm_w = gain((D_MODEL,))
    return {'x': x, 'attn_norm_w': attn_norm_w, 'w_in': w_in, 'gdn_conv_w': gdn_conv_w,
            'gdn_a_log': gdn_a_log, 'gdn_dt_bias': gdn_dt_bias, 'gdn_norm_w': gdn_norm_w,
            's5_lambda_re': s5_lambda_re, 's5_lambda_im': s5_lambda_im, 's5_log_dt': s5_log_dt,
            's5_b_re': s5_b_re, 's5_b_im': s5_b_im, 's5_c_re': s5_c_re, 's5_c_im': s5_c_im,
            's5_d': s5_d, 's5_w_glu': s5_w_glu, 's5_b_glu': s5_b_glu, 's5_norm_w': s5_norm_w,
            'diff_lambda_q1': diff_lambda_q1, 'diff_lambda_k1': diff_lambda_k1,
            'diff_lambda_q2': diff_lambda_q2, 'diff_lambda_k2': diff_lambda_k2,
            'diff_norm_w': diff_norm_w, 'w_out': w_out, 'ffn_norm_w': ffn_norm_w,
            'ffn_w_up': ffn_w_up, 'ffn_conv_w': ffn_conv_w, 'ffn_conv_b': ffn_conv_b,
            'ffn_w_down': ffn_w_down, 'final_norm_w': final_norm_w}

def first_block(x, attn_norm_w, w_in, gdn_conv_w, gdn_a_log, gdn_dt_bias, gdn_norm_w,
              s5_lambda_re, s5_lambda_im, s5_log_dt, s5_b_re, s5_b_im, s5_c_re, s5_c_im,
              s5_d, s5_w_glu, s5_b_glu, s5_norm_w, diff_lambda_q1, diff_lambda_k1,
              diff_lambda_q2, diff_lambda_k2, diff_norm_w, w_out, ffn_norm_w, ffn_w_up,
              ffn_conv_w, ffn_conv_b, ffn_w_down, final_norm_w):
    f32 = jnp.float32
    b, l, _ = x.shape
    for i in range(DEPTH):
        h = rms_norm(x, attn_norm_w[i])
        g_q, g_k, g_v, g_z, g_b, g_a, s_u, d_q, d_k, d_v = split_cols(h @ w_in[i], IN_SIZES)

        qkv = jax.nn.silu(causal_dwconv(jnp.concatenate([g_q, g_k, g_v], axis=-1), gdn_conv_w[i]))
        g_q, g_k, g_v = (t.reshape(b, l, GDN_HEADS, GDN_HEAD_DIM) for t in jnp.split(qkv, 3, axis=-1))
        beta = jax.nn.sigmoid(g_b.astype(f32))
        log_decay = (-jnp.exp(gdn_a_log[i].astype(f32))
                     * jax.nn.softplus(g_a.astype(f32) + gdn_dt_bias[i].astype(f32)))
        o_gdn = gated_delta_chunked(l2norm(g_q), l2norm(g_k), g_v.astype(f32), beta, log_decay)
        o_gdn = (rms_norm(o_gdn, gdn_norm_w[i].astype(f32))
                 * jax.nn.silu(g_z.astype(f32).reshape(b, l, GDN_HEADS, GDN_HEAD_DIM)))
        o_gdn = o_gdn.reshape(b, l, GDN_WIDTH).astype(x.dtype)

        o_s5 = rms_norm(s5_mixer(s_u, s5_lambda_re[i], s5_lambda_im[i], s5_log_dt[i], s5_b_re[i],
                                 s5_b_im[i], s5_c_re[i], s5_c_im[i], s5_d[i], s5_w_glu[i], s5_b_glu[i]),
                        s5_norm_w[i])

        lam_init = 0.8 - 0.6 * math.exp(-0.3 * i)
        lam = (jnp.exp(jnp.sum(diff_lambda_q1[i].astype(f32) * diff_lambda_k1[i].astype(f32)))
               - jnp.exp(jnp.sum(diff_lambda_q2[i].astype(f32) * diff_lambda_k2[i].astype(f32)))
               + lam_init)
        o_diff = diff_attention(d_q.reshape(b, l, DIFF_HEADS, 2, DIFF_HEAD_DIM),
                                d_k.reshape(b, l, DIFF_HEADS, 2, DIFF_HEAD_DIM),
                                d_v.reshape(b, l, DIFF_HEADS, DIFF_V_DIM), lam)
        o_diff = (rms_norm(o_diff, diff_norm_w[i]) * (1.0 - lam_init)).reshape(b, l, DIFF_WIDTH)

        x = x + jnp.concatenate([o_gdn, o_s5, o_diff], axis=-1) @ w_out[i]

        x = x + conv_glu_ffn(rms_norm(x, ffn_norm_w[i]), ffn_w_up[i], ffn_conv_w[i],
                             ffn_conv_b[i], ffn_w_down[i])
    return rms_norm(x, final_norm_w)


_first_inputs = first_inputs


def first_inputs(seed=0):
    import zlib

    import numpy as np

    out = dict(_first_inputs(seed))
    spreads = {}
    factors = {'attn_norm_w': 5.219,
     'gdn_norm_w': 159.277,
     's5_lambda_re': 200.0,
     's5_b_glu': 64.0,
     's5_norm_w': 200.0,
     'diff_lambda_q2': 3.44,
     'diff_norm_w': 200.0,
     'ffn_norm_w': 138.417,
     'ffn_conv_b': 135.95,
     'final_norm_w': 199.997,
     's5_lambda_im': 29.664,
     's5_log_dt': 31.48,
     's5_b_re': 41.472,
     's5_b_im': 40.552,
     's5_c_re': 42.224,
     's5_c_im': 40.6}
    for name, (base, spread) in spreads.items():
        noise = np.random.default_rng([zlib.crc32(name.encode()), seed]).standard_normal(out[name].shape)
        drawn = base * np.exp(spread * noise) if base else spread * noise
        out[name] = __import__('jax').numpy.asarray(drawn.astype(out[name].dtype))
    for name, factor in factors.items():
        out[name] = (out[name] * factor).astype(out[name].dtype)
    return out


_narrow_inputs = first_inputs


def first_inputs(seed=0):

    out = dict(_narrow_inputs(seed))
    wider = {'gdn_norm_w': 4.79,
     's5_norm_w': 12.0,
     'diff_norm_w': 12.0,
     'ffn_norm_w': 4.52,
     'ffn_conv_b': 4.53,
     'final_norm_w': 6.59}
    for name, times in wider.items():
        mean = out[name].mean()
        out[name] = (mean + times * (out[name] - mean)).astype(out[name].dtype)
    return out


DEPTH_2 = 2

D_MIX = 1024
MLA_HEADS = 6
MLA_Q_RANK = 256
MLA_KV_RANK = 128
MLA_NOPE = 64
MLA_ROPE = 32
MLA_V = 64
ROPE_THETA = 10000.0
POOL_WINDOWS = (2, 4, 8, 16)
POOL_GROUP = 64
POOL_WIDTH = POOL_GROUP * len(POOL_WINDOWS)
FOX_HEADS = 6
FOX_HEAD_DIM = 64
FOX_GATE_BIAS_INIT = 2.0
BLOCK_Q = 128
IN_Q_A = MLA_Q_RANK
IN_KV_A = MLA_KV_RANK
IN_K_ROPE = MLA_ROPE
IN_POOL = POOL_WIDTH
IN_FOX_QKV = 3 * FOX_HEADS * FOX_HEAD_DIM
IN_FOX_F = FOX_HEADS
N_IN = IN_Q_A + IN_KV_A + IN_K_ROPE + IN_POOL + IN_FOX_QKV + IN_FOX_F


def rmsnorm(x, g):
    xf = x.astype(jnp.float32)
    y = xf * lax.rsqrt(jnp.mean(xf * xf, axis=-1, keepdims=True) + EPS)
    return y.astype(x.dtype) * g

def rope(x, pos):
    r = x.shape[-1]
    inv_freq = ROPE_THETA ** (-jnp.arange(0, r, 2, dtype=jnp.float32) / r)
    ang = pos.astype(jnp.float32)[:, None] * inv_freq[None, :]
    cos = jnp.cos(ang).astype(x.dtype)
    sin = jnp.sin(ang).astype(x.dtype)
    x1, x2 = x[..., : r // 2], x[..., r // 2:]
    return jnp.concatenate([x1 * cos - x2 * sin, x2 * cos + x1 * sin], axis=-1)

def causal_block_attention(q, k, v, scale, log_decay_cum=None):
    b, h, s, dk = q.shape
    dv = v.shape[-1]
    nb = s // BLOCK_Q
    qb = q.reshape(b, h, nb, BLOCK_Q, dk).transpose(2, 0, 1, 3, 4)
    kpos = jnp.arange(s)
    xs = (jnp.arange(nb), qb)
    if log_decay_cum is not None:
        xs = xs + (log_decay_cum.reshape(b, h, nb, BLOCK_Q).transpose(2, 0, 1, 3),)

    def one_block(args):
        i, q_blk = args[0], args[1]
        sc = jnp.einsum('bhqd,bhkd->bhqk', q_blk, k, preferred_element_type=jnp.float32) * scale
        if log_decay_cum is not None:
            c_blk = args[2]
            sc = sc + c_blk[..., :, None] - log_decay_cum[..., None, :].astype(jnp.float32)
        qpos = i * BLOCK_Q + jnp.arange(BLOCK_Q)
        sc = jnp.where(kpos[None, :] <= qpos[:, None], sc, -jnp.inf)
        p = jax.nn.softmax(sc, axis=-1).astype(v.dtype)
        return jnp.einsum('bhqk,bhkd->bhqd', p, v)

    out = lax.map(one_block, xs)
    return out.transpose(1, 2, 0, 3, 4).reshape(b, h, s, dv)

def mla_mixer(q_a, kv_a, k_rope, q_a_norm, w_q_b, kv_a_norm, w_kv_b, pos):
    b, s, _ = q_a.shape
    q = (rmsnorm(q_a, q_a_norm) @ w_q_b).reshape(b, s, MLA_HEADS, MLA_NOPE + MLA_ROPE).transpose(0, 2, 1, 3)
    q_nope, q_pe = q[..., :MLA_NOPE], rope(q[..., MLA_NOPE:], pos)
    kv = (rmsnorm(kv_a, kv_a_norm) @ w_kv_b).reshape(b, s, MLA_HEADS, MLA_NOPE + MLA_V).transpose(0, 2, 1, 3)
    k_nope, v = kv[..., :MLA_NOPE], kv[..., MLA_NOPE:]
    k_pe = jnp.broadcast_to(rope(k_rope, pos)[:, None], (b, MLA_HEADS, s, MLA_ROPE))
    qf = jnp.concatenate([q_nope, q_pe], axis=-1)
    kf = jnp.concatenate([k_nope, k_pe], axis=-1)
    o = causal_block_attention(qf, kf, v, 1.0 / math.sqrt(MLA_NOPE + MLA_ROPE))
    return o.transpose(0, 2, 1, 3).reshape(b, s, MLA_HEADS * MLA_V)

def pool_mixer(u, pool_w, pool_scale):
    b, s, _ = u.shape
    ng = len(POOL_WINDOWS)
    ug = u.reshape(b, s, ng, POOL_GROUP)
    cs = jnp.cumsum(ug.astype(jnp.float32), axis=1)
    count = jnp.arange(1, s + 1, dtype=jnp.float32)
    means = []
    for g, w in enumerate(POOL_WINDOWS):
        c = cs[:, :, g]
        prev = jnp.pad(c[:, : s - w], ((0, 0), (w, 0), (0, 0)))
        means.append((c - prev) / jnp.minimum(count, float(w))[None, :, None])
    pooled = jnp.stack(means, axis=2).astype(u.dtype) - ug
    y = jnp.einsum('bsgc,gcd->bsgd', pooled, pool_w)
    return y.reshape(b, s, POOL_WIDTH) * pool_scale

def fox_mixer(qkv, f_logit, fox_b_f):
    b, s, _ = qkv.shape
    qkv = qkv.reshape(b, s, 3, FOX_HEADS, FOX_HEAD_DIM).transpose(2, 0, 3, 1, 4)
    q, k, v = qkv[0], qkv[1], qkv[2]
    log_f = jax.nn.log_sigmoid((f_logit + fox_b_f).astype(jnp.float32))
    cum = jnp.cumsum(log_f, axis=1).transpose(0, 2, 1)
    o = causal_block_attention(q, k, v, 1.0 / math.sqrt(FOX_HEAD_DIM), cum)
    return o.transpose(0, 2, 1, 3).reshape(b, s, FOX_HEADS * FOX_HEAD_DIM)

def swiglu(h, w_gu, w_down):
    gu = h @ w_gu
    g, u = gu[..., :D_FF], gu[..., D_FF:]
    return (jax.nn.silu(g) * u) @ w_down

def hybrid_mixing(h, w_in, q_a_norm, w_q_b, kv_a_norm, w_kv_b, pool_w, pool_scale, fox_b_f, w_out, pos):
    z = h @ w_in
    o0 = 0
    o1 = o0 + IN_Q_A
    o2 = o1 + IN_KV_A
    o3 = o2 + IN_K_ROPE
    o4 = o3 + IN_POOL
    o5 = o4 + IN_FOX_QKV
    o6 = o5 + IN_FOX_F
    ya = mla_mixer(z[..., o0:o1], z[..., o1:o2], z[..., o2:o3], q_a_norm, w_q_b, kv_a_norm, w_kv_b, pos)
    yb = pool_mixer(z[..., o3:o4], pool_w, pool_scale)
    yc = fox_mixer(z[..., o4:o5], z[..., o5:o6], fox_b_f)
    return jnp.concatenate([ya, yb, yc], axis=-1) @ w_out

def second_inputs(seed: int = 0) -> dict:
    key = jax.random.key(seed)
    ks = jax.random.split(key, 24)
    L, D, F = DEPTH_2, D_MODEL, D_FF
    f32 = jnp.float32

    def nrm(k, shape, fan_in):
        return jax.random.normal(k, shape, f32) * (fan_in ** -0.5)

    def gain(k, shape):
        return 1.0 + 0.02 * jax.random.normal(k, shape, f32)

    return {
        "x": jax.random.normal(ks[0], (BATCH, SEQ, D), f32),
        "ffn1_norm": gain(ks[1], (L, D)),
        "ffn1_w_gu": nrm(ks[2], (L, D, 2 * F), D),
        "ffn1_w_down": nrm(ks[3], (L, F, D), F),
        "mix_norm": gain(ks[4], (L, D)),
        "w_in": nrm(ks[5], (L, D, N_IN), D),
        "q_a_norm": gain(ks[6], (L, MLA_Q_RANK)),
        "w_q_b": nrm(ks[7], (L, MLA_Q_RANK, MLA_HEADS * (MLA_NOPE + MLA_ROPE)), MLA_Q_RANK),
        "kv_a_norm": gain(ks[8], (L, MLA_KV_RANK)),
        "w_kv_b": nrm(ks[9], (L, MLA_KV_RANK, MLA_HEADS * (MLA_NOPE + MLA_V)), MLA_KV_RANK),
        "pool_w": nrm(ks[10], (L, len(POOL_WINDOWS), POOL_GROUP, POOL_GROUP), POOL_GROUP),
        "pool_scale": gain(ks[11], (L, POOL_WIDTH)),
        "fox_b_f": FOX_GATE_BIAS_INIT + 0.5 * jax.random.normal(ks[12], (L, FOX_HEADS), f32),
        "w_out": nrm(ks[13], (L, D_MIX, D), D_MIX),
        "ffn2_norm": gain(ks[14], (L, D)),
        "ffn2_w_gu": nrm(ks[15], (L, D, 2 * F), D),
        "ffn2_w_down": nrm(ks[16], (L, F, D), F),
        "final_norm": gain(ks[17], (D,)),
    }

def second_block(x, ffn1_norm, ffn1_w_gu, ffn1_w_down, mix_norm, w_in, q_a_norm, w_q_b, kv_a_norm, w_kv_b,
              pool_w, pool_scale, fox_b_f, w_out, ffn2_norm, ffn2_w_gu, ffn2_w_down, final_norm):
    pos = jnp.arange(x.shape[1], dtype=jnp.int32)
    for l in range(DEPTH_2):
        x = x + 0.5 * swiglu(rmsnorm(x, ffn1_norm[l]), ffn1_w_gu[l], ffn1_w_down[l])
        x = x + hybrid_mixing(rmsnorm(x, mix_norm[l]), w_in[l], q_a_norm[l], w_q_b[l], kv_a_norm[l], w_kv_b[l],
                              pool_w[l], pool_scale[l], fox_b_f[l], w_out[l], pos)
        x = x + 0.5 * swiglu(rmsnorm(x, ffn2_norm[l]), ffn2_w_gu[l], ffn2_w_down[l])
    return rmsnorm(x, final_norm)


def setup_inputs(seed=0):
    out = dict(first_inputs(seed))
    for name, value in second_inputs(seed + 1).items():
        if name != "x":
            out[name + "_2"] = value
    return out


def reference(
    x, attn_norm_w, w_in, gdn_conv_w, gdn_a_log, gdn_dt_bias, gdn_norm_w, s5_lambda_re,
    s5_lambda_im, s5_log_dt, s5_b_re, s5_b_im, s5_c_re, s5_c_im, s5_d, s5_w_glu, s5_b_glu,
    s5_norm_w, diff_lambda_q1, diff_lambda_k1, diff_lambda_q2, diff_lambda_k2, diff_norm_w,
    w_out, ffn_norm_w, ffn_w_up, ffn_conv_w, ffn_conv_b, ffn_w_down, final_norm_w, ffn1_norm_2,
    ffn1_w_gu_2, ffn1_w_down_2, mix_norm_2, w_in_2, q_a_norm_2, w_q_b_2, kv_a_norm_2, w_kv_b_2,
    pool_w_2, pool_scale_2, fox_b_f_2, w_out_2, ffn2_norm_2, ffn2_w_gu_2, ffn2_w_down_2,
    final_norm_2,
):
    x = first_block(
        x, attn_norm_w, w_in, gdn_conv_w, gdn_a_log, gdn_dt_bias, gdn_norm_w, s5_lambda_re,
        s5_lambda_im, s5_log_dt, s5_b_re, s5_b_im, s5_c_re, s5_c_im, s5_d, s5_w_glu, s5_b_glu,
        s5_norm_w, diff_lambda_q1, diff_lambda_k1, diff_lambda_q2, diff_lambda_k2, diff_norm_w,
        w_out, ffn_norm_w, ffn_w_up, ffn_conv_w, ffn_conv_b, ffn_w_down, final_norm_w,
    )
    return second_block(
        x, ffn1_norm_2, ffn1_w_gu_2, ffn1_w_down_2, mix_norm_2, w_in_2, q_a_norm_2, w_q_b_2,
        kv_a_norm_2, w_kv_b_2, pool_w_2, pool_scale_2, fox_b_f_2, w_out_2, ffn2_norm_2,
        ffn2_w_gu_2, ffn2_w_down_2, final_norm_2,
    )


_drawn_inputs = setup_inputs


def setup_inputs(seed=0):
    import zlib

    import numpy as np

    out = dict(_drawn_inputs(seed))
    spreads = {}
    factors = {'ffn1_norm_2': 8.0,
     'ffn1_w_gu_2': 8.0,
     'ffn1_w_down_2': 8.0,
     'mix_norm_2': 8.0,
     'w_in_2': 8.0,
     'q_a_norm_2': 64.0,
     'w_q_b_2': 8.0,
     'kv_a_norm_2': 64.0,
     'w_kv_b_2': 8.0,
     'pool_w_2': 8.0,
     'pool_scale_2': 8.0,
     'fox_b_f_2': 200.0,
     'w_out_2': 8.0,
     'ffn2_norm_2': 21.374,
     'ffn2_w_gu_2': 8.0,
     'ffn2_w_down_2': 8.0,
     'final_norm_2': 22.764}
    for name, (base, spread) in spreads.items():
        noise = np.random.default_rng([zlib.crc32(name.encode()), seed]).standard_normal(out[name].shape)
        drawn = base * np.exp(spread * noise) if base else spread * noise
        out[name] = __import__('jax').numpy.asarray(drawn.astype(out[name].dtype))
    for name, factor in factors.items():
        out[name] = (out[name] * factor).astype(out[name].dtype)
    return out
```

```python
from contextlib import ExitStack, contextmanager

import numpy as np
import concourse.bass as bass
from concourse import mybir

F32 = mybir.dt.float32
F32R = mybir.dt.float32r
I32 = mybir.dt.int32
ALU = mybir.AluOpType
ACT = mybir.ActivationFunctionType
AX = mybir.AxisListType.X
ds = bass.ds

P = 128
T = 512
NT = T // P
D = 1024
DC = D // P
FF = 2816
FC = FF // P
EPS = 1e-6
LAYERS = 2
COLS = 256
NEG = -1.0e30

GH, GD = 4, 128
G_Q, G_Z, G_BA, S_U, D_Q, D_V = 0, 1536, 2048, 2056, 2568, 3592
QA, KVA, POOL, FOX_Q, FOX_V = 0, 256, 416, 672, 1440
IN2 = 1830
HEADS, HD, ROPE, QD = 6, 64, 32, 96
VF = IN2 - FOX_V
S5G, S5H, S5P = 32, 16, 64
PAIRS = S5G // 2
STEP = 8
NSTEP = T // STEP

U_DQK, U_DV, U_SU, U_GLU, U_G, U_WO, U_UP, U_DN, U_FIRST = 0, 4, 6, 8, 9, 17, 23, 45, 56
V_UP1, V_DN1, V_WIN, V_WO, V_UP2, V_DN2, U_LAYER = 0, 22, 33, 41, 45, 67, 78

PV = {}
_at = 0
for _n, _k in (("attn", 8), ("ffn", 8), ("fin1", 8), ("s5d", 4), ("bglu", 4), ("s5n", 4), ("gdnn", 1), ("diffn", 1),
               ("gconv", 48), ("fconv", 132), ("fbias", 44), ("fin2", 8), ("layer", 58)):
    PV[_n] = _at
    _at += _k
NPV = _at
LW = 29
PVT = -(-NPV // P)


LAM_INIT = 0.8 - 0.6 * float(np.exp(0.0))
ROUND = 1.5 * 2.0 ** 23
TWO_PI = (6.28125, 0.0019350051879882812, 2 * np.pi - 6.28125 - 0.0019350051879882812)


class Book:

    def __init__(self, known=None):
        self.known, self.places, self.pers, self.frames = known, {}, {}, {}


class Tally:

    def __init__(self, book, sem, name, engine):
        self.book, self.sem, self.name, self.cursor = book, sem, name, 0
        self.frames = book.frames.setdefault(engine, [])

    def tick(self, label, n=1):
        for f in self.frames:
            f["starts"].setdefault(self, self.cursor)
        self.cursor += n
        key = (self.name, label)
        assert key not in self.book.places, key
        self.book.places[key] = (self.cursor, [f["key"] for f in self.frames])
        self.newest = label
        return self.sem, n

    def __call__(self, label, **at):
        known = self.book.known
        if known is None:
            return self.sem, 1
        count, loops = known.places[(self.name, label)]
        for key in loops:
            count = count + at[key[0]] * known.pers[(self.name, key)]
        if isinstance(count, int):
            assert count >= 0
        return self.sem, count

    def last(self, **at):
        return self(self.newest, **at)


@contextmanager
def loop(book, engine, name, eng, key, n):
    frame = {"key": (key, name), "starts": {}}
    book.frames.setdefault(engine, []).append(frame)
    with eng.Fori(0, n) as i:
        yield i
    book.frames[engine].pop()
    for tally, start in frame["starts"].items():
        per = tally.cursor - start
        book.pers[(tally.name, frame["key"])] = per
        tally.cursor = start + per * n


class Unit:

    def __init__(self, const, layer=None, i=None):
        self.slot, self.first = const % 2, const == 0
        n, half = const, const // 2
        if layer is not None:
            n, half = n + U_FIRST + layer * U_LAYER, half + U_FIRST // 2 + layer * (U_LAYER // 2)
        if i is not None:
            n, half = n + i * 2, half + i
        self.n, self.half = n, half
        self.early = layer is None and i is None and const < 2
        self.landed = (half + 1) * 32
        self.split = n + 1
        self.done = (n + 1) * 8
        self.before = n * 8
        self.began = n * 8


def build(nc, A, out, book):
    with ExitStack() as ctx:
        def sb(name, shape, dt=F32):
            return ctx.enter_context(nc.sbuf_tensor(name, shape, dt))

        def sem(name):
            return ctx.enter_context(nc.semaphore(name))

        xT = sb("xT", [P, DC, T])
        raw = [sb(f"raw{s}", [P, 2048]) for s in range(2)]
        whi = [sb(f"weight_high{s}", [P, 2048], F32R) for s in range(2)]
        wlo = [sb(f"weight_low{s}", [P, 2048], F32R) for s in range(2)]
        cst = sb("constants", [P, 5, P])
        ident, tri, strict, causal, ones = (cst[:, i, :] for i in range(5))
        pv = sb("parameters", [P, PVT * P])
        lv = sb("layer_parameters", [P, LW])
        rb = sb("root", [P, T])
        rcol = sb("root_column", [P, NT])
        tmp = [sb(f"tmp{i}", [P, T + 2]) for i in range(6)]
        small = sb("small", [P, 96])
        xa = ExitStack()
        gb = [xa.enter_context(nc.sbuf_tensor(f"delta{i}", [P, T], F32)) for i in range(16)]
        xa.close()
        xhi = sb("xw_high", [P, DC, T], F32R)
        xlo = sb("xw_low", [P, DC, T], F32R)
        region = ExitStack()

        def tb(name, shape, dt=F32):
            return region.enter_context(nc.sbuf_tensor(name, shape, dt))

        mohi = tb("mixed_high", [P, 12, T], F32R)
        molo = tb("mixed_low", [P, 12, T], F32R)
        sub = ExitStack()

        def ub(name, shape, dt=F32):
            return sub.enter_context(nc.sbuf_tensor(name, shape, dt))

        xin = ub("x_in", [P, NT, D])
        rows = ub("parameter_rows", [P, PVT, P])
        sub.close()
        sub = ExitStack()
        dqk = ub("diff_qk", [P, 8, T])
        dv = ub("diff_v", [P, NT, T])
        osum = ub("diff_out", [P, 4, T])
        lamb = ub("lambda_rows", [P, 4 * 64])
        sub.close()
        sub = ExitStack()
        su = ub("s5_u", [P, 4, T])
        bbd = [ub(f"s5_b{c}", [P, PAIRS, 32]) for c in "ri"]
        cbd = [ub(f"s5_c{c}", [P, PAIRS, 32]) for c in "ri"]
        lvp = [ub(f"s5_level{c}", [P, 6, PAIRS]) for c in "ri"]
        pw = [ub(f"s5_power{c}", [P, STEP + 1, PAIRS]) for c in "ri"]
        st = [ub(f"s5_state{c}", [P, PAIRS, NSTEP]) for c in "ri"]
        cp = [ub(f"s5_cp{c}", [P, 4, STEP + 1, 32]) for c in "ri"]
        kbd = ub("s5_kernel", [P, STEP, P])
        sub.close()
        sub = ExitStack()
        zg = ub("delta_z", [P, 16, T + 3])
        lvl = ub("level_masks", [P, 7, P])
        baw = ub("gate_weights", [P, DC, 8])
        bah = ub("gate_weights_high", [P, DC, 8], F32R)
        bal = ub("gate_weights_low", [P, DC, 8], F32R)
        gates = ub("gates", [P, 64])
        sub.close()
        region.close()
        region = ExitStack()
        z2 = tb("z", [P, 12, T])
        vf = tb("fox_v_gates", [P, NT, VF + 2])
        qf = tb("mla_q", [P, HEADS, T])
        kf = tb("mla_k", [P, HEADS, T])
        mv = tb("mla_v", [P, NT, HEADS * HD])
        wqb = tb("w_q_b", [P, 2, HEADS * QD])
        wkvb = tb("w_kv_b", [P, HEADS, 2 * HD])
        ropet = tb("rope_tables", [P, 2, T])
        poolt = tb("pool_counts", [P, 2, T])
        poolw = tb("pool_w", [P, 2, P])
        turn = tb("rope_turn", [P, QD])
        region.close()
        hhi = sb("hidden_high", [P, FC, T], F32R)
        hlo = sb("hidden_low", [P, FC, T], F32R)

        ps = ctx.enter_context(nc.psum_tensor("psum", [P, 8, T], F32))

        landed = [sem(f"unit_landed{s}") for s in range(2)]
        high_ready, low_ready, consumed = sem("high_ready"), sem("low_ready"), sem("units_consumed")
        params_in, x_in, mixer_in, lambda_in, gate_in = (sem(n) for n in
                                                          ("params_in", "x_in_landed", "mixer_in", "lambda_in", "gate_in"))
        s5_in, layer_in, stored = sem("s5_in"), sem("layer_in"), sem("output_stored")
        pe_t = Tally(book, sem("products_ready"), "pe", "pe")
        ve_t = Tally(book, sem("vector_ready"), "ve", "ve")
        sc_t = Tally(book, sem("scalar_ready"), "sc", "sc")
        po_t = Tally(book, sem("pool_ready"), "po", "po")
        dm_t = Tally(book, mixer_in, "dm", "sp")
        blk = ctx.enter_context(nc.Block())

        def prow(name, k):
            r = PV[name] + k
            return r % P, r // P

        def pcol(name, k):
            return pv[:, PV[name] + k:PV[name] + k + 1]

        def bank(i):
            return ps[:, i, :]

        def slots(a, b):
            return st[0][:, :, :].rearrange("p b n -> p (b n)")[:, 16 * a:16 * b]

        def slot(a):
            return slots(a, a + 1)

        def raw_out(t):
            return raw[t // 2][:, D * (t % 2):D * (t % 2) + D]

        def wbj(c):
            return tmp[2 + c][:, 0:T]

        @blk.sync
        def _(sp):
            nparam = 0

            def rows_in(name, src, k):
                nonlocal nparam
                at = PV[name]
                done = 0
                while done < k:
                    m = min(k - done, P - (at + done) % P)
                    sp.dma_start(rows[(at + done) % P:(at + done) % P + m, (at + done) // P, :],
                                 src[done:done + m, :]).then_inc(params_in, 16)
                    done += m
                    nparam += 1

            def of128(ap):
                return ap.rearrange("a (k p) -> (a k) p", p=P)

            sp.dma_start(xin[:, :, :], A["x"][0].rearrange("(t p) d -> p t d", p=P)).then_inc(x_in, 16)
            sp.dma_start(cst[:, :, :], A["constants"]).then_inc(x_in, 16)
            for name, src, k in (("attn", "attn_norm_w", 8), ("ffn", "ffn_norm_w", 8), ("s5d", "s5_d", 4),
                                 ("bglu", "s5_b_glu", 4), ("s5n", "s5_norm_w", 4), ("gdnn", "gdn_norm_w", 1),
                                 ("diffn", "diff_norm_w", 1), ("fbias", "ffn_conv_b", 44)):
                rows_in(name, of128(A[src]), k)
            for name, src in (("fin1", "final_norm_w"), ("fin2", "final_norm_2")):
                rows_in(name, A[src].rearrange("(k p) -> k p", p=P), 8)
            rows_in("gconv", of128(A["gdn_conv_w"][0]), 48)
            rows_in("fconv", of128(A["ffn_conv_w"][0]), 132)
            for l in range(LAYERS):
                at = 29 * l
                for src, k in (("ffn1_norm_2", 8), ("mix_norm_2", 8), ("ffn2_norm_2", 8), ("q_a_norm_2", 2),
                               ("kv_a_norm_2", 1), ("pool_scale_2", 2)):
                    PV["_"] = PV["layer"] + at
                    rows_in("_", A[src][l:l + 1, :].rearrange("a (k p) -> (a k) p", p=P), k)
                    at += k
            book.nparam = nparam

            def free(u):
                if not u.early:
                    sp.wait_ge(high_ready, u.split - 2)
                    sp.wait_ge(low_ready, u.split - 2)

            def load_cols(u, w, c0, c1=None):
                free(u)
                dst = raw[u.slot][:, :].rearrange("p (k c) -> p k c", k=DC)
                src = w.rearrange("(k p) c -> p k c", p=P)
                if c1 is None:
                    for h in range(2):
                        sp.dma_start(dst[:, 4 * h:4 * h + 4, :], src[:, 4 * h:4 * h + 4, ds(c0, COLS)])\
                          .then_inc(landed[u.slot], 16)
                else:
                    for h, c in enumerate((c0, c1)):
                        sp.dma_start(dst[:, :, P * h:P * h + P], src[:, :, ds(c, P)]).then_inc(landed[u.slot], 16)

            def load_rows(u, w, r0):
                free(u)
                for h in range(2):
                    sp.dma_start(raw[u.slot][:, 1024 * h:1024 * h + 1024], w[ds(r0 + P * h, P), :])\
                      .then_inc(landed[u.slot], 16)

            w_in = A["w_in"][0]
            for i in range(4):
                load_cols(Unit(U_DQK + i), w_in, D_Q + COLS * i)
                if i == 1:
                    for n, v in enumerate(("q1", "k1", "q2", "k2")):
                        sp.dma_start(lamb[:, 64 * n:64 * n + 64],
                                     A["diff_lambda_" + v][0:1, :].to_broadcast([P, 64])).then_inc(lambda_in, 16)
            for i in range(2):
                load_cols(Unit(U_DV + i), w_in, D_V + COLS * i)
            for i in range(2):
                load_cols(Unit(U_SU + i), w_in, S_U + COLS * i)
            sp.wait_ge(*ve_t(("diff low", 3)))
            sp.wait_ge(*sc_t(("diff high", 3)))
            for c, n in enumerate(("re", "im")):
                sp.dma_start(tmp[0][0:16, P * c:P * c + P],
                             A[f"s5_lambda_{n}"][0].rearrange("(b e) p -> b (e p)", e=2)).then_inc(s5_in, 16)
                for e in range(2):
                    sp.dma_start(bbd[c][64 * e:64 * e + 64, :, 16 * e:16 * e + 16],
                                 A[f"s5_b_{n}"][0].rearrange("(b e) p h -> e p b h", e=2)[e]).then_inc(s5_in, 16)
                for q in range(2):
                    for b in range(8):
                        sp.dma_start(tmp[2 + c][16 * b:16 * b + 16, P * q:P * q + P].rearrange("h (e p) -> h e p", e=2),
                                     A[f"s5_c_{n}"][0].rearrange("(b e) h p -> b h e p", e=2)[8 * q + b])\
                          .then_inc(s5_in, 16)
            sp.dma_start(tmp[1][0:16, 0:2], A["s5_log_dt"][0].rearrange("(b e) -> b e", e=2)).then_inc(s5_in, 16)
            free(Unit(U_GLU))
            for h in range(2):
                sp.dma_start(raw[Unit(U_GLU).slot][:, 1024 * h:1024 * h + 1024].rearrange("p (k c) -> p k c", k=2),
                             A["s5_w_glu"][0][256 * h:256 * h + 256, :].rearrange("(k p) c -> p k c", p=P))\
                  .then_inc(landed[Unit(U_GLU).slot], 16)
            with loop(book, "sp", "g", sp, "i", 4) as i:
                load_cols(Unit(U_G, i=i), w_in, i * (2 * COLS))
                load_cols(Unit(U_G + 1, i=i), w_in, i * (2 * COLS) + COLS)
            sp.wait_ge(*ve_t(("s5 out low", 3)))
            sp.wait_ge(*po_t("s5 free"))
            sp.dma_start(lvl[:, :, :], A["levels"]).then_inc(gate_in, 16)
            with nc.allow_non_contiguous_dma(reason="eight columns"):
                sp.dma_start(baw[:, :, :], w_in[:, G_BA:G_BA + 8].rearrange("(k p) c -> p k c", p=P))\
                  .then_inc(gate_in, 16)
            sp.dma_start(gates[:, 48:52], A["gdn_a_log"][0:1, :].to_broadcast([P, 4])).then_inc(gate_in, 16)
            sp.dma_start(gates[:, 52:56], A["gdn_dt_bias"][0:1, :].to_broadcast([P, 4])).then_inc(gate_in, 16)
            for i in range(6):
                load_rows(Unit(U_WO + i), A["w_out"][0], 2 * P * i)

            def load_ffn(up, down, w_up, w_down, name, layer=None):
                with loop(book, "sp", name, sp, "i", 11) as i:
                    load_cols(Unit(up, layer, i), w_up, i * COLS)
                    load_cols(Unit(up + 1, layer, i), w_up, i * COLS + FF)
                load_rows(Unit(down, layer), w_down, 0)
                with loop(book, "sp", name + "d", sp, "i", 4) as i:
                    load_rows(Unit(down + 1, layer, i), w_down, i * (4 * P) + 2 * P)
                    load_rows(Unit(down + 2, layer, i), w_down, i * (4 * P) + 4 * P)
                for k in range(2):
                    load_rows(Unit(down + 9 + k, layer), w_down, (9 + k) * 2 * P)

            load_ffn(U_UP, U_DN, A["ffn_w_up"][0], A["ffn_w_down"][0], "f0")
            with loop(book, "sp", "layer", sp, "layer", LAYERS) as l:
                def of(name):
                    a = A[name]
                    return a[ds(l, 1)].rearrange("a r c -> (a r) c")

                load_ffn(V_UP1, V_DN1, of("ffn1_w_gu_2"), of("ffn1_w_down_2"), "f1", l)
                win2 = of("w_in_2")
                load_cols(Unit(V_WIN, l), win2, QA)
                load_cols(Unit(V_WIN + 1, l), win2, KVA, KVA + 64)
                sp.wait_ge(consumed, Unit(V_WIN, l).before)
                sp.dma_start(wqb[:, :, :], of("w_q_b_2").rearrange("(k p) c -> p k c", p=P)).then_inc(layer_in, 16)
                sp.dma_start(wkvb[:, :, :].rearrange("p h c -> p (h c)"), of("w_kv_b_2")).then_inc(layer_in, 16)
                sp.dma_start(ropet[0:QD, :, :], A["rope"]).then_inc(layer_in, 16)
                sp.dma_start(poolt[:, :, :], A["counts"]).then_inc(layer_in, 16)
                sp.dma_start(turn[0:QD, :], A["turn"]).then_inc(layer_in, 16)
                pwl = A["pool_w_2"][ds(l, 1)].rearrange("a (k g) c d -> g (a c) k d", g=2)
                for g in range(2):
                    r = slice(HD * g, HD * g + HD)
                    sp.dma_start(poolw[r, :, r], pwl[g]).then_inc(layer_in, 16)
                sp.dma_start(small[:, 64:70], A["fox_b_f_2"][ds(l, 1), :].to_broadcast([P, HEADS]))\
                  .then_inc(layer_in, 16)
                for k in range(4):
                    load_cols(Unit(V_WIN + 2 + k, l), win2, POOL + COLS * k)
                load_cols(Unit(V_WIN + 6, l), win2, FOX_V)
                u = Unit(V_WIN + 7, l)
                free(u)
                dst = raw[u.slot][:, :].rearrange("p (k c) -> p k c", k=DC)
                src = win2.rearrange("(k p) c -> p k c", p=P)
                for h in range(2):
                    sp.dma_start(dst[:, 4 * h:4 * h + 4, 0:VF - COLS], src[:, 4 * h:4 * h + 4, FOX_V + COLS:IN2])\
                      .then_inc(landed[u.slot], 16)
                for k in range(4):
                    load_rows(Unit(V_WO + k, l), of("w_out_2"), 2 * P * k)
                load_ffn(V_UP2, V_DN2, of("ffn2_w_gu_2"), of("ffn2_w_down_2"), "f2", l)
            for t in range(NT):
                sp.wait_ge(*ve_t(("out half", t, 1)))
                sp.dma_start(out[0, P * t:P * t + P, :], raw_out(t)).then_inc(stored, 16)
            sp.wait_ge(stored, 16 * NT)

        @blk.gpsimd
        def _(po):
            def low(u, n=2048):
                po.wait_ge(high_ready, u.split)
                po.tensor_tensor(wlo[u.slot][:, 0:n], raw[u.slot][:, 0:n], whi[u.slot][:, 0:n].bitcast(F32),
                                 ALU.subtract).then_inc(low_ready, 1)

            def sum_squares(tag, **at):
                for j in range(1, DC):
                    po.wait_ge(*sc_t(("square", tag, j), **at))
                    if j > 1:
                        po.wait_ge(*po_t.last(**at))
                    po.tensor_tensor(tmp[2][:, 0:T], tmp[2 if j > 1 else 0][:, 0:T], tmp[j % 2][:, 0:T], ALU.add)\
                      .then_inc(*po_t.tick(("sum", tag, j)))

            def ffn(up, name, layer=None):
                at = {} if layer is None else {"layer": layer}
                with loop(book, "po", name, po, "i", 11) as i:
                    for h in range(2):
                        low(Unit(up + 1 + h, layer, i))
                    for c in range(2):
                        po.wait_ge(*sc_t(("hidden high", name, c), i=i, **at))
                        po.tensor_tensor(hlo[:, ds(i * 2 + c, 1), :].rearrange("p a t -> p (a t)"), tmp[4 + c][:, 0:T],
                                         hhi[:, ds(i * 2 + c, 1), :].rearrange("p a t -> p (a t)").bitcast(F32),
                                         ALU.subtract).then_inc(*po_t.tick(("hidden low", name, c)))
                dn = up + 22
                low(Unit(dn + 1, layer))
                with loop(book, "po", name + "d", po, "i", 4) as i:
                    low(Unit(dn + 2, layer, i))
                    low(Unit(dn + 3, layer, i))
                low(Unit(dn + 10, layer))

            po.memset(small[:, 95:96], 0.0).then_inc(*po_t.tick("start"))
            low(Unit(0))
            sum_squares("attn")
            for u in range(1, U_SU + 2):
                low(Unit(u))
            po.wait_ge(*ve_t(("diff low", 3)))
            po.wait_ge(*sc_t(("diff high", 3)))
            for c in range(2):
                po.memset(cbd[c][:, :, :], 0.0).then_inc(*po_t.tick(("zero c", c)))
            po.memset(kbd[:, :, :], 0.0).then_inc(*po_t.tick("zero k"))
            low(Unit(U_GLU))
            low(Unit(U_G))
            po.memset(small[:, 94:95], 0.0).then_inc(*po_t.tick("s5 free"))
            with loop(book, "po", "g", po, "i", 4) as i:
                low(Unit(U_G + 1, i=i))
                low(Unit(U_G + 2, i=i))
            for u in range(U_WO + 1, U_WO + 6):
                low(Unit(u))
            low(Unit(U_UP))
            sum_squares("ffn")
            ffn(U_UP, "f0")
            sum_squares("fin1")
            with loop(book, "po", "layer", po, "layer", LAYERS) as l:
                low(Unit(V_UP1, l))
                sum_squares("n1", layer=l)
                ffn(V_UP1, "f1", l)
                low(Unit(V_WIN, l))
                sum_squares("nm", layer=l)
                for u in range(V_WIN + 1, V_WIN + 7):
                    low(Unit(u, l))
                u = Unit(V_WIN + 7, l)
                po.wait_ge(high_ready, u.split)
                lo_part = wlo[u.slot][:, :].rearrange("p (k c) -> p k c", k=DC)[:, :, 0:VF - COLS]
                po.tensor_tensor(lo_part, raw[u.slot][:, :].rearrange("p (k c) -> p k c", k=DC)[:, :, 0:VF - COLS],
                                 whi[u.slot][:, :].rearrange("p (k c) -> p k c", k=DC)[:, :, 0:VF - COLS].bitcast(F32),
                                 ALU.subtract).then_inc(low_ready, 1)
                for u in range(V_WO, V_WO + 4):
                    low(Unit(u, l))
                low(Unit(V_UP2, l))
                sum_squares("n2", layer=l)
                ffn(V_UP2, "f2", l)
            sum_squares("fin2")

        @blk.tensor
        def _(pe):
            def three(dst, lh, ll, rh, rl, start, stop):
                pe.matmul(dst, lh, rh, start=start, stop=False, skip_group_check=True)
                pe.matmul(dst, ll, rh, start=False, stop=False, skip_group_check=True)
                return pe.matmul(dst, lh, rl, start=False, stop=stop, skip_group_check=True)

            def cols_unit(u, banks, waits=()):
                pe.wait_ge(low_ready, u.split)
                for c in range(2):
                    if waits:
                        pe.wait_ge(*waits[c])
                    for k in range(DC):
                        w = slice(COLS * k + P * c, COLS * k + P * c + P)
                        m = three(bank(banks[c]), whi[u.slot][:, w], wlo[u.slot][:, w], xhi[:, k, :], xlo[:, k, :],
                                  k == 0, k == DC - 1)
                    m.then_inc(consumed, 4)

            def tokens_unit(u, n, c0, waits=None):
                pe.wait_ge(low_ready, u.split)
                for t in range(NT):
                    if waits:
                        pe.wait_ge(*waits[t])
                    for k in range(DC):
                        w = slice(COLS * k, COLS * k + n)
                        x = slice(P * t, P * t + P)
                        m = three(ps[:, t, c0:c0 + n], xhi[:, k, x], xlo[:, k, x], whi[u.slot][:, w],
                                  wlo[u.slot][:, w], k == 0, k == DC - 1)
                    m.then_inc(consumed, 2)

            def rows_unit(u, rh, rl, start, stop, first_wait=None):
                pe.wait_ge(low_ready, u.split)
                for j in range(DC):
                    if first_wait and j in first_wait:
                        pe.wait_ge(*first_wait[j])
                    for k in range(2):
                        w = slice(1024 * k + P * j, 1024 * k + P * j + P)
                        m = three(bank((j + 4) % 8), whi[u.slot][:, w], wlo[u.slot][:, w], rh(k), rl(k),
                                  start and k == 0, stop and k == 1)
                    if stop:
                        m.then_inc(consumed, 1)
                if not stop:
                    m.then_inc(consumed, 8)

            def total(tag, column=False, **at):
                pe.wait_ge(*po_t(("sum", tag, DC - 1), **at))
                pe.matmul(bank(7), ones, tmp[2][:, 0:T], start=True, stop=True).then_inc(*pe_t.tick(("total", tag)))
                if column:
                    pe.wait_ge(*ve_t(("root", tag), **at))
                    for t in range(NT):
                        m = pe.matmul(ps[:, 6, t:t + 1], rb[:, P * t:P * t + P], ident[:, 0:1], start=True, stop=True)
                    m.then_inc(*pe_t.tick(("root column", tag)))

            def xw_ready(tag, **at):
                pe.wait_ge(*ve_t(("xw low", tag, DC - 1), **at))

            def ffn(up, name, layer=None):
                at = {} if layer is None else {"layer": layer}
                with loop(book, "pe", name, pe, "i", 11) as i:
                    cols_unit(Unit(up, layer, i), (0, 1), [ve_t(("gate", name, c), i=i - 1, **at) for c in range(2)])
                    cols_unit(Unit(up + 1, layer, i), (2, 3), [ve_t(("hidden", name, c), i=i - 1, **at) for c in range(2)])
                dn = up + 22

                def hid(hc):
                    return (lambda k: hhi[:, ds(hc + k, 1), :].rearrange("p a t -> p (a t)"),
                            lambda k: hlo[:, ds(hc + k, 1), :].rearrange("p a t -> p (a t)"))

                def ready(i):
                    return po_t(("hidden low", name, 1), i=i, **at)

                last = {4 + c: ve_t(("gate", name, c), i=10, **at) for c in range(2)}
                last |= {6 + c: ve_t(("hidden", name, c), i=10, **at) for c in range(2)}
                pe.wait_ge(*ready(0))
                rows_unit(Unit(dn, layer), *hid(0), True, False, last)
                with loop(book, "pe", name + "d", pe, "i", 4) as i:
                    pe.wait_ge(*ready(i * 2 + 1))
                    rows_unit(Unit(dn + 1, layer, i), *hid(i * 4 + 2), False, False)
                    pe.wait_ge(*ready(i * 2 + 2))
                    rows_unit(Unit(dn + 2, layer, i), *hid(i * 4 + 4), False, False)
                pe.wait_ge(*ready(9))
                rows_unit(Unit(dn + 9, layer), *hid(18), False, False)
                pe.wait_ge(*ready(10))
                rows_unit(Unit(dn + 10, layer), *hid(20), False, True)

            pe.wait_ge(params_in, 16 * book.nparam)
            pe.wait_ge(x_in, 32)
            for t in range(PVT):
                n = min(P, NPV - P * t)
                m = pe.transpose(ps[:, 7, P * t:P * t + n], rows[0:n, t, :], ident[0:n, 0:n])
            m.then_inc(*pe_t.tick("parameters"))
            for j in range(DC):
                if j == 7:
                    pe.wait_ge(*ve_t("parameters"))
                for t in range(NT):
                    m = pe.transpose(ps[:, j, P * t:P * t + P], xin[:, t, P * j:P * j + P], ident)
                m.then_inc(*pe_t.tick(("x", j)))

            xw_ready("attn")
            total("attn", column=True)
            for i in range(4):
                w = [ve_t(("dqk", 2 * i + c - 4)) for c in range(2)] if i >= 2 else ()
                cols_unit(Unit(U_DQK + i), (2 * i % 4, 2 * i % 4 + 1), w)
            tokens_unit(Unit(U_DV), COLS, 0, [ve_t(("dqk", 4 + t)) for t in range(NT)])
            tokens_unit(Unit(U_DV + 1), COLS, COLS, [ve_t(("dv", 0, t)) for t in range(NT)])

            def transposes(dst, src, n, label, wait, rows_n=P):
                pe.wait_ge(*wait)
                for k in range(n):
                    m = pe.transpose(bank(dst)[:, P * k:P * k + P], src[:, P * k:P * k + P], ident)
                m.then_inc(*pe_t.tick(label))

            for t in range(NT):
                for h in range(4):
                    for c in range(2):
                        n = P * (t + 1)
                        pe.wait_ge(*ve_t(("dqk", 4 + h)))
                        prev = (t, h - 1) if h else (t - 1, 3)
                        if prev[0] >= 0:
                            pe.wait_ge(*ve_t(("diff scores", *prev, c)))
                        r = slice(64 * c, 64 * c + 64)
                        pe.matmul(ps[:, 4 + c, 0:n], dqk[r, h, P * t:P * t + P], dqk[r, 4 + h, 0:n], start=True,
                                  stop=True).then_inc(*pe_t.tick(("diff scores", t, h, c)))
                    if (t, h) != (0, 0):
                        pe.wait_ge(*sc_t(("diff turned", *prev)))
                    transposes(6, tmp[0], t + 1, ("diff turned", t, h), ve_t(("diff weights", t, h)))
                    pe.wait_ge(*sc_t(("diff turned", t, h)))
                    if (t, h) != (0, 0):
                        pe.wait_ge(*ve_t(("diff out", *prev)))
                    pe.wait_ge(*ve_t(("dv", 1, NT - 1)))
                    for k in range(t + 1):
                        m = pe.matmul(ps[:, 7, 0:P], dv[:, k, P * h:P * h + P], tmp[2][:, P * k:P * k + P],
                                      start=(k == 0), stop=(k == t))
                    m.then_inc(*pe_t.tick(("diff out", t, h)))
            for h in range(4):
                pe.wait_ge(*sc_t(("diff square", h)))
                if h:
                    pe.wait_ge(*ve_t(("diff mean", h - 1)))
                pe.matmul(bank(6), ones, tmp[4][:, 0:T], start=True, stop=True).then_inc(*pe_t.tick(("diff mean", h)))

            for i in range(2):
                cols_unit(Unit(U_SU + i), (2 * i, 2 * i + 1), [ve_t(("dv", 1, 2 * i + c)) for c in range(2)])
            pe.wait_ge(s5_in, 16 * 39)
            pe.wait_ge(*sc_t("dt rows"))
            pe.wait_ge(*ve_t(("diff mean", 3)))
            pe.wait_ge(*ve_t(("diff out", 3, 3)))
            for c in range(2):
                pe.transpose(ps[:, 4, 16 * c:16 * c + 16], tmp[0][0:16, P * c:P * c + P], ident[0:16, 0:16])
                for q in range(2):
                    pe.transpose(ps[:, 5, 256 * c + P * q:256 * c + P * q + P], tmp[2 + c][:, P * q:P * q + P], ident)
            pe.transpose(ps[:, 4, 32:48], tmp[1][0:16, P:2 * P], ident[0:16, 0:16]).then_inc(*pe_t.tick("s5 params"))
            for j in range(STEP):
                for q in range(4):
                    if q == 0:
                        pe.wait_ge(*ve_t(("s5 wb", j)))
                    if q >= 2 or j:
                        pe.wait_ge(*sc_t(("s5 wbt", j, q - 2) if q >= 2 else ("s5 wbt", j - 1, q + 2)))
                    else:
                        pe.wait_ge(*ve_t(("su", 3)))
                    for c in range(2):
                        m = pe.transpose(ps[:, q % 2, P * c:P * c + P],
                                         wbj(c)[:, P * q:P * q + P], ident)
                    m.then_inc(*pe_t.tick(("s5 wbt", j, q)))
                    pe.wait_ge(*sc_t(("s5 wbt", j, q)))
                    for b in range(4):
                        for c in range(2):
                            r = slice(32 * b, 32 * b + 32)
                            o = NSTEP * (4 * c + q)
                            m = pe.matmul(ps[:, 4 + b, o:o + NSTEP], tmp[4 + q % 2][r, P * c:P * c + P],
                                          su[r, q, j:T:STEP], start=(j == 0 and q == 0 and c == 0),
                                          stop=(j == STEP - 1), skip_group_check=True)
                    m.then_inc(*pe_t.tick(("s5 add", j, q)))
            for q in range(4):
                pe.wait_ge(*ve_t(("s5 cp", q)))
                if q:
                    pe.wait_ge(*sc_t(("s5 kernel", q - 1, 3)))
                for b in range(4):
                    pair = 4 * q + b
                    for c in range(2):
                        m = pe.matmul(ps[32 * b:32 * b + 32, 2, 0:256],
                                      bbd[c][:, pair, :], cp[c][:, b, 0:STEP, :].rearrange("p t h -> p (t h)"),
                                      start=(c == 0), stop=(c == 1))
                m.then_inc(*pe_t.tick(("s5 kernel", q)))
                pe.wait_ge(*sc_t(("s5 kernel", q, 3)))
                if q == 0:
                    pe.wait_ge(*ve_t("s5 scanned"))
                    pe.wait_ge(*sc_t(("s5 wbt", STEP - 1, 3)))
                if q >= 2:
                    pe.wait_ge(*ve_t(("s5 y", q - 2)))
                o = ps[:, q % 2, :].rearrange("p (c t) -> p c t", t=STEP)
                uu = su[:, q, :].rearrange("p (c t) -> p c t", t=STEP)
                for lag in range(STEP):
                    pe.matmul(o[:, :, lag:STEP], kbd[:, lag, :], uu[:, :, 0:STEP - lag], start=(lag == 0), stop=False,
                              skip_group_check=True)
                for t in range(STEP):
                    for b in range(4):
                        for c in range(2):
                            m = pe.matmul(o[32 * b:32 * b + 32, 1:NSTEP, t], cp[c][:, b, t + 1, :],
                                          st[c][:, 4 * q + b, 0:NSTEP - 1], start=False, stop=False,
                                          skip_group_check=True)
                m.then_inc(*pe_t.tick(("s5 y", q)))
            u = Unit(U_GLU)
            pe.wait_ge(low_ready, u.split)
            pe.wait_ge(*ve_t(("s5 gelu low", 3)))
            pe.wait_ge(*ve_t("s5 scanned"))
            for j in range(4):
                for k in range(4):
                    w = slice(512 * k + P * j, 512 * k + P * j + P)
                    m = three(bank(3 + j), whi[u.slot][:, w], wlo[u.slot][:, w], mohi[:, 4 + k, :], molo[:, 4 + k, :],
                              k == 0, k == 3)
                m.then_inc(consumed, 2)
            pe.wait_ge(*ve_t("s5 squares"))
            pe.matmul(bank(7), ones, tmp[4][:, 0:T], start=True, stop=True).then_inc(*pe_t.tick("s5 mean"))

            pe.wait_ge(*ve_t(("s5 out low", 3)))
            with loop(book, "pe", "g", pe, "i", 4) as i:
                for h in range(2):
                    cols_unit(Unit(U_G + h, i=i), (2 * h, 2 * h + 1),
                              [ve_t(("zg", 2 * h + c), i=i - 1) for c in range(2)])
            pe.wait_ge(*ve_t("gate weights"))
            for t in range(NT):
                x = slice(P * t, P * t + P)
                for k in range(DC):
                    m = three(ps[:, 4, 8 * t:8 * t + 8], xhi[:, k, x], xlo[:, k, x], bah[:, k, :], bal[:, k, :],
                              k == 0, k == DC - 1)
            m.then_inc(*pe_t.tick("gates"))
            for n in range(8):
                pe.wait_ge(*sc_t(("qk square", n)))
                if n >= 2:
                    pe.wait_ge(*ve_t(("qk mean", n - 2)))
                pe.matmul(bank(5 + n % 2), ones, tmp[4 + n % 2][:, 0:T], start=True, stop=True)\
                  .then_inc(*pe_t.tick(("qk mean", n)))
            pe.wait_ge(*ve_t("log decay"))
            for t in range(NT):
                m = pe.matmul(ps[:, 4, 64 + 4 * t:68 + 4 * t], tri, gates[:, 4 * t + 16:4 * t + 20], start=True, stop=True)
            m.then_inc(*pe_t.tick("cumulated"))
            pe.wait_ge(*ve_t("cumulated"))
            pe.wait_ge(*ve_t(("qk normed", 7)))
            kb, qb, gcR, beR, decT, LT, atT, CT, Dm, DT, X, kTok, vbT, kbe, kl, nwT = gb
            vn, qe, S = tmp[3], tmp[4], tmp[5]
            with loop(book, "pe", "blk", pe, "b", NT) as b:
                def v(label):
                    return ve_t(label, b=b)

                def hs(h):
                    return slice(P * h, P * h + P)

                pe.wait_ge(*v("columns"))
                for h in range(GH):
                    pe.matmul(ps[:, 0, hs(h)], gates[:, 56 + h:57 + h].to_broadcast([P, P]), tri, start=True, stop=True)
                    m = pe.matmul(ps[:, 1, hs(h)], gates[:, 60 + h:61 + h].to_broadcast([P, P]), ident, start=True,
                                  stop=True)
                m.then_inc(*pe_t.tick("row forms"))
                pe.wait_ge(*sc_t("blocks", b=b))
                for h in range(GH):
                    pe.matmul(ps[:, 2, hs(h)], kb[:, hs(h)], kb[:, hs(h)], start=True, stop=True)
                    m = pe.matmul(ps[:, 3, hs(h)], kb[:, hs(h)], qb[:, hs(h)], start=True, stop=True)
                m.then_inc(*pe_t.tick("kk"))
                for h in range(GH):
                    pe.transpose(ps[:, 4, hs(h)], kb[:, hs(h)], ident)
                    m = pe.transpose(ps[:, 5, hs(h)], X[:, hs(h)], ident)
                m.then_inc(*pe_t.tick("turned"))
                for s in range(7):
                    pe.wait_ge(*v(("level", s)))
                    if s == 0:
                        pe.wait_ge(*v("kk used"))
                    else:
                        pe.wait_ge(*v(("DT", s - 1)))
                    for h in range(GH):
                        m = pe.matmul(ps[:, 6, hs(h)], CT[:, hs(h)], Dm[:, hs(h)], start=True, stop=True)
                    m.then_inc(*pe_t.tick(("X", s)))
                    pe.wait_ge(*sc_t(("X", s), b=b))
                    for h in range(GH):
                        pe.matmul(ps[:, 0, hs(h)], DT[:, hs(h)], X[:, hs(h)], start=True, stop=True)
                    for h in range(GH):
                        m = pe.matmul(ps[:, 1, hs(h)], X[:, hs(h)], DT[:, hs(h)], start=True, stop=True)
                    m.then_inc(*pe_t.tick(("DD", s)))
                pe.wait_ge(*v(("DT", 6)))
                pe.wait_ge(*v("kbe"))
                for h in range(GH):
                    m = pe.matmul(ps[:, 2, hs(h)], kbe[:, hs(h)], DT[:, hs(h)], start=True, stop=True)
                m.then_inc(*pe_t.tick("w"))
                pe.wait_ge(*sc_t("w", b=b))
                for h in range(GH):
                    pe.matmul(ps[:, 3, hs(h)], DT[:, hs(h)], vbT[:, hs(h)], start=True, stop=False)
                    m = pe.matmul(ps[:, 3, hs(h)], nwT[:, hs(h)], S[:, hs(h)], start=False, stop=True)
                m.then_inc(*pe_t.tick("v new"))
                pe.wait_ge(*v("v new"))
                pe.wait_ge(*v("kl"))
                for h in range(GH):
                    pe.matmul(ps[:, 4, hs(h)], S[:, hs(h)], qe[:, hs(h)], start=True, stop=False)
                    pe.matmul(ps[:, 4, hs(h)], vn[:, hs(h)], atT[:, hs(h)], start=False, stop=True)
                    m = pe.matmul(ps[:, 5, hs(h)], kl[:, hs(h)], vn[:, hs(h)], start=True, stop=True)
                m.then_inc(*pe_t.tick("delta out"))
            for h in range(GH):
                pe.wait_ge(*sc_t(("delta square", h)))
                if h >= 2:
                    pe.wait_ge(*ve_t(("delta mean", h - 2)))
                else:
                    pe.wait_ge(*ve_t("state", b=NT - 1))
                pe.matmul(bank(6 + h % 2), ones, tmp[h % 2][:, 0:T], start=True, stop=True)\
                  .then_inc(*pe_t.tick(("delta mean", h)))
            pe.wait_ge(*ve_t(("delta low", 3)))
            for i in range(6):
                rows_unit(Unit(U_WO + i), lambda k, i=i: mohi[:, 2 * i + k, :], lambda k, i=i: molo[:, 2 * i + k, :],
                          i == 0, i == 5)
            xw_ready("ffn")
            total("ffn")
            ffn(U_UP, "f0")
            total("fin1")

            with loop(book, "pe", "layer", pe, "layer", LAYERS) as l:
                xw_ready("n1", layer=l)
                total("n1", layer=l)
                ffn(V_UP1, "f1", l)
                xw_ready("nm", layer=l)
                total("nm", column=True, layer=l)

                def v(label):
                    return ve_t(label, layer=l)

                def s_(label):
                    return sc_t(label, layer=l)

                for i in range(6):
                    w = [v(("z", 2 * i + c - 4)) for c in range(2)] if i >= 2 else ()
                    cols_unit(Unit(V_WIN + i, l), (2 * i % 4, 2 * i % 4 + 1), w)
                tokens_unit(Unit(V_WIN + 6, l), COLS, 0, [v(("z", 8 + t)) for t in range(NT)])
                tokens_unit(Unit(V_WIN + 7, l), VF - COLS, COLS, [v(("vf", 0, t)) for t in range(NT)])
                for n in range(2):
                    pe.wait_ge(*s_(("mla square", 2 * n)) if n == 0 else s_(("mla square", 2)))
                    if n == 0:
                        pe.matmul(bank(4), ones, tmp[0][:, 0:T], start=True, stop=False)
                        pe.wait_ge(*s_(("mla square", 1)))
                        pe.matmul(bank(4), ones, tmp[1][:, 0:T], start=False, stop=True)\
                          .then_inc(*pe_t.tick("q_a mean"))
                    else:
                        pe.matmul(bank(5), ones, tmp[2][:, 0:T], start=True, stop=True)\
                          .then_inc(*pe_t.tick("kv_a mean"))
                pe.wait_ge(layer_in, l * 128 + 128)
                pe.wait_ge(*v("kv_a"))
                for h in range(HEADS):
                    if h >= 1:
                        pe.wait_ge(*v(("mla q", h - 1)))
                    for k in range(2):
                        m = pe.matmul(ps[0:QD, 4, :], wqb[:, k, QD * h:QD * h + QD], z2[:, k, :], start=(k == 0),
                                      stop=(k == 1))
                    m.then_inc(*pe_t.tick(("mla q", h)))
                    pe.wait_ge(*s_(("mla q", h)))
                    pe.matmul(ps[0:QD, 5, :], turn[0:QD, :], qf[0:QD, h, :], start=True, stop=True)\
                      .then_inc(*pe_t.tick(("mla q turned", h)))
                    pe.matmul(ps[0:HD, 6, :], wkvb[:, h, 0:HD], z2[:, 2, :], start=True, stop=True)\
                      .then_inc(*pe_t.tick(("mla k", h)))
                    if h + 1 < HEADS:
                        pe.wait_ge(*s_(("mla k", h)))
                pe.wait_ge(*v(("mla q", HEADS - 1)))
                pe.matmul(ps[0:QD, 7, :], turn[0:QD, :], z2[0:QD, 3, :], start=True, stop=True)\
                  .then_inc(*pe_t.tick("k rope"))
                for t in range(NT):
                    pe.wait_ge(*v(("vf", 1, t)))
                    m = pe.matmul(ps[:, t, 0:HEADS * HD], z2[:, 2, P * t:P * t + P],
                                  wkvb[:, :, HD:2 * HD], start=True, stop=True)
                    m.then_inc(*pe_t.tick(("mla v", t)))
                pe.wait_ge(*v("log f"))
                pe.wait_ge(*s_(("mla q", HEADS - 1)))
                for t in range(NT):
                    for k in range(t + 1):
                        m = pe.matmul(ps[:, 4, HEADS * t:HEADS * t + HEADS], tri if k == t else ones,
                                      small[:, HEADS * k:HEADS * k + HEADS], start=(k == 0), stop=(k == t))
                m.then_inc(*pe_t.tick("fox sum"))
                pe.wait_ge(*v("pooled"))
                pe.wait_ge(*v("fox columns"))
                pe.wait_ge(*v("kf"))
                pe.wait_ge(*s_(("mla k", HEADS - 1)))
                for k in range(2):
                    m = pe.matmul(bank(4 + k), poolw[:, k, :], z2[:, 4 + k, :], start=True, stop=True)
                m.then_inc(*pe_t.tick("pool out"))
                pe.wait_ge(*v(("pool low", 1)))

                def attention(kind, q_of, k_of, v_of):
                    for h in range(HEADS):
                        if kind == "fox":
                            if h:
                                pe.wait_ge(*s_(("fox row", h - 1)))
                            for t in range(NT):
                                m = pe.matmul(ps[:, 7, P * t:P * t + P],
                                              small[:, 24 + HEADS * t + h:25 + HEADS * t + h].to_broadcast([P, P]),
                                              ident, start=True, stop=True)
                            m.then_inc(*pe_t.tick(("fox row", h)))
                        for t in range(NT):
                            n = P * (t + 1)
                            step = h * NT + t
                            if step >= 2:
                                pe.wait_ge(*v((kind, "scores", step - 2)))
                            pe.matmul(ps[:, step % 2, 0:n], q_of(h, t), k_of(h, n), start=True, stop=True)\
                              .then_inc(*pe_t.tick((kind, "scores", step)))
                            if step >= 1:
                                pe.wait_ge(*s_((kind, "turned", step - 1)))
                            transposes(2, tmp[step % 2], t + 1, (kind, "turned", step), v((kind, "weights", step)))
                            pe.wait_ge(*s_((kind, "turned", step)))
                            if step >= 1:
                                pe.wait_ge(*v((kind, "out", step - 1)))
                            o = slice(64 * (h % 2), 64 * (h % 2) + 64)
                            for k in range(t + 1):
                                m = pe.matmul(ps[o, 3, 0:P], v_of(h, k), tmp[2][:, P * k:P * k + P], start=(k == 0),
                                              stop=(k == t))
                            m.then_inc(*pe_t.tick((kind, "out", step)))

                pe.wait_ge(*v(("mla v", NT - 1)))
                pe.wait_ge(*v("kf"))
                attention("mla", lambda h, t: qf[0:QD, h, P * t:P * t + P], lambda h, n: kf[0:QD, h, 0:n],
                          lambda h, k: mv[:, k, HD * h:HD * h + HD])

                def fr(h):
                    return slice(64 * (h % 2), 64 * (h % 2) + 64)

                pe.wait_ge(*v(("mla", "low", 2)))
                attention("fox", lambda h, t: z2[fr(h), 6 + h // 2, P * t:P * t + P],
                          lambda h, n: z2[fr(h), 9 + h // 2, 0:n], lambda h, k: vf[:, k, HD * h:HD * h + HD])
                pe.wait_ge(*v(("fox", "low", 2)))
                for i in range(4):
                    rows_unit(Unit(V_WO + i, l), lambda k, i=i: xhi[:, 2 * i + k, :], lambda k, i=i: xlo[:, 2 * i + k, :],
                              i == 0, i == 3)
                xw_ready("n2", layer=l)
                total("n2", layer=l)
                ffn(V_UP2, "f2", l)
            total("fin2")
            for t in range(NT):
                for j in range(DC):
                    if t == 0:
                        pe.wait_ge(*ve_t(("y", j)))
                    if t and j % 4 == 0:
                        pe.wait_ge(*ve_t(("out half", t - 1, j // 4)))
                    m = pe.transpose(ps[:, j // 4, P * (j % 4):P * (j % 4) + P], xT[:, j, P * t:P * t + P], ident)
                    if j % 4 == 3:
                        m.then_inc(*pe_t.tick(("out half", t, j // 4)))


        @blk.scalar
        def _(sc):
            def high(u):
                sc.wait_ge(landed[u.slot], u.landed)
                if not u.early:
                    sc.wait_ge(consumed, u.before - 8)
                sc.activation(whi[u.slot][:, :], raw[u.slot][:, :], ACT.Copy).then_inc(high_ready, 1)

            def norm(tag, weight, x_of=None, reads=None, **at):
                x_of = x_of or (lambda j: ve_t(("x", tag, j), **at))
                for j in range(DC):
                    sc.wait_ge(*x_of(j))
                    if j == DC - 2 and reads is not None:
                        sc.wait_ge(consumed, reads.done)
                    if weight is not None:
                        sc.activation(xhi[:, j, :], xT[:, j, :], ACT.Copy, scale=weight(j))\
                          .then_inc(*sc_t.tick(("xw high", tag, j)))
                    if j >= 2:
                        sc.wait_ge(*po_t(("sum", tag, max(j - 2, 1)), **at))
                    sc.activation(tmp[j % 2][:, 0:T], xT[:, j, :], ACT.Square).then_inc(*sc_t.tick(("square", tag, j)))
                sc.wait_ge(*ve_t(("mean", tag), **at))
                sc.activation(rb[:, :], rb[:, :], ACT.Sqrt).then_inc(*sc_t.tick(("sqrt", tag)))

            def ffn(up, name, bias, layer=None):
                at = {} if layer is None else {"layer": layer}
                with loop(book, "sc", name, sc, "i", 11) as i:
                    high(Unit(up + 1, layer, i))
                    for c in range(2):
                        sc.wait_ge(*ve_t(("gate in" if bias else "gate", name, c), i=i, **at))
                        kw = {"bias": small[:, 12 + c:13 + c]} if bias else {}
                        sc.activation(tmp[c][:, 0:T], tmp[c][:, 0:T], ACT.Silu, **kw).then_inc(*sc_t.tick(("silu", name, c)))
                    high(Unit(up + 2, layer, i))
                    for c in range(2):
                        sc.wait_ge(*ve_t(("hidden", name, c), i=i, **at))
                        sc.activation(hhi[:, ds(i * 2 + c, 1), :].rearrange("p a t -> p (a t)"), tmp[4 + c][:, 0:T],
                                      ACT.Copy).then_inc(*sc_t.tick(("hidden high", name, c)))
                dn = up + 22
                high(Unit(dn + 1, layer))
                with loop(book, "sc", name + "d", sc, "i", 4) as i:
                    high(Unit(dn + 2, layer, i))
                    high(Unit(dn + 3, layer, i))
                high(Unit(dn + 10, layer))

            high(Unit(0))
            norm("attn", lambda j: pcol("attn", j))
            for u in range(1, U_SU + 2):
                high(Unit(u))
                if u == U_DV + 1:
                    sc.wait_ge(*ve_t("lambda sums"))
                    sc.activation(small[:, 22:24], small[:, 20:22], ACT.Exp).then_inc(*sc_t.tick("lambda"))
            for t in range(NT):
                n = P * (t + 1)
                for h in range(4):
                    for c in range(2):
                        sc.wait_ge(*ve_t(("diff max", t, h, c)))
                        sc.activation(tmp[c][:, 0:n], tmp[c][:, 0:n], ACT.Exp, bias=small[:, 26 + c:27 + c],
                                      accum_out=small[:, 28 + c:29 + c]).then_inc(*sc_t.tick(("diff exp", t, h, c)))
                    sc.wait_ge(*pe_t(("diff turned", t, h)))
                    if (t, h) != (0, 0):
                        sc.wait_ge(*pe_t(("diff out", *((t, h - 1) if h else (t - 1, 3)))))
                    sc.activation(tmp[2][:, 0:n], ps[:, 6, 0:n], ACT.Copy).then_inc(*sc_t.tick(("diff turned", t, h)))
            for h in range(4):
                sc.wait_ge(*ve_t(("diff out", NT - 1, h)))
                if h:
                    sc.wait_ge(*pe_t(("diff mean", h - 1)))
                sc.activation(tmp[4][:, 0:T], osum[:, h, :], ACT.Square).then_inc(*sc_t.tick(("diff square", h)))
                sc.wait_ge(*ve_t(("diff mean", h)))
                sc.activation(tmp[5][:, 0:T], tmp[5][:, 0:T], ACT.Sqrt).then_inc(*sc_t.tick(("diff sqrt", h)))
                sc.wait_ge(*ve_t(("diff normed", h)))
                sc.activation(mohi[:, 8 + h, :], osum[:, h, :], ACT.Copy, scale=1.0 - LAM_INIT)\
                  .then_inc(*sc_t.tick(("diff high", h)))
            sc.wait_ge(s5_in, 16 * 39)
            sc.activation(tmp[1][0:16, P:2 * P].rearrange("b (e p) -> b e p", e=2),
                          tmp[1][0:16, 0:2].unsqueeze(2).to_broadcast([16, 2, 64]), ACT.Exp).then_inc(*sc_t.tick("dt rows"))
            sc.wait_ge(*ve_t("s5 phase"))
            sc.activation(slot(5), slot(3), ACT.Exp).then_inc(*sc_t.tick("s5 size"))
            sc.activation(slot(7), slot(6), ACT.Sin).then_inc(*sc_t.tick("s5 sin"))
            sc.activation(slot(8), slot(6), ACT.Sin, scale=0.5).then_inc(*sc_t.tick("s5 half sin"))
            for j in range(STEP):
                for q in range(4):
                    sc.wait_ge(*pe_t(("s5 wbt", j, q)))
                    if 4 * j + q >= 2:
                        sc.wait_ge(*pe_t(("s5 add", (4 * j + q - 2) // 4, (q - 2) % 4)))
                    if j == 0 and q == 0:
                        sc.wait_ge(*ve_t("s5 bbar"))
                    sc.activation(tmp[4 + q % 2][:, 0:2 * P], ps[:, q % 2, 0:2 * P], ACT.Copy)\
                      .then_inc(*sc_t.tick(("s5 wbt", j, q)))
            for q in range(4):
                sc.wait_ge(*pe_t(("s5 kernel", q)))
                if q:
                    sc.wait_ge(*pe_t(("s5 y", q - 1)))
                else:
                    sc.wait_ge(*po_t("zero k"))
                for b in range(4):
                    r = slice(32 * b, 32 * b + 32)
                    sc.activation(kbd[r, :, 32 * b:32 * b + 32], ps[r, 2, 0:256].rearrange("p (t h) -> p t h", h=32),
                                  ACT.Copy).then_inc(*sc_t.tick(("s5 kernel", q, b)))
            high(Unit(U_GLU))
            for q in range(4):
                sc.wait_ge(*ve_t(("s5 y", q)))
                sc.activation(su[:, q, :], su[:, q, :], ACT.Gelu_apprx_tanh).then_inc(*sc_t.tick(("s5 gelu", q)))
            for q in range(4):
                sc.wait_ge(*sc_t(("s5 gelu", q)))
                sc.activation(mohi[:, 4 + q, :], su[:, q, :], ACT.Copy).then_inc(*sc_t.tick(("s5 high", q)))
            high(Unit(U_G))
            for j in range(4):
                sc.wait_ge(consumed, Unit(U_GLU).began + 2 * j + 2)
                sc.activation(tmp[j][:, 0:T], bank(3 + j), ACT.Sigmoid, bias=pcol("bglu", j))\
                  .then_inc(*sc_t.tick(("s5 sigmoid", j)))
            sc.wait_ge(*ve_t("s5 mean"))
            sc.activation(tmp[5][:, 0:T], tmp[5][:, 0:T], ACT.Sqrt).then_inc(*sc_t.tick("s5 sqrt"))
            for j in range(4):
                sc.wait_ge(*ve_t(("s5 out", j)))
                sc.activation(mohi[:, 4 + j, :], su[:, j, :], ACT.Copy).then_inc(*sc_t.tick(("s5 out high", j)))
            with loop(book, "sc", "g", sc, "i", 4) as i:
                high(Unit(U_G + 1, i=i))
                high(Unit(U_G + 2, i=i))
            sc.wait_ge(gate_in, 64)
            sc.activation(bah[:, :, :], baw[:, :, :], ACT.Copy).then_inc(*sc_t.tick("gate high"))
            for n in range(12):
                sc.wait_ge(*ve_t(("conv", n)))
                sc.activation(zg[:, n, 3:T + 3], tmp[2 + n % 2][:, 0:T], ACT.Silu).then_inc(*sc_t.tick(("conv silu", n)))
            for h in range(GH):
                sc.wait_ge(*ve_t(("zg", h), i=3))
                sc.activation(zg[:, 12 + h, 3:T + 3], zg[:, 12 + h, 3:T + 3], ACT.Silu)\
                  .then_inc(*sc_t.tick(("z silu", h)))
            for n in range(8):
                if n >= 2:
                    sc.wait_ge(*pe_t(("qk mean", n - 2)))
                sc.wait_ge(*sc_t(("conv silu", n)))
                sc.activation(tmp[4 + n % 2][:, 0:T], zg[:, n, 3:T + 3], ACT.Square)\
                  .then_inc(*sc_t.tick(("qk square", n)))
                sc.wait_ge(*ve_t(("qk mean", n)))
                sc.activation(tmp[n % 2][:, 0:T], tmp[n % 2][:, 0:T], ACT.Sqrt).then_inc(*sc_t.tick(("qk sqrt", n)))
            sc.wait_ge(*ve_t(("ba", NT - 1)))
            sc.activation(gates[:, 0:16].rearrange("p (t h) -> p t h", h=4),
                          small[:, 0:32].rearrange("p (t c) -> p t c", c=8)[:, :, 0:4], ACT.Sigmoid)\
              .then_inc(*sc_t.tick("beta"))
            sc.wait_ge(*ve_t("gate size"))
            sc.activation(small[:, 48:64], small[:, 48:64], ACT.Exp, scale=-1.0).then_inc(*sc_t.tick("gate exp"))
            sc.activation(gates[:, 48:52], gates[:, 48:52], ACT.Exp).then_inc(*sc_t.tick("a exp"))
            sc.wait_ge(*sc_t("gate exp"))
            sc.activation(small[:, 48:64], small[:, 48:64], ACT.Ln, bias=1.0).then_inc(*sc_t.tick("gate ln"))
            with loop(book, "sc", "blk", sc, "b", NT) as b:
                def blk_of(c0):
                    return zg[:, c0:c0 + 4, ds(b * P + 3, P)]

                def heads(x):
                    return x[:, 0:T].rearrange("p (h t) -> p h t", h=GH)

                sc.wait_ge(*ve_t("columns", b=b))
                for c0, dst in ((4, gb[0]), (0, gb[1])):
                    sc.activation(heads(dst), blk_of(c0), ACT.Copy).then_inc(*sc_t.tick(("block", c0)))
                sc.activation(heads(gb[10]), blk_of(8), ACT.Copy).then_inc(*sc_t.tick("blocks"))
                sc.activation(small[:, 68:72], small[:, 64:68], ACT.Exp).then_inc(*sc_t.tick("exp columns"))
                sc.wait_ge(*ve_t("row forms", b=b))
                sc.activation(tmp[0][:, 0:T], gb[2][:, :], ACT.Exp).then_inc(*sc_t.tick("exp rows"))
                sc.wait_ge(*ve_t("decay", b=b))
                sc.activation(gb[4][:, :], gb[4][:, :], ACT.Exp).then_inc(*sc_t.tick("decay"))
                sc.activation(small[:, 76:80], small[:, 76:80], ACT.Exp).then_inc(*sc_t.tick("to last"))
                sc.wait_ge(*pe_t("turned", b=b))
                sc.activation(gb[11][:, :], bank(4), ACT.Copy).then_inc(*sc_t.tick("kTok"))
                for s in range(7):
                    sc.wait_ge(*pe_t(("X", s), b=b))
                    sc.activation(gb[10][:, :], bank(6), ACT.Copy).then_inc(*sc_t.tick(("X", s)))
                sc.wait_ge(*pe_t("w", b=b))
                sc.activation(gb[15][:, :], bank(2), ACT.Copy, scale=-1.0).then_inc(*sc_t.tick("w"))
            for h in range(GH):
                if h >= 2:
                    sc.wait_ge(*pe_t(("delta mean", h - 2)))
                else:
                    sc.wait_ge(*ve_t("state", b=NT - 1))
                sc.activation(tmp[h % 2][:, 0:T], zg[:, h, 3:T + 3], ACT.Square).then_inc(*sc_t.tick(("delta square", h)))
                sc.wait_ge(*ve_t(("delta mean", h)))
                sc.activation(tmp[2 + h % 2][:, 0:T], tmp[2 + h % 2][:, 0:T], ACT.Sqrt)\
                  .then_inc(*sc_t.tick(("delta sqrt", h)))
                sc.wait_ge(*ve_t(("delta normed", h)))
                sc.activation(mohi[:, h, :], zg[:, h, 3:T + 3], ACT.Copy).then_inc(*sc_t.tick(("delta high", h)))
            for u in range(U_WO + 1, U_WO + 6):
                high(Unit(u))
            high(Unit(U_UP))
            norm("ffn", lambda j: pcol("ffn", j))
            ffn(U_UP, "f0", True)
            norm("fin1", None)

            with loop(book, "sc", "layer", sc, "layer", LAYERS) as l:
                def v(label):
                    return ve_t(label, layer=l)

                def p_(label):
                    return pe_t(label, layer=l)

                high(Unit(V_UP1, l))
                norm("n1", lambda j: lv[:, j:j + 1], layer=l)
                ffn(V_UP1, "f1", False, l)
                high(Unit(V_WIN, l))
                norm("nm", lambda j: lv[:, 8 + j:9 + j], layer=l)
                for u in range(V_WIN + 1, V_WIN + 7):
                    high(Unit(u, l))
                u = Unit(V_WIN + 7, l)
                sc.wait_ge(landed[u.slot], u.landed)
                sc.wait_ge(consumed, u.before - 8)
                sc.activation(whi[u.slot][:, :].rearrange("p (k c) -> p k c", k=DC)[:, :, 0:VF - COLS],
                              raw[u.slot][:, :].rearrange("p (k c) -> p k c", k=DC)[:, :, 0:VF - COLS],
                              ACT.Copy).then_inc(high_ready, 1)
                high(Unit(V_WO, l))
                for n in range(3):
                    sc.wait_ge(*v(("z", n)))
                    sc.activation(tmp[n][:, 0:T], z2[:, n, :], ACT.Square).then_inc(*sc_t.tick(("mla square", n)))
                sc.wait_ge(*v("mla means"))
                for n in range(2):
                    sc.activation(tmp[3 + n][:, 0:T], tmp[3 + n][:, 0:T], ACT.Sqrt).then_inc(*sc_t.tick(("mla sqrt", n)))
                for h in range(HEADS):
                    sc.wait_ge(*p_(("mla q", h)))
                    sc.activation(qf[0:QD, h, :], ps[0:QD, 4, :], ACT.Copy, scale=QD ** -0.5)\
                      .then_inc(*sc_t.tick(("mla q", h)))
                    sc.wait_ge(*p_(("mla k", h)))
                    sc.activation(kf[0:HD, h, :], ps[0:HD, 6, :], ACT.Copy).then_inc(*sc_t.tick(("mla k", h)))
                sc.wait_ge(*v("f size"))
                sc.activation(small[:, 24:48], small[:, 24:48], ACT.Exp, scale=-1.0).then_inc(*sc_t.tick("f exp"))
                sc.wait_ge(*sc_t("f exp", layer=l))
                sc.activation(small[:, 24:48], small[:, 24:48], ACT.Ln, bias=1.0).then_inc(*sc_t.tick("f ln"))
                for k in range(2):
                    sc.wait_ge(*v(("pool out", k)))
                    sc.activation(xhi[:, 3 + k, :], z2[:, 4 + k, :], ACT.Copy).then_inc(*sc_t.tick(("pool high", k)))

                def attention(kind, chunk):
                    for h in range(HEADS):
                        if kind == "fox":
                            sc.wait_ge(*p_(("fox row", h)))
                            if h:
                                sc.wait_ge(*v((kind, "scores", NT * h - 1)))
                            sc.activation(tmp[4][:, 0:T], bank(7), ACT.Copy).then_inc(*sc_t.tick(("fox row", h)))
                        for t in range(NT):
                            n, step = P * (t + 1), h * NT + t
                            s = tmp[step % 2][:, 0:n]
                            sc.wait_ge(*v((kind, "max", step)))
                            sc.activation(s, s, ACT.Exp, bias=small[:, 71:72], accum_out=small[:, 72:73])\
                              .then_inc(*sc_t.tick((kind, "exp", step)))
                            sc.wait_ge(*p_((kind, "turned", step)))
                            if step:
                                sc.wait_ge(*p_((kind, "out", step - 1)))
                            sc.activation(tmp[2][:, 0:n], ps[:, 2, 0:n], ACT.Copy)\
                              .then_inc(*sc_t.tick((kind, "turned", step)))
                        if h % 2:
                            sc.wait_ge(*v((kind, "out", NT * h + NT - 1)))
                            sc.activation(xhi[:, chunk + h // 2, :], tmp[3][:, 0:T], ACT.Copy)\
                              .then_inc(*sc_t.tick((kind, "high", h // 2)))

                attention("mla", 0)
                attention("fox", 5)
                for u in range(V_WO + 1, V_WO + 4):
                    high(Unit(u, l))
                high(Unit(V_UP2, l))
                norm("n2", lambda j: lv[:, 16 + j:17 + j], reads=Unit(V_WO + 3, l), layer=l)
                ffn(V_UP2, "f2", False, l)
            norm("fin2", None, lambda j: ve_t(("x", "end", j), layer=LAYERS - 1))

        @blk.vector
        def _(ve):
            def own(**at):
                ve.wait_ge(*ve_t.last(**at))

            def mean(tag, n, dst, src, eps, sqrt_label, **at):
                ve.tensor_scalar(dst, src, 1.0 / n, eps, ALU.mult, ALU.add).then_inc(*ve_t.tick(tag))
                ve.wait_ge(*sc_t(sqrt_label, **at))
                ve.reciprocal(dst, dst).then_inc(*ve_t.tick(("root of", tag)))
                own(**at)

            def residual(tag, unit, scale, weight, x_tag=None, **at):
                for j in range(DC + 2):
                    if j < DC:
                        ve.wait_ge(consumed, unit.began + j + 1)
                        ve.scalar_tensor_tensor(out=xT[:, j, :], in0=bank((j + 4) % 8), scalar=scale, in1=xT[:, j, :],
                                                op0=ALU.mult, op1=ALU.add).then_inc(*ve_t.tick(("x", x_tag or tag, j)))
                    if j >= 2 and weight is not None:
                        low(tag, weight, j - 2, **at)

            def low(tag, weight, j, **at):
                ve.wait_ge(*sc_t(("xw high", tag, j), **at))
                ve.wait_ge(*ve_t(("x", tag, j), **at))
                ve.scalar_tensor_tensor(out=xlo[:, j, :], in0=xT[:, j, :], scalar=weight(j),
                                        in1=xhi[:, j, :].bitcast(F32), op0=ALU.mult, op1=ALU.subtract)\
                  .then_inc(*ve_t.tick(("xw low", tag, j)))

            def root(tag, column=False, wait=True, **at):
                ve.wait_ge(*pe_t(("total", tag), **at))
                ve.tensor_scalar(rb[:, :], bank(7), 1.0 / D, EPS, ALU.mult, ALU.add).then_inc(*ve_t.tick(("mean", tag)))
                ve.wait_ge(*sc_t(("sqrt", tag), **at))
                ve.reciprocal(rb[:, :], rb[:, :]).then_inc(*ve_t.tick(("root", tag)))
                if wait:
                    own(**at)
                if column:
                    ve.wait_ge(*pe_t(("root column", tag), **at))
                    ve.tensor_copy(rcol[:, :], ps[:, 6, 0:NT]).then_inc(*ve_t.tick(("rcol", tag)))
                    own(**at)

            def mul(dst, a, b, label, op=ALU.mult):
                ve.tensor_tensor(dst, a, b, op).then_inc(*ve_t.tick(label))

            def gated(up, name, tag, layer=None):
                at = {} if layer is None else {"layer": layer}
                with loop(book, "ve", name, ve, "i", 11) as i:
                    ve.wait_ge(*ve_t(("hidden", name, 1), i=i - 1, **at))
                    ve.wait_ge(*ve_t(("root", tag), **at))
                    for c in range(2):
                        ve.wait_ge(consumed, Unit(up, layer, i).began + 4 * c + 4)
                        mul(tmp[c][:, 0:T], bank(c), rb[:, :], ("gate", name, c))
                    for c in range(2):
                        ve.wait_ge(consumed, Unit(up + 1, layer, i).began + 4 * c + 4)
                        mul(tmp[2 + c][:, 0:T], bank(2 + c), rb[:, :], ("up", name, c))
                        own(i=i, **at)
                        ve.wait_ge(*sc_t(("silu", name, c), i=i, **at))
                        ve.wait_ge(*po_t(("hidden low", name, c), i=i - 1, **at))
                        mul(tmp[4 + c][:, 0:T], tmp[2 + c][:, 0:T], tmp[c][:, 0:T], ("hidden", name, c))

            def conv_gated(up, name):
                Z = (tmp[2], tmp[3])
                for z in Z:
                    ve.memset(z[:, 0:2], 0.0).then_inc(*ve_t.tick(("pad", z is Z[0])))
                wt = pv[:, PV["fconv"]:PV["fconv"] + 4 * 44].rearrange("p (k g f) -> p k g f", k=4, g=2)
                with loop(book, "ve", name, ve, "i", 11) as i:
                    ve.wait_ge(*ve_t(("hidden", name, 1), i=i - 1))
                    for g in range(2):
                        ve.tensor_copy(small[:, 0:16].rearrange("p (k g c) -> p k g c", k=4, g=2)[:, :, g, :],
                                       wt[:, :, g, ds(i * 2, 2)]).then_inc(*ve_t.tick(("taps", g)))
                    own(i=i)
                    for g in range(2):
                        for c in range(2):
                            n = 2 * g + c
                            ve.wait_ge(consumed, Unit(up + g, None, i).began + 4 * c + 4)
                            z = Z[c]
                            mul(z[:, 2:T + 2], bank(n), rb[:, :], (("gate", "upz")[g], name, c))
                            own(i=i)
                            dst = tmp[4 * g + c][:, 0:T]
                            if g:
                                ve.wait_ge(*po_t(("hidden low", name, c), i=i - 1))
                            ve.tensor_scalar(dst, z[:, 0:T], small[:, n:n + 1], None, ALU.mult)\
                              .then_inc(*ve_t.tick(("tap", name, n, 0)))
                            for k in (1, 2):
                                own(i=i)
                                ve.scalar_tensor_tensor(out=dst, in0=z[:, k:T + k], scalar=small[:, 4 * k + n:4 * k + n + 1],
                                                        in1=dst, op0=ALU.mult, op1=ALU.add)\
                                  .then_inc(*ve_t.tick(("gate in", name, c) if k == 2 and g == 0 else ("tap", name, n, k)))
                            if g:
                                own(i=i)
                                ve.wait_ge(*sc_t(("silu", name, c), i=i))
                                ve.scalar_tensor_tensor(out=dst, in0=dst, scalar=small[:, 14 + c:15 + c],
                                                        in1=tmp[c][:, 0:T], op0=ALU.add, op1=ALU.mult)\
                                  .then_inc(*ve_t.tick(("hidden", name, c)))

            ve.wait_ge(*pe_t("parameters"))
            ve.tensor_copy(pv[:, 0:NPV], ps[:, 7, 0:NPV]).then_inc(*ve_t.tick("parameters"))
            for j in range(DC):
                ve.wait_ge(*pe_t(("x", j)))
                ve.tensor_copy(xT[:, j, :], bank(j)).then_inc(*ve_t.tick(("x", "attn", j)))
                if j >= 1:
                    low("attn", lambda j: pcol("attn", j), j - 1)
            low("attn", lambda j: pcol("attn", j), DC - 1)
            root("attn", column=True)
            for n in range(8):
                ve.wait_ge(consumed, Unit(U_DQK + n // 2).began + 4 * (n % 2) + 4)
                ve.scalar_tensor_tensor(out=dqk[:, n, :], in0=bank(n % 4), scalar=0.125 if n < 4 else 1.0, in1=rb[:, :],
                                        op0=ALU.mult, op1=ALU.mult).then_inc(*ve_t.tick(("dqk", n)))
            ve.wait_ge(lambda_in, 64)
            for k in range(2):
                mul(lamb[:, P * k:P * k + 64], lamb[:, P * k:P * k + 64], lamb[:, P * k + 64:P * k + P], ("lambda", k))
            own()
            ve.tensor_reduce(small[:, 20:22], lamb[:, :].rearrange("p (k d) -> p k d", k=2)[:, :, 0:64], AX, ALU.add)\
              .then_inc(*ve_t.tick("lambda sums"))
            for u in range(2):
                for t in range(NT):
                    ve.wait_ge(consumed, Unit(U_DV + u).began + 2 * t + 2)
                    ve.tensor_scalar(dv[:, t, COLS * u:COLS * u + COLS], ps[:, t, COLS * u:COLS * u + COLS],
                                     rcol[:, t:t + 1], None, ALU.mult).then_inc(*ve_t.tick(("dv", u, t)))
            ve.wait_ge(*sc_t("lambda"))
            mul(small[:, 24:25], small[:, 23:24], small[:, 22:23], "minus lambda", ALU.subtract)
            own()
            ve.tensor_scalar(small[:, 25:26], small[:, 24:25], -LAM_INIT, None, ALU.add).then_inc(*ve_t.tick("- lambda"))
            own()

            def scores(dst, src, t, label, row=None, col=None):
                n, o = P * (t + 1), P * t
                if row is not None:
                    ve.scalar_tensor_tensor(out=dst[:, 0:n], in0=src[:, 0:n], scalar=col, in1=row[:, 0:n],
                                            op0=ALU.add, op1=ALU.subtract).then_inc(*ve_t.tick((label, "shift")))
                    return
                if t:
                    ve.tensor_copy(dst[:, 0:o], src[:, 0:o]).then_inc(*ve_t.tick((label, "copy")))
                mul(dst[:, o:n], src[:, o:n], causal, label, ALU.add)

            for t in range(NT):
                n = P * (t + 1)
                for h in range(4):
                    if (t, h) != (0, 0):
                        ve.wait_ge(*pe_t(("diff turned", *((t, h - 1) if h else (t - 1, 3)))))
                    for c in range(2):
                        ve.wait_ge(*pe_t(("diff scores", t, h, c)))
                        scores(tmp[c], bank(4 + c), t, ("diff scores", t, h, c))
                        own()
                        ve.tensor_reduce(small[:, 32 + c:33 + c], tmp[c][:, 0:n], AX, ALU.max)\
                          .then_inc(*ve_t.tick(("diff most", t, h, c)))
                        own()
                        ve.tensor_scalar(small[:, 26 + c:27 + c], small[:, 32 + c:33 + c], -1.0, None, ALU.mult)\
                          .then_inc(*ve_t.tick(("diff max", t, h, c)))
                    ve.wait_ge(*sc_t(("diff exp", t, h, 1)))
                    ve.reciprocal(small[:, 30:32], small[:, 28:30]).then_inc(*ve_t.tick(("diff inverse", t, h)))
                    own()
                    mul(small[:, 34:35], small[:, 31:32], small[:, 25:26], ("diff share", t, h))
                    ve.tensor_scalar(tmp[0][:, 0:n], tmp[0][:, 0:n], small[:, 30:31], None, ALU.mult)\
                      .then_inc(*ve_t.tick(("diff first", t, h)))
                    own()
                    ve.scalar_tensor_tensor(out=tmp[0][:, 0:n], in0=tmp[1][:, 0:n], scalar=small[:, 34:35],
                                            in1=tmp[0][:, 0:n], op0=ALU.mult, op1=ALU.add)\
                      .then_inc(*ve_t.tick(("diff weights", t, h)))
                    ve.wait_ge(*pe_t(("diff out", t, h)))
                    ve.tensor_copy(osum[:, h, P * t:P * t + P], ps[:, 7, 0:P]).then_inc(*ve_t.tick(("diff out", t, h)))
            for h in range(4):
                ve.wait_ge(*pe_t(("diff mean", h)))
                mean(("diff mean", h), P, tmp[5][:, 0:T], bank(6), EPS, ("diff sqrt", h))
                ve.scalar_tensor_tensor(out=osum[:, h, :], in0=osum[:, h, :], scalar=pcol("diffn", 0),
                                        in1=tmp[5][:, 0:T], op0=ALU.mult, op1=ALU.mult)\
                  .then_inc(*ve_t.tick(("diff normed", h)))
                ve.wait_ge(*sc_t(("diff high", h)))
                own()
                ve.scalar_tensor_tensor(out=molo[:, 8 + h, :], in0=osum[:, h, :], scalar=1.0 - LAM_INIT,
                                        in1=mohi[:, 8 + h, :].bitcast(F32), op0=ALU.mult, op1=ALU.subtract)\
                  .then_inc(*ve_t.tick(("diff low", h)))
            own()
            for c in range(2):
                for e in range(2):
                    ve.memset(bbd[c][64 * e:64 * e + 64, :, 16 * (1 - e):16 * (1 - e) + 16], 0.0)\
                      .then_inc(*ve_t.tick(("zero b", c, e)))
            for n in range(4):
                ve.wait_ge(consumed, Unit(U_SU + n // 2).began + 4 * (n % 2) + 4)
                mul(su[:, n, :], bank(n), rb[:, :], ("su", n))
            ve.wait_ge(*pe_t("s5 params"))
            ve.tensor_scalar(slot(0), ps[:, 4, 0:16], -1e-4, None, ALU.min).then_inc(*ve_t.tick("s5 lr"))
            ve.tensor_copy(slots(1, 3), ps[:, 4, 16:48]).then_inc(*ve_t.tick("s5 li dt"))
            own()
            mul(slot(3), slot(0), slot(2), "s5 zr")
            mul(slot(4), slot(1), slot(2), "s5 zi")
            own()
            ve.tensor_scalar(slot(9), slot(4), 1.0 / (2 * np.pi), ROUND, ALU.mult, ALU.add).then_inc(*ve_t.tick("turns"))
            own()
            ve.tensor_scalar(slot(9), slot(9), -ROUND, None, ALU.add).then_inc(*ve_t.tick("whole turns"))
            own()
            for n, part in enumerate(TWO_PI):
                ve.scalar_tensor_tensor(out=slot(4), in0=slot(9), scalar=-part, in1=slot(4), op0=ALU.mult, op1=ALU.add)\
                  .then_inc(*ve_t.tick(("phase", n)))
                own()
            ve.tensor_scalar(slot(6), slot(4), 3.1415925, -3.1415925, ALU.min, ALU.max).then_inc(*ve_t.tick("s5 phase"))
            for c in range(2):
                ve.wait_ge(*po_t(("zero c", c)))
                for e in range(2):
                    r = slice(64 * e, 64 * e + 64)
                    ve.tensor_scalar(cbd[c][r, :, 16 * e:16 * e + 16],
                                     ps[r, 5, 256 * c:256 * c + 256].rearrange("p (b h) -> p b h", h=16),
                                     -1.0 if c else 1.0, None, ALU.mult).then_inc(*ve_t.tick(("s5 c", c, e)))
            ve.wait_ge(*sc_t("s5 half sin"))
            mul(slot(8), slot(8), slot(8), "s5 sin2")
            own()
            ve.tensor_scalar(slot(8), slot(8), -2.0, 1.0, ALU.mult, ALU.add).then_inc(*ve_t.tick("s5 cos"))
            ve.memset(pw[0][:, 0, :], 1.0).then_inc(*ve_t.tick("s5 one"))
            ve.memset(pw[1][:, 0, :], 0.0).then_inc(*ve_t.tick("s5 zero"))
            own()
            mul(pw[0][:, 1, :], slot(5), slot(8), "s5 p1r")
            mul(pw[1][:, 1, :], slot(5), slot(7), "s5 p1i")
            own()

            def cmul(dst, a, b, label, s=(40, 41), n=1, dims=None):
                t0, t1 = (slots(x, x + n) if dims is None else slots(x, x + n).rearrange(dims[0], **dims[1])
                          for x in (s[0], s[0] + n))
                mul(t0, a[0], b[0], (label, 0))
                mul(t1, a[1], b[1], (label, 1))
                own()
                mul(t0, t0, t1, (label, 2), ALU.subtract)
                own()
                mul(t1, a[0], b[1], (label, 3))
                t2 = slots(s[0] + 2 * n, s[0] + 3 * n)
                t2 = t2 if dims is None else t2.rearrange(dims[0], **dims[1])
                mul(t2, a[1], b[0], (label, 4))
                own()
                mul(dst[1], t1, t2, (label, 5), ALU.add)
                ve.tensor_copy(dst[0], t0).then_inc(*ve_t.tick((label, 6)))
                own()

            def powers(a, b):
                return [pw[c][:, a:b, :] for c in range(2)]

            for m in (1, 2, 4):
                cmul(powers(m + 1, 2 * m + 1), powers(1, m + 1),
                     [pw[c][:, m:m + 1, :].to_broadcast([P, m, PAIRS]) for c in range(2)], ("s5 power", m), n=m,
                     dims=("p (m b) -> p m b", {"m": m}))
            for k in range(6):
                if k == 0:
                    for c in range(2):
                        ve.tensor_copy(lvp[c][:, 0, :], pw[c][:, STEP, :]).then_inc(*ve_t.tick(("s5 level", 0, c)))
                    own()
                else:
                    cmul([lvp[c][:, k, :] for c in range(2)], [lvp[c][:, k - 1, :] for c in range(2)],
                         [lvp[c][:, k - 1, :] for c in range(2)], ("s5 level", k))
            ve.tensor_scalar(slot(10), pw[0][:, 1, :], -1.0, None, ALU.add).then_inc(*ve_t.tick("s5 nr"))
            mul(slot(14), slot(0), slot(0), "s5 lr2")
            mul(slot(15), slot(1), slot(1), "s5 li2")
            own()
            mul(slot(14), slot(14), slot(15), "s5 l2", ALU.add)
            own()
            ve.reciprocal(slot(14), slot(14)).then_inc(*ve_t.tick("s5 1/l2"))
            mul(slot(12), slot(10), slot(0), "s5 w0")
            mul(slot(13), pw[1][:, 1, :], slot(1), "s5 w1")
            mul(slot(15), pw[1][:, 1, :], slot(0), "s5 w2")
            mul(slot(16), slot(10), slot(1), "s5 w3")
            own()
            mul(slot(12), slot(12), slot(13), "s5 w4", ALU.add)
            mul(slot(15), slot(15), slot(16), "s5 w5", ALU.subtract)
            own()
            mul(slot(12), slot(12), slot(14), "s5 w6")
            mul(slot(13), slot(15), slot(14), "s5 w7")
            own()

            def wide(x):
                return x.unsqueeze(2).to_broadcast([P, PAIRS, 32])

            def flat(x):
                return x[:, 0:T].rearrange("p (b h) -> p b h", h=32)

            t4, t5 = flat(tmp[4]), flat(tmp[5])
            B, w_ = [bbd[c][:, :, :] for c in range(2)], [slot(12), slot(13)]
            mul(t4, B[0], wide(w_[0]), "bb0")
            mul(t5, B[1], wide(w_[1]), "bb1")
            own()
            mul(t4, t4, t5, "bb2", ALU.subtract)
            own()
            mul(t5, B[0], wide(w_[1]), "bb3")
            mul(B[1], B[1], wide(w_[0]), "bb4")
            own()
            mul(B[1], B[1], t5, "bb5", ALU.add)
            ve.tensor_copy(B[0], t4).then_inc(*ve_t.tick("s5 bbar"))
            own()
            for j in range(STEP):
                m = STEP - 1 - j
                if j:
                    ve.wait_ge(*pe_t(("s5 wbt", j - 1, 3)))
                Pr, Pi = (wide(pw[c][:, m, :]) for c in range(2))
                t0, t1 = flat(tmp[0]), flat(tmp[1])
                mul(t0, B[0], Pr, ("wb", j, 0))
                mul(t1, B[1], Pi, ("wb", j, 1))
                own()
                mul(flat(tmp[2]), t0, t1, ("wb", j, 2), ALU.subtract)
                own()
                mul(t0, B[0], Pi, ("wb", j, 3))
                mul(t1, B[1], Pr, ("wb", j, 4))
                own()
                mul(flat(tmp[3]), t0, t1, ("s5 wb", j), ALU.add)
            ve.wait_ge(*pe_t(("s5 add", STEP - 1, 3)))
            for c in range(2):
                for b in range(4):
                    ve.tensor_copy(st[c][:, b:PAIRS:4, :],
                                   ps[:, 4 + b, 256 * c:256 * c + 256].rearrange("p (q n) -> p q n", q=4))\
                      .then_inc(*ve_t.tick(("s5 moved", c, b)))
            own()
            for k in range(6):
                d = 1 << k
                for half in range(2):
                    hp = slice(8 * half, 8 * half + 8)
                    w = NSTEP - d
                    tt = [tmp[x][:, 0:8 * w].rearrange("p (b n) -> p b n", b=8) for x in range(4)]
                    ar, ai = (lvp[c][:, k, hp].unsqueeze(2).to_broadcast([P, 8, w]) for c in range(2))
                    Sr, Si = (st[c][:, hp, 0:w] for c in range(2))
                    mul(tt[0], Sr, ar, ("scan", k, half, 0))
                    mul(tt[1], Si, ai, ("scan", k, half, 1))
                    mul(tt[2], Si, ar, ("scan", k, half, 2))
                    mul(tt[3], Sr, ai, ("scan", k, half, 3))
                    own()
                    mul(tt[0], tt[0], tt[1], ("scan", k, half, 4), ALU.subtract)
                    mul(tt[2], tt[2], tt[3], ("scan", k, half, 5), ALU.add)
                    own()
                    for c in range(2):
                        mul(st[c][:, hp, d:NSTEP], st[c][:, hp, d:NSTEP], tt[2 * c], ("scan", k, half, 6 + c), ALU.add)
                    own()
            ve.memset(small[:, 89:90], 0.0).then_inc(*ve_t.tick("s5 scanned"))
            for q in range(4):
                if q:
                    ve.wait_ge(*pe_t(("s5 y", q - 1)))
                    ve.scalar_tensor_tensor(out=su[:, q - 1, :], in0=su[:, q - 1, :], scalar=pcol("s5d", q - 1),
                                            in1=bank((q - 1) % 2), op0=ALU.mult, op1=ALU.add)\
                      .then_inc(*ve_t.tick(("s5 y", q - 1)))
                for b in range(4):
                    pair = 4 * q + b
                    Cr, Ci = (cbd[c][:, pair:pair + 1, :].to_broadcast([P, STEP + 1, 32]) for c in range(2))
                    Pr, Pi = (pw[c][:, :, pair:pair + 1].to_broadcast([P, STEP + 1, 32]) for c in range(2))
                    t4, t5, t3, t2 = (tmp[x][:, 0:288].rearrange("p (t h) -> p t h", h=32) for x in (4, 5, 3, 2))
                    mul(t4, Cr, Pr, ("cp", q, b, 0))
                    mul(t5, Ci, Pi, ("cp", q, b, 1))
                    mul(t3, Ci, Pr, ("cp", q, b, 2))
                    mul(t2, Cr, Pi, ("cp", q, b, 3))
                    own()
                    mul(cp[0][:, b, :, :], t4, t5, ("cp", q, b, 4), ALU.add)
                    mul(cp[1][:, b, :, :], t3, t2, ("s5 cp", q) if b == 3 else ("cp", q, b, 5), ALU.subtract)
                    own()
            ve.wait_ge(*pe_t(("s5 y", 3)))
            ve.scalar_tensor_tensor(out=su[:, 3, :], in0=su[:, 3, :], scalar=pcol("s5d", 3), in1=bank(1),
                                    op0=ALU.mult, op1=ALU.add).then_inc(*ve_t.tick(("s5 y", 3)))
            for q in range(4):
                ve.wait_ge(*sc_t(("s5 high", q)))
                mul(molo[:, 4 + q, :], su[:, q, :], mohi[:, 4 + q, :].bitcast(F32), ("s5 gelu low", q), ALU.subtract)
            for j in range(4):
                ve.wait_ge(*sc_t(("s5 sigmoid", j)))
                mul(su[:, j, :], su[:, j, :], tmp[j][:, 0:T], ("s5 gated", j))
                own()
                mul(tmp[5 if j else 4][:, 0:T], su[:, j, :], su[:, j, :], ("s5 sq", j))
                if j:
                    own()
                    mul(tmp[4][:, 0:T], tmp[4][:, 0:T], tmp[5][:, 0:T], "s5 squares" if j == 3 else ("s5 sum", j), ALU.add)
                    own()
            ve.wait_ge(*pe_t("s5 mean"))
            mean("s5 mean", 512, tmp[5][:, 0:T], bank(7), EPS, "s5 sqrt")
            for j in range(4):
                ve.scalar_tensor_tensor(out=su[:, j, :], in0=su[:, j, :], scalar=pcol("s5n", j), in1=tmp[5][:, 0:T],
                                        op0=ALU.mult, op1=ALU.mult).then_inc(*ve_t.tick(("s5 out", j)))
            for j in range(4):
                ve.wait_ge(*sc_t(("s5 out high", j)))
                mul(molo[:, 4 + j, :], su[:, j, :], mohi[:, 4 + j, :].bitcast(F32), ("s5 out low", j), ALU.subtract)
            own()
            ve.memset(zg[:, 0:12, 0:3], 0.0).then_inc(*ve_t.tick("zg pad"))
            with loop(book, "ve", "g", ve, "i", 4) as i:
                for n in range(4):
                    ve.wait_ge(consumed, Unit(U_G + n // 2, i=i).began + 4 * (n % 2) + 4)
                    mul(zg[:, ds(i * 4 + n, 1), 3:T + 3].rearrange("p a t -> p (a t)"), bank(n), rb[:, :], ("zg", n))
            ve.wait_ge(*sc_t("gate high"))
            mul(bal[:, :, :], baw[:, :, :], bah[:, :, :].bitcast(F32), "gate weights", ALU.subtract)
            own()
            for n in range(12):
                dst = tmp[2 + n % 2][:, 0:T]
                if n >= 2:
                    ve.wait_ge(*sc_t(("conv silu", n - 2)))
                for k in range(4):
                    w = pcol("gconv", 12 * k + n)
                    if k == 0:
                        ve.tensor_scalar(dst, zg[:, n, 0:T], w, None, ALU.mult).then_inc(*ve_t.tick(("gtap", n, 0)))
                    else:
                        own()
                        ve.scalar_tensor_tensor(out=dst, in0=zg[:, n, k:T + k], scalar=w, in1=dst, op0=ALU.mult,
                                                op1=ALU.add).then_inc(*ve_t.tick(("conv", n) if k == 3 else ("gtap", n, k)))
            ve.wait_ge(*pe_t("gates"))
            for t in range(NT):
                ve.tensor_scalar(small[:, 8 * t:8 * t + 8], ps[:, 4, 8 * t:8 * t + 8], rcol[:, t:t + 1], None, ALU.mult)\
                  .then_inc(*ve_t.tick(("ba", t)))
            own()
            sm = small[:, 0:32].rearrange("p (t c) -> p t c", c=8)
            x16 = small[:, 32:48].rearrange("p (t c) -> p t c", c=4)
            mul(x16, sm[:, :, 4:8], gates[:, 52:56].unsqueeze(1).to_broadcast([P, 4, 4]), "gate x", ALU.add)
            own()
            ve.scalar_tensor_tensor(out=small[:, 48:64], in0=small[:, 32:48], scalar=-1.0, in1=small[:, 32:48],
                                    op0=ALU.mult, op1=ALU.max).then_inc(*ve_t.tick("gate size"))
            for n in range(8):
                ve.wait_ge(*pe_t(("qk mean", n)))
                if n < 2:
                    ve.wait_ge(*sc_t(("s5 sigmoid", 3)))
                mean(("qk mean", n), 1.0, tmp[n % 2][:, 0:T], bank(5 + n % 2), EPS, ("qk sqrt", n))
                ve.scalar_tensor_tensor(out=zg[:, n, 3:T + 3], in0=zg[:, n, 3:T + 3],
                                        scalar=GD ** -0.5 if n < 4 else 1.0, in1=tmp[n % 2][:, 0:T], op0=ALU.mult,
                                        op1=ALU.mult).then_inc(*ve_t.tick(("qk normed", n)))
            ve.wait_ge(*sc_t("gate ln"))
            ve.scalar_tensor_tensor(out=small[:, 32:48], in0=small[:, 32:48], scalar=0.0, in1=small[:, 48:64],
                                    op0=ALU.max, op1=ALU.add).then_inc(*ve_t.tick("softplus"))
            own()
            ve.scalar_tensor_tensor(out=gates[:, 16:32].rearrange("p (t c) -> p t c", c=4), in0=x16, scalar=-1.0,
                                    in1=gates[:, 48:52].unsqueeze(1).to_broadcast([P, 4, 4]), op0=ALU.mult,
                                    op1=ALU.mult).then_inc(*ve_t.tick("log decay"))
            ve.wait_ge(*pe_t("cumulated"))
            ve.tensor_copy(gates[:, 32:48], ps[:, 4, 64:80]).then_inc(*ve_t.tick("cumulated"))
            ve.memset(tmp[5][:, 0:T], 0.0).then_inc(*ve_t.tick("state 0"))
            own()
            kb, qb, gcR, beR, decT, LT, atT, CT, Dm, DT, X, kTok, vbT, kbe, kl, nwT = gb
            vn, qe, S = tmp[3], tmp[4], tmp[5]

            def heads(x):
                return x[:, 0:T].rearrange("p (h t) -> p h t", h=GH)

            def per_head(c):
                return small[:, c:c + 4].unsqueeze(2).to_broadcast([P, GH, P])

            def mask(m):
                return m.unsqueeze(1).to_broadcast([P, GH, P])

            with loop(book, "ve", "blk", ve, "b", NT) as b:
                ve.tensor_copy(gates[:, 56:60], gates[:, ds(b * 4 + 16, 4)]).then_inc(*ve_t.tick("col g"))
                ve.tensor_copy(gates[:, 60:64], gates[:, ds(b * 4, 4)]).then_inc(*ve_t.tick("col beta"))
                ve.tensor_copy(small[:, 64:68], gates[:, ds(b * 4 + 32, 4)]).then_inc(*ve_t.tick("columns"))
                ve.wait_ge(*pe_t("row forms", b=b))
                ve.tensor_copy(beR[:, :], bank(1)).then_inc(*ve_t.tick("beta rows"))
                ve.tensor_copy(gcR[:, :], bank(0)).then_inc(*ve_t.tick("row forms"))
                own(b=b)
                mul(small[:, 76:80], heads(gcR)[:, :, P - 1], small[:, 64:68], "to last", ALU.subtract)
                for h in range(GH):
                    ve.tensor_scalar(decT[:, P * h:P * h + P], gcR[:, P * h:P * h + P], small[:, 64 + h:65 + h], 0.0,
                                     ALU.subtract, ALU.min).then_inc(*ve_t.tick("decay" if h == 3 else ("decay", h)))
                ve.wait_ge(*sc_t("decay", b=b))
                mul(heads(decT), heads(decT), mask(tri), "decay masked")
                ve.wait_ge(*pe_t("kk", b=b))
                own(b=b)
                mul(LT[:, :], bank(2), decT[:, :], "L0")
                own(b=b)
                mul(heads(LT), heads(LT), mask(strict), "L1")
                own(b=b)
                mul(LT[:, :], LT[:, :], beR[:, :], "L2")
                mul(atT[:, :], bank(3), decT[:, :], "kk used")
                for n, x in enumerate((Dm, DT)):
                    ve.tensor_copy(heads(x), mask(ident)).then_inc(*ve_t.tick(("eye", n)))
                own(b=b)
                for s in range(7):
                    mul(heads(CT), heads(LT), mask(lvl[:, s, :]), ("level", s))
                    if s == 0:
                        ve.wait_ge(*pe_t("turned", b=b))
                        ve.wait_ge(*sc_t("kTok", b=b))
                        mul(small[:, 72:76], small[:, 68:72], gates[:, 60:64], "beta exp g")
                        mul(heads(vbT), heads(bank(5)), gates[:, 60:64].unsqueeze(2).to_broadcast([P, GH, P]), "vb")
                        own(b=b)
                        mul(heads(kbe), heads(kTok), per_head(72), "kbe")
                        mul(heads(kl), heads(kTok), per_head(76), "kl0")
                        ve.wait_ge(*sc_t("exp rows", b=b))
                        ve.wait_ge(*sc_t("blocks", b=b))
                        mul(qe[:, 0:T], qb[:, :], tmp[0][:, 0:T], "kl")
                    ve.wait_ge(*pe_t(("DD", s), b=b))
                    if s < 6:
                        mul(Dm[:, :], Dm[:, :], bank(0), ("D", s), ALU.subtract)
                    mul(DT[:, :], DT[:, :], bank(1), ("DT", s), ALU.subtract)
                    own(b=b)
                ve.wait_ge(*pe_t("v new", b=b))
                ve.tensor_copy(vn[:, 0:T], bank(3)).then_inc(*ve_t.tick("v new"))
                ve.wait_ge(*pe_t("delta out", b=b))
                ve.tensor_scalar(zg[:, 0:4, ds(b * P + 3, P)], heads(bank(4)), 1.0, None, ALU.mult)\
                  .then_inc(*ve_t.tick("delta out"))
                for h in range(GH):
                    hs = slice(P * h, P * h + P)
                    ve.scalar_tensor_tensor(out=S[:, hs], in0=S[:, hs], scalar=tmp[0][:, P * h + P - 1:P * h + P],
                                            in1=ps[:, 5, hs], op0=ALU.mult, op1=ALU.add)\
                      .then_inc(*ve_t.tick("state" if h == 3 else ("state", h)))
                own(b=b)
            for h in range(GH):
                ve.wait_ge(*pe_t(("delta mean", h)))
                r = tmp[2 + h % 2][:, 0:T]
                mean(("delta mean", h), GD, r, bank(6 + h % 2), EPS, ("delta sqrt", h))
                o = zg[:, h, 3:T + 3]
                ve.scalar_tensor_tensor(out=o, in0=o, scalar=pcol("gdnn", 0), in1=r, op0=ALU.mult, op1=ALU.mult)\
                  .then_inc(*ve_t.tick(("delta root", h)))
                own()
                mul(o, o, zg[:, 12 + h, 3:T + 3], ("delta normed", h))
                ve.wait_ge(*sc_t(("delta high", h)))
                own()
                mul(molo[:, h, :], o, mohi[:, h, :].bitcast(F32), ("delta low", h), ALU.subtract)
            residual("ffn", Unit(U_WO + 5), 1.0, lambda j: pcol("ffn", j))
            root("ffn")
            conv_gated(U_UP, "f0")
            residual("fin1", Unit(U_DN + 10), 1.0, None)
            root("fin1")
            for j in range(DC):
                ve.scalar_tensor_tensor(out=xT[:, j, :], in0=xT[:, j, :], scalar=pcol("fin1", j), in1=rb[:, :],
                                        op0=ALU.mult, op1=ALU.mult).then_inc(*ve_t.tick(("fin1", j)))
            own()

            with loop(book, "ve", "layer", ve, "layer", LAYERS) as l:
                at = {"layer": l}

                def p_(label):
                    return pe_t(label, layer=l)

                def s_(label):
                    return sc_t(label, layer=l)

                ve.tensor_copy(lv[:, :], pv[:, ds(l * LW + PV["layer"], LW)]).then_inc(*ve_t.tick("layer columns"))
                own(**at)
                for j in range(DC):
                    ve.memset(small[:, 80 + j:81 + j], 0.0).then_inc(*ve_t.tick(("x", "n1", j)))
                for j in range(DC):
                    low("n1", lambda j: lv[:, j:j + 1], j, **at)
                root("n1", wait=False, **at)
                gated(V_UP1, "f1", "n1", l)
                residual("nm", Unit(V_DN1 + 10, l), 0.5, lambda j: lv[:, 8 + j:9 + j], **at)
                root("nm", column=True, **at)
                for n in range(12):
                    ve.wait_ge(consumed, Unit(V_WIN + n // 2, l).began + 4 * (n % 2) + 4)
                    ve.scalar_tensor_tensor(out=z2[:, n, :], in0=bank(n % 4), scalar=0.125 if 6 <= n < 9 else 1.0,
                                            in1=rb[:, :], op0=ALU.mult, op1=ALU.mult).then_inc(*ve_t.tick(("z", n)))
                for u in range(2):
                    for t in range(NT):
                        c = slice(COLS * u, COLS if u == 0 else VF)
                        ve.wait_ge(consumed, Unit(V_WIN + 6 + u, l).began + 2 * t + 2)
                        ve.tensor_scalar(vf[:, t, c], ps[:, t, c], rcol[:, t:t + 1], None, ALU.mult)\
                          .then_inc(*ve_t.tick(("vf", u, t)))
                for g in range(2):
                    ve.memset(poolw[HD * g:HD * g + HD, :, HD - HD * g:P - HD * g], 0.0).then_inc(*ve_t.tick(("pool zero", g)))
                ve.wait_ge(*p_("q_a mean"))
                ve.tensor_scalar(tmp[3][:, 0:T], bank(4), 1.0 / 256, EPS, ALU.mult, ALU.add).then_inc(*ve_t.tick("q_a mean"))
                ve.wait_ge(*p_("kv_a mean"))
                ve.tensor_scalar(tmp[4][:, 0:T], bank(5), 1.0 / 128, EPS, ALU.mult, ALU.add).then_inc(*ve_t.tick("mla means"))
                for n in range(2):
                    ve.wait_ge(*s_(("mla sqrt", n)))
                    ve.reciprocal(tmp[3 + n][:, 0:T], tmp[3 + n][:, 0:T]).then_inc(*ve_t.tick(("mla root", n)))
                own(**at)
                for n in range(3):
                    ve.scalar_tensor_tensor(out=z2[:, n, :], in0=z2[:, n, :], scalar=lv[:, 24 + n:25 + n],
                                            in1=tmp[3 + n // 2][:, 0:T], op0=ALU.mult, op1=ALU.mult)\
                      .then_inc(*ve_t.tick("kv_a" if n == 2 else ("q_a", n)))
                ve.wait_ge(layer_in, l * 128 + 128)
                for h in range(HEADS):
                    ve.wait_ge(*p_(("mla q turned", h)))
                    own(**at)
                    mul(tmp[3][0:QD, 0:T], ps[0:QD, 5, :], ropet[0:QD, 1, :], ("mla sin", h))
                    mul(qf[0:QD, h, :], qf[0:QD, h, :], ropet[0:QD, 0, :], ("mla cos", h))
                    own(**at)
                    mul(qf[0:QD, h, :], qf[0:QD, h, :], tmp[3][0:QD, 0:T], ("mla q", h), ALU.add)
                ve.wait_ge(*p_("k rope"))
                own(**at)
                kr = slice(HD, QD)
                mul(tmp[3][kr, 0:T], ps[kr, 7, :], ropet[kr, 1, :], "k sin")
                mul(z2[kr, 3, :], z2[kr, 3, :], ropet[kr, 0, :], "k cos")
                own(**at)
                mul(z2[kr, 3, :], z2[kr, 3, :], tmp[3][kr, 0:T], "k rope", ALU.add)
                own(**at)
                ve.tensor_copy(kf[kr, :, :], z2[kr, 3:4, :].to_broadcast([ROPE, HEADS, T])).then_inc(*ve_t.tick("kf"))
                for t in range(NT):
                    ve.wait_ge(*p_(("mla v", t)))
                    ve.tensor_copy(mv[:, t, :], ps[:, t, 0:HEADS * HD]).then_inc(*ve_t.tick(("mla v", t)))
                x24 = small[:, 0:24].rearrange("p (t h) -> p t h", h=HEADS)
                mul(x24, vf[:, :, 384:390], small[:, 64:70].unsqueeze(1).to_broadcast([P, NT, HEADS]), "f x", ALU.add)
                own(**at)
                ve.scalar_tensor_tensor(out=small[:, 24:48], in0=small[:, 0:24], scalar=-1.0, in1=small[:, 0:24],
                                        op0=ALU.mult, op1=ALU.max).then_inc(*ve_t.tick("f size"))
                ve.wait_ge(*s_("f ln"))
                ve.scalar_tensor_tensor(out=small[:, 0:24], in0=small[:, 0:24], scalar=0.0, in1=small[:, 24:48],
                                        op0=ALU.min, op1=ALU.subtract).then_inc(*ve_t.tick("log f"))
                ve.wait_ge(*p_("fox sum"))
                ve.tensor_copy(small[:, 24:48], ps[:, 4, 0:24]).then_inc(*ve_t.tick("fox columns"))
                for k in range(2):
                    z, src, d, done = z2[:, 4 + k, :], z2[:, 4 + k, :], 1, []
                    for n in range(2 + 2 * k):
                        dst = tmp[3 + n % 2][:, 0:T]
                        own(**at)
                        ve.tensor_copy(dst[:, 0:d], src[:, 0:d]).then_inc(*ve_t.tick(("pool", k, n, 0)))
                        mul(dst[:, d:T], src[:, d:T], src[:, 0:T - d], ("pool", k, n, 1), ALU.add)
                        src, d = dst, 2 * d
                    own(**at)
                    for g in range(2):
                        r = slice(64 * g, 64 * g + 64)
                        w = tmp[3 + g][r, 0:T]
                        mul(w, w, poolt[r, k, :], ("pool mean", k, g))
                        own(**at)
                        mul(z[r, :], w, z[r, :], "pooled" if k and g else ("pooled", k, g), ALU.subtract)
                ve.wait_ge(*p_("pool out"))
                for k in range(2):
                    ve.tensor_scalar(z2[:, 4 + k, :], bank(4 + k), lv[:, 27 + k:28 + k], None, ALU.mult)\
                      .then_inc(*ve_t.tick(("pool out", k)))
                for k in range(2):
                    ve.wait_ge(*s_(("pool high", k)))
                    own(**at)
                    mul(xlo[:, 3 + k, :], z2[:, 4 + k, :], xhi[:, 3 + k, :].bitcast(F32), ("pool low", k), ALU.subtract)

                def attention(kind, chunk):
                    for h in range(HEADS):
                        for t in range(NT):
                            n, step = P * (t + 1), h * NT + t
                            s = tmp[step % 2]
                            ve.wait_ge(*p_((kind, "scores", step)))
                            if step >= 2:
                                ve.wait_ge(*p_((kind, "turned", step - 2)))
                            if kind == "fox":
                                ve.wait_ge(*s_(("fox row", h)))
                                c = 24 + HEADS * t + h
                                ve.scalar_tensor_tensor(out=s[:, 0:n], in0=ps[:, step % 2, 0:n], scalar=small[:, c:c + 1],
                                                        in1=tmp[4][:, 0:n], op0=ALU.add, op1=ALU.subtract)\
                                  .then_inc(*ve_t.tick((kind, "shift", step)))
                                own(**at)
                                mul(s[:, P * t:n], s[:, P * t:n], causal, (kind, "scores", step), ALU.add)
                            else:
                                scores(s, ps[:, step % 2, :], t, (kind, "scores", step))
                            own(**at)
                            ve.tensor_reduce(small[:, 70:71], s[:, 0:n], AX, ALU.max)\
                              .then_inc(*ve_t.tick((kind, "most", step)))
                            own(**at)
                            ve.tensor_scalar(small[:, 71:72], small[:, 70:71], -1.0, None, ALU.mult)\
                              .then_inc(*ve_t.tick((kind, "max", step)))
                            ve.wait_ge(*s_((kind, "exp", step)))
                            ve.reciprocal(small[:, 74:75], small[:, 72:73]).then_inc(*ve_t.tick((kind, "inverse", step)))
                            own(**at)
                            ve.tensor_scalar(s[:, 0:n], s[:, 0:n], small[:, 74:75], None, ALU.mult)\
                              .then_inc(*ve_t.tick((kind, "weights", step)))
                            ve.wait_ge(*p_((kind, "out", step)))
                            if h >= 2 and h % 2 == 0 and t == 0:
                                ve.wait_ge(*s_((kind, "high", h // 2 - 1)))
                            o = slice(64 * (h % 2), 64 * (h % 2) + 64)
                            ve.tensor_copy(tmp[3][o, P * t:P * t + P], ps[o, 3, 0:P])\
                              .then_inc(*ve_t.tick((kind, "out", step)))
                        if h % 2:
                            ve.wait_ge(*s_((kind, "high", h // 2)))
                            own(**at)
                            ch = chunk + h // 2
                            mul(xlo[:, ch, :], tmp[3][:, 0:T], xhi[:, ch, :].bitcast(F32), (kind, "low", h // 2),
                                ALU.subtract)
                            own(**at)

                attention("mla", 0)
                attention("fox", 5)
                residual("n2", Unit(V_WO + 3, l), 1.0, lambda j: lv[:, 16 + j:17 + j], **at)
                root("n2", wait=False, **at)
                gated(V_UP2, "f2", "n2", l)
                residual("end", Unit(V_DN2 + 10, l), 0.5, None)
                own(**at)
            root("fin2")
            for j in range(DC):
                ve.scalar_tensor_tensor(out=xT[:, j, :], in0=xT[:, j, :], scalar=pcol("fin2", j), in1=rb[:, :],
                                        op0=ALU.mult, op1=ALU.mult).then_inc(*ve_t.tick(("y", j)))
            for t in range(NT):
                for k in range(2):
                    ve.wait_ge(*pe_t(("out half", t, k)))
                    ve.tensor_copy(raw_out(t)[:, T * k:T * k + T], bank(k)).then_inc(*ve_t.tick(("out half", t, k)))


def constants():
    i, j = np.arange(P)[:, None], np.arange(P)[None, :]
    cst = np.stack([i == j, i <= j, i < j, np.where(j > i, NEG, 0.0), np.ones((P, P))], 1).astype(np.float32)
    lev = np.stack([(i // (2 * s) == j // (2 * s)) & (j // s % 2 == 1) & (i // s % 2 == 0)
                    for s in (1, 2, 4, 8, 16, 32, 64)], 1).astype(np.float32)
    half = ROPE // 2
    inv = np.float32(10000.0) ** (-np.arange(0, ROPE, 2, dtype=np.float32) / np.float32(ROPE))
    ang = np.arange(T, dtype=np.float32)[None, :] * inv[:, None].astype(np.float32)
    rope = np.zeros((QD, 2, T), np.float32)
    rope[0:HD, 0] = 1.0
    rope[HD:QD, 0] = np.tile(np.cos(ang.astype(np.float64)), (2, 1))
    rope[HD:QD, 1] = np.tile(np.sin(ang.astype(np.float64)), (2, 1))
    turn = np.zeros((QD, QD), np.float32)
    for k in range(half):
        turn[HD + half + k, HD + k] = -1.0
        turn[HD + k, HD + half + k] = 1.0
    counts = np.zeros((P, 2, T), np.float32)
    for g, w in enumerate((2, 4, 8, 16)):
        counts[64 * (g % 2):64 * (g % 2) + 64, g // 2] = 1.0 / np.minimum(np.arange(1, T + 1), w)
    return {"constants": cst, "levels": lev, "rope": rope, "turn": turn, "counts": counts}


def kernel(**inputs):
    import concourse.bacc as bacc
    from concourse.bass_utils import run_bass_kernel_spmd

    def program(known):
        nc = bacc.Bacc("TRN2", target_bir_lowering=False, num_devices=1)
        dram = {n: nc.dram_tensor(f"in_{n}", a.shape, F32, kind="ExternalInput").ap() for n, a in arrays.items()}
        out = nc.dram_tensor("out", (1, T, D), F32, kind="ExternalOutput").ap()
        book = Book(known)
        build(nc, dram, out, book)
        return nc, book

    arrays = {n: np.ascontiguousarray(a) for n, a in inputs.items()} | constants()
    _, counts = program(None)
    nc, _ = program(counts)
    r = run_bass_kernel_spmd(nc, [{f"in_{n}": a for n, a in arrays.items()}], core_ids=[0])
    return r.results[0]["out"]
```

```python
from contextlib import ExitStack, contextmanager

import numpy as np
import concourse.bass as bass
from concourse import mybir

F32 = mybir.dt.float32
F32R = mybir.dt.float32r
I32 = mybir.dt.int32
ALU = mybir.AluOpType
ACT = mybir.ActivationFunctionType
AX = mybir.AxisListType.X
ds = bass.ds

P = 128
T = 512
NT = T // P
D = 1024
DC = D // P
FF = 2816
FC = FF // P
EPS = 1e-6
LAYERS = 2
COLS = 256
NEG = -1.0e30

GH, GD = 4, 128
G_Q, G_Z, G_BA, S_U, D_Q, D_V = 0, 1536, 2048, 2056, 2568, 3592
QA, KVA, POOL, FOX_Q, FOX_V = 0, 256, 416, 672, 1440
IN2 = 1830
HEADS, HD, ROPE, QD = 6, 64, 32, 96
VF = IN2 - FOX_V
S5G, S5H, S5P = 32, 16, 64
PAIRS = S5G // 2
STEP = 8
NSTEP = T // STEP

U_DQK, U_DV, U_SU, U_GLU, U_G, U_WO, U_UP, U_DN, U_FIRST = 0, 4, 6, 8, 9, 17, 23, 45, 56
V_UP1, V_DN1, V_WIN, V_WO, V_UP2, V_DN2, U_LAYER = 0, 22, 33, 41, 45, 67, 78

PV = {}
_at = 0
for _n, _k in (("attn", 8), ("ffn", 8), ("fin1", 8), ("s5d", 4), ("bglu", 4), ("s5n", 4), ("gdnn", 1), ("diffn", 1),
               ("gconv", 48), ("fconv", 132), ("fbias", 44), ("fin2", 8), ("layer", 58)):
    PV[_n] = _at
    _at += _k
NPV = _at
LW = 29
PVT = -(-NPV // P)


LAM_INIT = 0.8 - 0.6 * float(np.exp(0.0))
ROUND = 1.5 * 2.0 ** 23
TWO_PI = (6.28125, 0.0019350051879882812, 2 * np.pi - 6.28125 - 0.0019350051879882812)


class Book:

    def __init__(self, known=None):
        self.known, self.places, self.pers, self.frames = known, {}, {}, {}


class Tally:

    def __init__(self, book, sem, name, engine):
        self.book, self.sem, self.name, self.cursor = book, sem, name, 0
        self.frames = book.frames.setdefault(engine, [])

    def tick(self, label, n=1):
        for f in self.frames:
            f["starts"].setdefault(self, self.cursor)
        self.cursor += n
        key = (self.name, label)
        assert key not in self.book.places, key
        self.book.places[key] = (self.cursor, [f["key"] for f in self.frames])
        self.newest = label
        return self.sem, n

    def __call__(self, label, **at):
        known = self.book.known
        if known is None:
            return self.sem, 1
        count, loops = known.places[(self.name, label)]
        for key in loops:
            count = count + at[key[0]] * known.pers[(self.name, key)]
        if isinstance(count, int):
            assert count >= 0
        return self.sem, count

    def last(self, **at):
        return self(self.newest, **at)


@contextmanager
def loop(book, engine, name, eng, key, n):
    frame = {"key": (key, name), "starts": {}}
    book.frames.setdefault(engine, []).append(frame)
    with eng.Fori(0, n) as i:
        yield i
    book.frames[engine].pop()
    for tally, start in frame["starts"].items():
        per = tally.cursor - start
        book.pers[(tally.name, frame["key"])] = per
        tally.cursor = start + per * n


class Unit:

    def __init__(self, const, layer=None, i=None):
        self.slot, self.first = const % 2, const == 0
        n, half = const, const // 2
        if layer is not None:
            n, half = n + U_FIRST + layer * U_LAYER, half + U_FIRST // 2 + layer * (U_LAYER // 2)
        if i is not None:
            n, half = n + i * 2, half + i
        self.n, self.half = n, half
        self.early = layer is None and i is None and const < 2
        self.landed = (half + 1) * 32
        self.split = n + 1
        self.done = (n + 1) * 8
        self.before = n * 8
        self.began = n * 8


def build(nc, A, out, book):
    with ExitStack() as ctx:
        def sb(name, shape, dt=F32):
            return ctx.enter_context(nc.sbuf_tensor(name, shape, dt))

        def sem(name):
            return ctx.enter_context(nc.semaphore(name))

        xT = sb("xT", [P, DC, T])
        raw = [sb(f"raw{s}", [P, 2048]) for s in range(2)]
        whi = [sb(f"weight_high{s}", [P, 2048], F32R) for s in range(2)]
        wlo = [sb(f"weight_low{s}", [P, 2048], F32R) for s in range(2)]
        cst = sb("constants", [P, 5, P])
        ident, tri, strict, causal, ones = (cst[:, i, :] for i in range(5))
        pv = sb("parameters", [P, PVT * P])
        lv = sb("layer_parameters", [P, LW])
        rb = sb("root", [P, T])
        rcol = sb("root_column", [P, NT])
        tmp = [sb(f"tmp{i}", [P, T + 2]) for i in range(6)]
        small = sb("small", [P, 96])
        xa = ExitStack()
        gb = [xa.enter_context(nc.sbuf_tensor(f"delta{i}", [P, T], F32)) for i in range(16)]
        xa.close()
        xhi = sb("xw_high", [P, DC, T], F32R)
        xlo = sb("xw_low", [P, DC, T], F32R)
        region = ExitStack()

        def tb(name, shape, dt=F32):
            return region.enter_context(nc.sbuf_tensor(name, shape, dt))

        mohi = tb("mixed_high", [P, 12, T], F32R)
        molo = tb("mixed_low", [P, 12, T], F32R)
        sub = ExitStack()

        def ub(name, shape, dt=F32):
            return sub.enter_context(nc.sbuf_tensor(name, shape, dt))

        xin = ub("x_in", [P, NT, D])
        rows = ub("parameter_rows", [P, PVT, P])
        sub.close()
        sub = ExitStack()
        dqk = ub("diff_qk", [P, 8, T])
        dv = ub("diff_v", [P, NT, T])
        osum = ub("diff_out", [P, 4, T])
        lamb = ub("lambda_rows", [P, 4 * 64])
        dx = [ub(f"diff_turn{i}", [P, T]) for i in range(3)]
        sub.close()
        sub = ExitStack()
        su = ub("s5_u", [P, 4, T])
        bbd = [ub(f"s5_b{c}", [P, PAIRS, 32]) for c in "ri"]
        cbd = [ub(f"s5_c{c}", [P, PAIRS, 32]) for c in "ri"]
        lvp = [ub(f"s5_level{c}", [P, 6, PAIRS]) for c in "ri"]
        pw = [ub(f"s5_power{c}", [P, STEP + 1, PAIRS]) for c in "ri"]
        st = [ub(f"s5_state{c}", [P, PAIRS, NSTEP]) for c in "ri"]
        cp = [ub(f"s5_cp{c}", [P, 4, STEP + 1, 32]) for c in "ri"]
        kbd = ub("s5_kernel", [P, STEP, P])
        sub.close()
        sub = ExitStack()
        zg = ub("delta_z", [P, 16, T + 3])
        lvl = ub("level_masks", [P, 7, P])
        baw = ub("gate_weights", [P, DC, 8])
        bah = ub("gate_weights_high", [P, DC, 8], F32R)
        bal = ub("gate_weights_low", [P, DC, 8], F32R)
        gates = ub("gates", [P, 64])
        sub.close()
        region.close()
        region = ExitStack()
        z2 = tb("z", [P, 12, T])
        vf = tb("fox_v_gates", [P, NT, VF + 2])
        qf = tb("mla_q", [P, HEADS, T])
        kf = tb("mla_k", [P, HEADS, T])
        mv = tb("mla_v", [P, NT, HEADS * HD])
        wqb = tb("w_q_b", [P, 2, HEADS * QD])
        wkvb = tb("w_kv_b", [P, HEADS, 2 * HD])
        ropet = tb("rope_tables", [P, 2, T])
        poolt = tb("pool_counts", [P, 2, T])
        poolw = tb("pool_w", [P, 2, P])
        turn = tb("rope_turn", [P, QD])
        ax = [tb(f"attention_turn{i}", [P, T]) for i in range(3)]
        region.close()
        hhi = sb("hidden_high", [P, FC, T], F32R)
        hlo = sb("hidden_low", [P, FC, T], F32R)

        ps = ctx.enter_context(nc.psum_tensor("psum", [P, 8, T], F32))

        landed = [sem(f"unit_landed{s}") for s in range(2)]
        high_ready, low_ready, consumed = sem("high_ready"), sem("low_ready"), sem("units_consumed")
        params_in, x_in, mixer_in, lambda_in, gate_in = (sem(n) for n in
                                                          ("params_in", "x_in_landed", "mixer_in", "lambda_in", "gate_in"))
        s5_in, layer_in, stored = sem("s5_in"), sem("layer_in"), sem("output_stored")
        pe_t = Tally(book, sem("products_ready"), "pe", "pe")
        ve_t = Tally(book, sem("vector_ready"), "ve", "ve")
        sc_t = Tally(book, sem("scalar_ready"), "sc", "sc")
        po_t = Tally(book, sem("pool_ready"), "po", "po")
        dm_t = Tally(book, mixer_in, "dm", "sp")
        blk = ctx.enter_context(nc.Block())

        def prow(name, k):
            r = PV[name] + k
            return r % P, r // P

        def pcol(name, k):
            return pv[:, PV[name] + k:PV[name] + k + 1]

        def bank(i):
            return ps[:, i, :]

        dmap = lambda n, c: (tmp[0], tmp[1], dx[0])[n % 3] if c == 0 else tmp[2 + n % 2]
        dturn = lambda n: (tmp[4], dx[1])[n % 2]
        asc = lambda n: (tmp[0], tmp[1], ax[0], ax[1])[n % 4]
        aturn = lambda n: (tmp[2], ax[2])[n % 2]
        arow = lambda h: tmp[4 + h % 2]
        CHUNKS = (0, 1, 2, 5, 6, 7)
        DN = NT * 4
        AN = 2 * HEADS * NT
        SB, TB_, OB = (0, 1, 4), (2, 5), (3, 6)

        def slots(a, b):
            return st[0][:, :, :].rearrange("p b n -> p (b n)")[:, 16 * a:16 * b]

        def slot(a):
            return slots(a, a + 1)

        def raw_out(t):
            return raw[t // 2][:, D * (t % 2):D * (t % 2) + D]

        def wbj(c):
            return tmp[2 + c][:, 0:T]

        @blk.sync
        def _(sp):
            nparam = 0

            def rows_in(name, src, k):
                nonlocal nparam
                at = PV[name]
                done = 0
                while done < k:
                    m = min(k - done, P - (at + done) % P)
                    sp.dma_start(rows[(at + done) % P:(at + done) % P + m, (at + done) // P, :],
                                 src[done:done + m, :]).then_inc(params_in, 16)
                    done += m
                    nparam += 1

            def of128(ap):
                return ap.rearrange("a (k p) -> (a k) p", p=P)

            sp.dma_start(xin[:, :, :], A["x"][0].rearrange("(t p) d -> p t d", p=P)).then_inc(x_in, 16)
            sp.dma_start(cst[:, :, :], A["constants"]).then_inc(x_in, 16)
            for name, src, k in (("attn", "attn_norm_w", 8), ("ffn", "ffn_norm_w", 8), ("s5d", "s5_d", 4),
                                 ("bglu", "s5_b_glu", 4), ("s5n", "s5_norm_w", 4), ("gdnn", "gdn_norm_w", 1),
                                 ("diffn", "diff_norm_w", 1), ("fbias", "ffn_conv_b", 44)):
                rows_in(name, of128(A[src]), k)
            for name, src in (("fin1", "final_norm_w"), ("fin2", "final_norm_2")):
                rows_in(name, A[src].rearrange("(k p) -> k p", p=P), 8)
            rows_in("gconv", of128(A["gdn_conv_w"][0]), 48)
            rows_in("fconv", of128(A["ffn_conv_w"][0]), 132)
            for l in range(LAYERS):
                at = 29 * l
                for src, k in (("ffn1_norm_2", 8), ("mix_norm_2", 8), ("ffn2_norm_2", 8), ("q_a_norm_2", 2),
                               ("kv_a_norm_2", 1), ("pool_scale_2", 2)):
                    PV["_"] = PV["layer"] + at
                    rows_in("_", A[src][l:l + 1, :].rearrange("a (k p) -> (a k) p", p=P), k)
                    at += k
            book.nparam = nparam

            def free(u):
                if not u.early:
                    sp.wait_ge(high_ready, u.split - 2)
                    sp.wait_ge(low_ready, u.split - 2)

            def load_cols(u, w, c0, c1=None):
                free(u)
                dst = raw[u.slot][:, :].rearrange("p (k c) -> p k c", k=DC)
                src = w.rearrange("(k p) c -> p k c", p=P)
                if c1 is None:
                    for h in range(2):
                        sp.dma_start(dst[:, 4 * h:4 * h + 4, :], src[:, 4 * h:4 * h + 4, ds(c0, COLS)])\
                          .then_inc(landed[u.slot], 16)
                else:
                    for h, c in enumerate((c0, c1)):
                        sp.dma_start(dst[:, :, P * h:P * h + P], src[:, :, ds(c, P)]).then_inc(landed[u.slot], 16)

            def load_rows(u, w, r0):
                free(u)
                for h in range(2):
                    sp.dma_start(raw[u.slot][:, 1024 * h:1024 * h + 1024], w[ds(r0 + P * h, P), :])\
                      .then_inc(landed[u.slot], 16)

            w_in = A["w_in"][0]
            for i in range(4):
                load_cols(Unit(U_DQK + i), w_in, D_Q + COLS * i)
                if i == 1:
                    for n, v in enumerate(("q1", "k1", "q2", "k2")):
                        sp.dma_start(lamb[:, 64 * n:64 * n + 64],
                                     A["diff_lambda_" + v][0:1, :].to_broadcast([P, 64])).then_inc(lambda_in, 16)
            for i in range(2):
                load_cols(Unit(U_DV + i), w_in, D_V + COLS * i)
            for i in range(2):
                load_cols(Unit(U_SU + i), w_in, S_U + COLS * i)
            sp.wait_ge(*ve_t(("diff low", 3)))
            sp.wait_ge(*sc_t(("diff high", 3)))
            for c, n in enumerate(("re", "im")):
                sp.dma_start(tmp[0][0:16, P * c:P * c + P],
                             A[f"s5_lambda_{n}"][0].rearrange("(b e) p -> b (e p)", e=2)).then_inc(s5_in, 16)
                for e in range(2):
                    sp.dma_start(bbd[c][64 * e:64 * e + 64, :, 16 * e:16 * e + 16],
                                 A[f"s5_b_{n}"][0].rearrange("(b e) p h -> e p b h", e=2)[e]).then_inc(s5_in, 16)
                for q in range(2):
                    for b in range(8):
                        sp.dma_start(tmp[2 + c][16 * b:16 * b + 16, P * q:P * q + P].rearrange("h (e p) -> h e p", e=2),
                                     A[f"s5_c_{n}"][0].rearrange("(b e) h p -> b h e p", e=2)[8 * q + b])\
                          .then_inc(s5_in, 16)
            sp.dma_start(tmp[1][0:16, 0:2], A["s5_log_dt"][0].rearrange("(b e) -> b e", e=2)).then_inc(s5_in, 16)
            free(Unit(U_GLU))
            for h in range(2):
                sp.dma_start(raw[Unit(U_GLU).slot][:, 1024 * h:1024 * h + 1024].rearrange("p (k c) -> p k c", k=2),
                             A["s5_w_glu"][0][256 * h:256 * h + 256, :].rearrange("(k p) c -> p k c", p=P))\
                  .then_inc(landed[Unit(U_GLU).slot], 16)
            with loop(book, "sp", "g", sp, "i", 4) as i:
                load_cols(Unit(U_G, i=i), w_in, i * (2 * COLS))
                load_cols(Unit(U_G + 1, i=i), w_in, i * (2 * COLS) + COLS)
            sp.wait_ge(*ve_t(("s5 out low", 3)))
            sp.wait_ge(*po_t("s5 free"))
            sp.dma_start(lvl[:, :, :], A["levels"]).then_inc(gate_in, 16)
            with nc.allow_non_contiguous_dma(reason="eight columns"):
                sp.dma_start(baw[:, :, :], w_in[:, G_BA:G_BA + 8].rearrange("(k p) c -> p k c", p=P))\
                  .then_inc(gate_in, 16)
            sp.dma_start(gates[:, 48:52], A["gdn_a_log"][0:1, :].to_broadcast([P, 4])).then_inc(gate_in, 16)
            sp.dma_start(gates[:, 52:56], A["gdn_dt_bias"][0:1, :].to_broadcast([P, 4])).then_inc(gate_in, 16)
            for i in range(6):
                load_rows(Unit(U_WO + i), A["w_out"][0], 2 * P * i)

            def load_ffn(up, down, w_up, w_down, name, layer=None):
                with loop(book, "sp", name, sp, "i", 11) as i:
                    load_cols(Unit(up, layer, i), w_up, i * COLS)
                    load_cols(Unit(up + 1, layer, i), w_up, i * COLS + FF)
                load_rows(Unit(down, layer), w_down, 0)
                with loop(book, "sp", name + "d", sp, "i", 4) as i:
                    load_rows(Unit(down + 1, layer, i), w_down, i * (4 * P) + 2 * P)
                    load_rows(Unit(down + 2, layer, i), w_down, i * (4 * P) + 4 * P)
                for k in range(2):
                    load_rows(Unit(down + 9 + k, layer), w_down, (9 + k) * 2 * P)

            load_ffn(U_UP, U_DN, A["ffn_w_up"][0], A["ffn_w_down"][0], "f0")
            with loop(book, "sp", "layer", sp, "layer", LAYERS) as l:
                def of(name):
                    a = A[name]
                    return a[ds(l, 1)].rearrange("a r c -> (a r) c")

                load_ffn(V_UP1, V_DN1, of("ffn1_w_gu_2"), of("ffn1_w_down_2"), "f1", l)
                win2 = of("w_in_2")
                load_cols(Unit(V_WIN, l), win2, QA)
                load_cols(Unit(V_WIN + 1, l), win2, KVA, KVA + 64)
                sp.wait_ge(consumed, Unit(V_WIN, l).before)
                sp.dma_start(wqb[:, :, :], of("w_q_b_2").rearrange("(k p) c -> p k c", p=P)).then_inc(layer_in, 16)
                sp.dma_start(wkvb[:, :, :].rearrange("p h c -> p (h c)"), of("w_kv_b_2")).then_inc(layer_in, 16)
                sp.dma_start(ropet[0:QD, :, :], A["rope"]).then_inc(layer_in, 16)
                sp.dma_start(poolt[:, :, :], A["counts"]).then_inc(layer_in, 16)
                sp.dma_start(turn[0:QD, :], A["turn"]).then_inc(layer_in, 16)
                pwl = A["pool_w_2"][ds(l, 1)].rearrange("a (k g) c d -> g (a c) k d", g=2)
                for g in range(2):
                    r = slice(HD * g, HD * g + HD)
                    sp.dma_start(poolw[r, :, r], pwl[g]).then_inc(layer_in, 16)
                sp.dma_start(small[:, 64:70], A["fox_b_f_2"][ds(l, 1), :].to_broadcast([P, HEADS]))\
                  .then_inc(layer_in, 16)
                for k in range(4):
                    load_cols(Unit(V_WIN + 2 + k, l), win2, POOL + COLS * k)
                load_cols(Unit(V_WIN + 6, l), win2, FOX_V)
                u = Unit(V_WIN + 7, l)
                free(u)
                dst = raw[u.slot][:, :].rearrange("p (k c) -> p k c", k=DC)
                src = win2.rearrange("(k p) c -> p k c", p=P)
                for h in range(2):
                    sp.dma_start(dst[:, 4 * h:4 * h + 4, 0:VF - COLS], src[:, 4 * h:4 * h + 4, FOX_V + COLS:IN2])\
                      .then_inc(landed[u.slot], 16)
                for k in range(4):
                    load_rows(Unit(V_WO + k, l), of("w_out_2"), 2 * P * k)
                load_ffn(V_UP2, V_DN2, of("ffn2_w_gu_2"), of("ffn2_w_down_2"), "f2", l)
            for t in range(NT):
                sp.wait_ge(*ve_t(("out half", t, 1)))
                sp.dma_start(out[0, P * t:P * t + P, :], raw_out(t)).then_inc(stored, 16)
            sp.wait_ge(stored, 16 * NT)

        @blk.gpsimd
        def _(po):
            def low(u, n=2048):
                po.wait_ge(high_ready, u.split)
                po.tensor_tensor(wlo[u.slot][:, 0:n], raw[u.slot][:, 0:n], whi[u.slot][:, 0:n].bitcast(F32),
                                 ALU.subtract).then_inc(low_ready, 1)

            def sum_squares(tag, **at):
                for j in range(1, DC):
                    po.wait_ge(*sc_t(("square", tag, j), **at))
                    if j > 1:
                        po.wait_ge(*po_t.last(**at))
                    po.tensor_tensor(tmp[2][:, 0:T], tmp[2 if j > 1 else 0][:, 0:T], tmp[j % 2][:, 0:T], ALU.add)\
                      .then_inc(*po_t.tick(("sum", tag, j)))

            def ffn(up, name, layer=None):
                at = {} if layer is None else {"layer": layer}
                with loop(book, "po", name, po, "i", 11) as i:
                    for h in range(2):
                        low(Unit(up + 1 + h, layer, i))
                    for c in range(2):
                        po.wait_ge(*sc_t(("hidden high", name, c), i=i, **at))
                        po.tensor_tensor(hlo[:, ds(i * 2 + c, 1), :].rearrange("p a t -> p (a t)"), tmp[4 + c][:, 0:T],
                                         hhi[:, ds(i * 2 + c, 1), :].rearrange("p a t -> p (a t)").bitcast(F32),
                                         ALU.subtract).then_inc(*po_t.tick(("hidden low", name, c)))
                dn = up + 22
                low(Unit(dn + 1, layer))
                with loop(book, "po", name + "d", po, "i", 4) as i:
                    low(Unit(dn + 2, layer, i))
                    low(Unit(dn + 3, layer, i))
                low(Unit(dn + 10, layer))

            po.memset(small[:, 95:96], 0.0).then_inc(*po_t.tick("start"))
            low(Unit(0))
            sum_squares("attn")
            for u in range(1, U_SU + 2):
                low(Unit(u))
            po.wait_ge(*ve_t(("diff low", 3)))
            po.wait_ge(*sc_t(("diff high", 3)))
            for c in range(2):
                po.memset(cbd[c][:, :, :], 0.0).then_inc(*po_t.tick(("zero c", c)))
            po.memset(kbd[:, :, :], 0.0).then_inc(*po_t.tick("zero k"))
            low(Unit(U_GLU))
            low(Unit(U_G))
            po.memset(small[:, 94:95], 0.0).then_inc(*po_t.tick("s5 free"))
            with loop(book, "po", "g", po, "i", 4) as i:
                low(Unit(U_G + 1, i=i))
                low(Unit(U_G + 2, i=i))
            for u in range(U_WO + 1, U_WO + 6):
                low(Unit(u))
            low(Unit(U_UP))
            sum_squares("ffn")
            ffn(U_UP, "f0")
            sum_squares("fin1")
            with loop(book, "po", "layer", po, "layer", LAYERS) as l:
                low(Unit(V_UP1, l))
                sum_squares("n1", layer=l)
                ffn(V_UP1, "f1", l)
                low(Unit(V_WIN, l))
                sum_squares("nm", layer=l)
                for u in range(V_WIN + 1, V_WIN + 7):
                    low(Unit(u, l))
                u = Unit(V_WIN + 7, l)
                po.wait_ge(high_ready, u.split)
                lo_part = wlo[u.slot][:, :].rearrange("p (k c) -> p k c", k=DC)[:, :, 0:VF - COLS]
                po.tensor_tensor(lo_part, raw[u.slot][:, :].rearrange("p (k c) -> p k c", k=DC)[:, :, 0:VF - COLS],
                                 whi[u.slot][:, :].rearrange("p (k c) -> p k c", k=DC)[:, :, 0:VF - COLS].bitcast(F32),
                                 ALU.subtract).then_inc(low_ready, 1)
                for u in range(V_WO, V_WO + 4):
                    low(Unit(u, l))
                low(Unit(V_UP2, l))
                sum_squares("n2", layer=l)
                ffn(V_UP2, "f2", l)
            sum_squares("fin2")

        @blk.tensor
        def _(pe):
            def three(dst, lh, ll, rh, rl, start, stop):
                pe.matmul(dst, lh, rh, start=start, stop=False, skip_group_check=True)
                pe.matmul(dst, ll, rh, start=False, stop=False, skip_group_check=True)
                return pe.matmul(dst, lh, rl, start=False, stop=stop, skip_group_check=True)

            def cols_unit(u, banks, waits=()):
                pe.wait_ge(low_ready, u.split)
                for c in range(2):
                    if waits:
                        pe.wait_ge(*waits[c])
                    for k in range(DC):
                        w = slice(COLS * k + P * c, COLS * k + P * c + P)
                        m = three(bank(banks[c]), whi[u.slot][:, w], wlo[u.slot][:, w], xhi[:, k, :], xlo[:, k, :],
                                  k == 0, k == DC - 1)
                    m.then_inc(consumed, 4)

            def tokens_unit(u, n, c0, waits=None):
                pe.wait_ge(low_ready, u.split)
                for t in range(NT):
                    if waits:
                        pe.wait_ge(*waits[t])
                    for k in range(DC):
                        w = slice(COLS * k, COLS * k + n)
                        x = slice(P * t, P * t + P)
                        m = three(ps[:, t, c0:c0 + n], xhi[:, k, x], xlo[:, k, x], whi[u.slot][:, w],
                                  wlo[u.slot][:, w], k == 0, k == DC - 1)
                    m.then_inc(consumed, 2)

            def rows_unit(u, rh, rl, start, stop, first_wait=None):
                pe.wait_ge(low_ready, u.split)
                for j in range(DC):
                    if first_wait and j in first_wait:
                        pe.wait_ge(*first_wait[j])
                    for k in range(2):
                        w = slice(1024 * k + P * j, 1024 * k + P * j + P)
                        m = three(bank((j + 4) % 8), whi[u.slot][:, w], wlo[u.slot][:, w], rh(k), rl(k),
                                  start and k == 0, stop and k == 1)
                    if stop:
                        m.then_inc(consumed, 1)
                if not stop:
                    m.then_inc(consumed, 8)

            def total(tag, column=False, **at):
                pe.wait_ge(*po_t(("sum", tag, DC - 1), **at))
                pe.matmul(bank(7), ones, tmp[2][:, 0:T], start=True, stop=True).then_inc(*pe_t.tick(("total", tag)))
                if column:
                    pe.wait_ge(*ve_t(("root", tag), **at))
                    for t in range(NT):
                        m = pe.matmul(ps[:, 6, t:t + 1], rb[:, P * t:P * t + P], ident[:, 0:1], start=True, stop=True)
                    m.then_inc(*pe_t.tick(("root column", tag)))

            def xw_ready(tag, **at):
                pe.wait_ge(*ve_t(("xw low", tag, DC - 1), **at))

            def ffn(up, name, layer=None):
                at = {} if layer is None else {"layer": layer}
                with loop(book, "pe", name, pe, "i", 11) as i:
                    cols_unit(Unit(up, layer, i), (0, 1), [ve_t(("gate", name, c), i=i - 1, **at) for c in range(2)])
                    cols_unit(Unit(up + 1, layer, i), (2, 3), [ve_t(("up", name, c), i=i - 1, **at) for c in range(2)])
                dn = up + 22

                def hid(hc):
                    return (lambda k: hhi[:, ds(hc + k, 1), :].rearrange("p a t -> p (a t)"),
                            lambda k: hlo[:, ds(hc + k, 1), :].rearrange("p a t -> p (a t)"))

                def ready(i):
                    return po_t(("hidden low", name, 1), i=i, **at)

                last = {4 + c: ve_t(("gate", name, c), i=10, **at) for c in range(2)}
                last |= {6 + c: ve_t(("up", name, c), i=10, **at) for c in range(2)}
                pe.wait_ge(*ready(0))
                rows_unit(Unit(dn, layer), *hid(0), True, False, last)
                with loop(book, "pe", name + "d", pe, "i", 4) as i:
                    pe.wait_ge(*ready(i * 2 + 1))
                    rows_unit(Unit(dn + 1, layer, i), *hid(i * 4 + 2), False, False)
                    pe.wait_ge(*ready(i * 2 + 2))
                    rows_unit(Unit(dn + 2, layer, i), *hid(i * 4 + 4), False, False)
                pe.wait_ge(*ready(9))
                rows_unit(Unit(dn + 9, layer), *hid(18), False, False)
                pe.wait_ge(*ready(10))
                rows_unit(Unit(dn + 10, layer), *hid(20), False, True)

            pe.wait_ge(params_in, 16 * book.nparam)
            pe.wait_ge(x_in, 32)
            for t in range(PVT):
                n = min(P, NPV - P * t)
                m = pe.transpose(ps[:, 7, P * t:P * t + n], rows[0:n, t, :], ident[0:n, 0:n])
            m.then_inc(*pe_t.tick("parameters"))
            for j in range(DC):
                if j == 7:
                    pe.wait_ge(*ve_t("parameters"))
                for t in range(NT):
                    m = pe.transpose(ps[:, j, P * t:P * t + P], xin[:, t, P * j:P * j + P], ident)
                m.then_inc(*pe_t.tick(("x", j)))

            xw_ready("attn")
            total("attn", column=True)
            for i in range(4):
                w = [ve_t(("dqk", 2 * i + c - 4)) for c in range(2)] if i >= 2 else ()
                cols_unit(Unit(U_DQK + i), (2 * i % 4, 2 * i % 4 + 1), w)
            tokens_unit(Unit(U_DV), COLS, 0, [ve_t(("dqk", 4 + t)) for t in range(NT)])
            tokens_unit(Unit(U_DV + 1), COLS, COLS, [ve_t(("dv", 0, t)) for t in range(NT)])

            def transposes(dst, src, n, label):
                for k in range(n):
                    m = pe.transpose(bank(dst)[:, P * k:P * k + P], src[:, P * k:P * k + P], ident)
                m.then_inc(*pe_t.tick(label))

            for slot_n in range(DN + 3):
                n = slot_n
                if n < DN:
                    t, h = divmod(n, 4)
                    if n < 4:
                        pe.wait_ge(*ve_t(("dqk", 4 + n)))
                    if n < 2:
                        for k in range(2):
                            pe.wait_ge(*ve_t(("dv", 1, 2 * n + k)))
                    else:
                        pe.wait_ge(*ve_t(("diff scores", n - 2, 1)))
                    for c in range(2):
                        r = slice(64 * c, 64 * c + 64)
                        pe.matmul(ps[:, 2 * (n % 2) + c, 0:P * (t + 1)], dqk[r, h, P * t:P * t + P],
                                  dqk[r, 4 + h, 0:P * (t + 1)], start=True, stop=True)\
                          .then_inc(*pe_t.tick(("diff scores", n, c)))
                n = slot_n - 2
                if 0 <= n < DN:
                    pe.wait_ge(*ve_t(("diff weights", n)))
                    if n >= 2:
                        pe.wait_ge(*sc_t(("diff turned", n - 2)))
                    transposes(4 + n % 2, dmap(n, 0), n // 4 + 1, ("diff turned", n))
                n = slot_n - 3
                if 0 <= n < DN:
                    t, h = divmod(n, 4)
                    pe.wait_ge(*sc_t(("diff turned", n)))
                    if n >= 2:
                        pe.wait_ge(*ve_t(("diff out", n - 2)))
                    for k in range(t + 1):
                        m = pe.matmul(ps[:, 6 + n % 2, 0:P], dv[:, k, P * h:P * h + P], dturn(n)[:, P * k:P * k + P],
                                      start=(k == 0), stop=(k == t))
                    m.then_inc(*pe_t.tick(("diff out", n)))
            for h in range(4):
                pe.wait_ge(*sc_t(("diff square", h)))
                if h >= 2:
                    pe.wait_ge(*ve_t(("diff mean", h - 2)))
                pe.matmul(bank(4 + h % 2), ones, tmp[h % 2][:, 0:T], start=True, stop=True)\
                  .then_inc(*pe_t.tick(("diff mean", h)))

            for i in range(2):
                cols_unit(Unit(U_SU + i), (2 * i, 2 * i + 1), [ve_t(("diff scores", DN - 2 + i, c)) for c in range(2)])
            pe.wait_ge(s5_in, 16 * 39)
            pe.wait_ge(*sc_t("dt rows"))
            pe.wait_ge(*ve_t(("diff mean", 3)))
            pe.wait_ge(*ve_t(("diff out", DN - 1)))
            for c in range(2):
                pe.transpose(ps[:, 4, 16 * c:16 * c + 16], tmp[0][0:16, P * c:P * c + P], ident[0:16, 0:16])
                for q in range(2):
                    pe.transpose(ps[:, 5, 256 * c + P * q:256 * c + P * q + P], tmp[2 + c][:, P * q:P * q + P], ident)
            pe.transpose(ps[:, 4, 32:48], tmp[1][0:16, P:2 * P], ident[0:16, 0:16]).then_inc(*pe_t.tick("s5 params"))
            for j in range(STEP):
                for q in range(4):
                    if q == 0:
                        pe.wait_ge(*ve_t(("s5 wb", j)))
                    if q >= 2 or j:
                        pe.wait_ge(*sc_t(("s5 wbt", j, q - 2) if q >= 2 else ("s5 wbt", j - 1, q + 2)))
                    else:
                        pe.wait_ge(*ve_t(("su", 3)))
                    for c in range(2):
                        m = pe.transpose(ps[:, q % 2, P * c:P * c + P],
                                         wbj(c)[:, P * q:P * q + P], ident)
                    m.then_inc(*pe_t.tick(("s5 wbt", j, q)))
                    pe.wait_ge(*sc_t(("s5 wbt", j, q)))
                    for b in range(4):
                        for c in range(2):
                            r = slice(32 * b, 32 * b + 32)
                            o = NSTEP * (4 * c + q)
                            m = pe.matmul(ps[:, 4 + b, o:o + NSTEP], tmp[4 + q % 2][r, P * c:P * c + P],
                                          su[r, q, j:T:STEP], start=(j == 0 and q == 0 and c == 0),
                                          stop=(j == STEP - 1), skip_group_check=True)
                    m.then_inc(*pe_t.tick(("s5 add", j, q)))
            for q in range(4):
                pe.wait_ge(*ve_t(("s5 cp", q)))
                if q:
                    pe.wait_ge(*sc_t(("s5 kernel", q - 1, 3)))
                for b in range(4):
                    pair = 4 * q + b
                    for c in range(2):
                        m = pe.matmul(ps[32 * b:32 * b + 32, 2, 0:256],
                                      bbd[c][:, pair, :], cp[c][:, b, 0:STEP, :].rearrange("p t h -> p (t h)"),
                                      start=(c == 0), stop=(c == 1))
                m.then_inc(*pe_t.tick(("s5 kernel", q)))
                pe.wait_ge(*sc_t(("s5 kernel", q, 3)))
                if q == 0:
                    pe.wait_ge(*ve_t("s5 scanned"))
                    pe.wait_ge(*sc_t(("s5 wbt", STEP - 1, 3)))
                if q >= 2:
                    pe.wait_ge(*ve_t(("s5 y", q - 2)))
                o = ps[:, q % 2, :].rearrange("p (c t) -> p c t", t=STEP)
                uu = su[:, q, :].rearrange("p (c t) -> p c t", t=STEP)
                for lag in range(STEP):
                    pe.matmul(o[:, :, lag:STEP], kbd[:, lag, :], uu[:, :, 0:STEP - lag], start=(lag == 0), stop=False,
                              skip_group_check=True)
                for t in range(STEP):
                    for b in range(4):
                        for c in range(2):
                            m = pe.matmul(o[32 * b:32 * b + 32, 1:NSTEP, t], cp[c][:, b, t + 1, :],
                                          st[c][:, 4 * q + b, 0:NSTEP - 1], start=False, stop=False,
                                          skip_group_check=True)
                m.then_inc(*pe_t.tick(("s5 y", q)))
            u = Unit(U_GLU)
            pe.wait_ge(low_ready, u.split)
            pe.wait_ge(*ve_t(("s5 gelu low", 3)))
            pe.wait_ge(*ve_t("s5 scanned"))
            for j in range(4):
                for k in range(4):
                    w = slice(512 * k + P * j, 512 * k + P * j + P)
                    m = three(bank(3 + j), whi[u.slot][:, w], wlo[u.slot][:, w], mohi[:, 4 + k, :], molo[:, 4 + k, :],
                              k == 0, k == 3)
                m.then_inc(consumed, 2)
            pe.wait_ge(*ve_t("s5 squares"))
            pe.matmul(bank(7), ones, tmp[4][:, 0:T], start=True, stop=True).then_inc(*pe_t.tick("s5 mean"))

            pe.wait_ge(*ve_t(("s5 out low", 3)))
            with loop(book, "pe", "g", pe, "i", 4) as i:
                for h in range(2):
                    cols_unit(Unit(U_G + h, i=i), (2 * h, 2 * h + 1),
                              [ve_t(("zg", 2 * h + c), i=i - 1) for c in range(2)])
            pe.wait_ge(*ve_t("gate weights"))
            for t in range(NT):
                x = slice(P * t, P * t + P)
                for k in range(DC):
                    m = three(ps[:, 4, 8 * t:8 * t + 8], xhi[:, k, x], xlo[:, k, x], bah[:, k, :], bal[:, k, :],
                              k == 0, k == DC - 1)
            m.then_inc(*pe_t.tick("gates"))
            for n in range(8):
                pe.wait_ge(*sc_t(("qk square", n)))
                if n >= 2:
                    pe.wait_ge(*ve_t(("qk mean", n - 2)))
                pe.matmul(bank(5 + n % 2), ones, tmp[4 + n % 2][:, 0:T], start=True, stop=True)\
                  .then_inc(*pe_t.tick(("qk mean", n)))
            pe.wait_ge(*ve_t("log decay"))
            for t in range(NT):
                m = pe.matmul(ps[:, 4, 64 + 4 * t:68 + 4 * t], tri, gates[:, 4 * t + 16:4 * t + 20], start=True, stop=True)
            m.then_inc(*pe_t.tick("cumulated"))
            pe.wait_ge(*ve_t("cumulated"))
            pe.wait_ge(*ve_t(("qk normed", 7)))
            kb, qb, gcR, beR, decT, LT, atT, CT, Dm, DT, X, kTok, vbT, kbe, kl, nwT = gb
            vn, qe, S = tmp[3], tmp[4], tmp[5]
            with loop(book, "pe", "blk", pe, "b", NT) as b:
                def v(label):
                    return ve_t(label, b=b)

                def hs(h):
                    return slice(P * h, P * h + P)

                pe.wait_ge(*v("columns"))
                for h in range(GH):
                    pe.matmul(ps[:, 0, hs(h)], gates[:, 56 + h:57 + h].to_broadcast([P, P]), tri, start=True, stop=True)
                    m = pe.matmul(ps[:, 1, hs(h)], gates[:, 60 + h:61 + h].to_broadcast([P, P]), ident, start=True,
                                  stop=True)
                m.then_inc(*pe_t.tick("row forms"))
                pe.wait_ge(*sc_t("blocks", b=b))
                for h in range(GH):
                    pe.matmul(ps[:, 2, hs(h)], kb[:, hs(h)], kb[:, hs(h)], start=True, stop=True)
                    m = pe.matmul(ps[:, 3, hs(h)], kb[:, hs(h)], qb[:, hs(h)], start=True, stop=True)
                m.then_inc(*pe_t.tick("kk"))
                for h in range(GH):
                    pe.transpose(ps[:, 4, hs(h)], kb[:, hs(h)], ident)
                    m = pe.transpose(ps[:, 5, hs(h)], X[:, hs(h)], ident)
                m.then_inc(*pe_t.tick("turned"))
                for s in range(7):
                    pe.wait_ge(*v(("level", s)))
                    if s == 0:
                        pe.wait_ge(*v("kk used"))
                    else:
                        pe.wait_ge(*v(("DT", s - 1)))
                    for h in range(GH):
                        m = pe.matmul(ps[:, 6, hs(h)], CT[:, hs(h)], Dm[:, hs(h)], start=True, stop=True)
                    m.then_inc(*pe_t.tick(("X", s)))
                    pe.wait_ge(*sc_t(("X", s), b=b))
                    for h in range(GH):
                        pe.matmul(ps[:, 0, hs(h)], DT[:, hs(h)], X[:, hs(h)], start=True, stop=True)
                    for h in range(GH):
                        m = pe.matmul(ps[:, 1, hs(h)], X[:, hs(h)], DT[:, hs(h)], start=True, stop=True)
                    m.then_inc(*pe_t.tick(("DD", s)))
                pe.wait_ge(*v(("DT", 6)))
                pe.wait_ge(*v("kbe"))
                for h in range(GH):
                    m = pe.matmul(ps[:, 2, hs(h)], kbe[:, hs(h)], DT[:, hs(h)], start=True, stop=True)
                m.then_inc(*pe_t.tick("w"))
                pe.wait_ge(*sc_t("w", b=b))
                for h in range(GH):
                    pe.matmul(ps[:, 3, hs(h)], DT[:, hs(h)], vbT[:, hs(h)], start=True, stop=False)
                    m = pe.matmul(ps[:, 3, hs(h)], nwT[:, hs(h)], S[:, hs(h)], start=False, stop=True)
                m.then_inc(*pe_t.tick("v new"))
                pe.wait_ge(*v("v new"))
                pe.wait_ge(*v("kl"))
                for h in range(GH):
                    pe.matmul(ps[:, 4, hs(h)], S[:, hs(h)], qe[:, hs(h)], start=True, stop=False)
                    pe.matmul(ps[:, 4, hs(h)], vn[:, hs(h)], atT[:, hs(h)], start=False, stop=True)
                    m = pe.matmul(ps[:, 5, hs(h)], kl[:, hs(h)], vn[:, hs(h)], start=True, stop=True)
                m.then_inc(*pe_t.tick("delta out"))
            for h in range(GH):
                pe.wait_ge(*sc_t(("delta square", h)))
                if h >= 2:
                    pe.wait_ge(*ve_t(("delta mean", h - 2)))
                else:
                    pe.wait_ge(*ve_t("state", b=NT - 1))
                pe.matmul(bank(6 + h % 2), ones, tmp[h % 2][:, 0:T], start=True, stop=True)\
                  .then_inc(*pe_t.tick(("delta mean", h)))
            pe.wait_ge(*ve_t(("delta low", 3)))
            for i in range(6):
                rows_unit(Unit(U_WO + i), lambda k, i=i: mohi[:, 2 * i + k, :], lambda k, i=i: molo[:, 2 * i + k, :],
                          i == 0, i == 5)
            xw_ready("ffn")
            total("ffn")
            ffn(U_UP, "f0")
            total("fin1")

            with loop(book, "pe", "layer", pe, "layer", LAYERS) as l:
                xw_ready("n1", layer=l)
                total("n1", layer=l)
                ffn(V_UP1, "f1", l)
                xw_ready("nm", layer=l)
                total("nm", column=True, layer=l)

                def v(label):
                    return ve_t(label, layer=l)

                def s_(label):
                    return sc_t(label, layer=l)

                for i in range(6):
                    w = [v(("z", 2 * i + c - 4)) for c in range(2)] if i >= 2 else ()
                    cols_unit(Unit(V_WIN + i, l), (2 * i % 4, 2 * i % 4 + 1), w)
                tokens_unit(Unit(V_WIN + 6, l), COLS, 0, [v(("z", 8 + t)) for t in range(NT)])
                tokens_unit(Unit(V_WIN + 7, l), VF - COLS, COLS, [v(("vf", 0, t)) for t in range(NT)])
                for n in range(2):
                    pe.wait_ge(*s_(("mla square", 2 * n)) if n == 0 else s_(("mla square", 2)))
                    if n == 0:
                        pe.matmul(bank(4), ones, tmp[0][:, 0:T], start=True, stop=False)
                        pe.wait_ge(*s_(("mla square", 1)))
                        pe.matmul(bank(4), ones, tmp[1][:, 0:T], start=False, stop=True)\
                          .then_inc(*pe_t.tick("q_a mean"))
                    else:
                        pe.matmul(bank(5), ones, tmp[2][:, 0:T], start=True, stop=True)\
                          .then_inc(*pe_t.tick("kv_a mean"))
                pe.wait_ge(layer_in, l * 128 + 128)
                pe.wait_ge(*v("kv_a"))
                for h in range(HEADS):
                    if h >= 1:
                        pe.wait_ge(*v(("mla q", h - 1)))
                    for k in range(2):
                        m = pe.matmul(ps[0:QD, 4, :], wqb[:, k, QD * h:QD * h + QD], z2[:, k, :], start=(k == 0),
                                      stop=(k == 1))
                    m.then_inc(*pe_t.tick(("mla q", h)))
                    pe.wait_ge(*s_(("mla q", h)))
                    pe.matmul(ps[0:QD, 5, :], turn[0:QD, :], qf[0:QD, h, :], start=True, stop=True)\
                      .then_inc(*pe_t.tick(("mla q turned", h)))
                    pe.matmul(ps[0:HD, 6, :], wkvb[:, h, 0:HD], z2[:, 2, :], start=True, stop=True)\
                      .then_inc(*pe_t.tick(("mla k", h)))
                    if h + 1 < HEADS:
                        pe.wait_ge(*s_(("mla k", h)))
                pe.wait_ge(*v(("mla q", HEADS - 1)))
                pe.matmul(ps[0:QD, 7, :], turn[0:QD, :], z2[0:QD, 3, :], start=True, stop=True)\
                  .then_inc(*pe_t.tick("k rope"))
                for t in range(NT):
                    pe.wait_ge(*v(("vf", 1, t)))
                    m = pe.matmul(ps[:, t, 0:HEADS * HD], z2[:, 2, P * t:P * t + P],
                                  wkvb[:, :, HD:2 * HD], start=True, stop=True)
                    m.then_inc(*pe_t.tick(("mla v", t)))
                pe.wait_ge(*v("log f"))
                pe.wait_ge(*s_(("mla q", HEADS - 1)))
                for t in range(NT):
                    for k in range(t + 1):
                        m = pe.matmul(ps[:, 4, HEADS * t:HEADS * t + HEADS], tri if k == t else ones,
                                      small[:, HEADS * k:HEADS * k + HEADS], start=(k == 0), stop=(k == t))
                m.then_inc(*pe_t.tick("fox sum"))
                pe.wait_ge(*v("pooled"))
                pe.wait_ge(*v("fox columns"))
                pe.wait_ge(*v("kf"))
                pe.wait_ge(*s_(("mla k", HEADS - 1)))
                for k in range(2):
                    m = pe.matmul(bank(4 + k), poolw[:, k, :], z2[:, 4 + k, :], start=True, stop=True)
                m.then_inc(*pe_t.tick("pool out"))
                pe.wait_ge(*v(("pool low", 1)))

                def fr(h):
                    return slice(64 * (h % 2), 64 * (h % 2) + 64)

                def operands(n):
                    kind, h, t = n // (HEADS * NT), n // NT % HEADS, n % NT
                    if kind == 0:
                        return (qf[0:QD, h, P * t:P * t + P], kf[0:QD, h, 0:P * (t + 1)],
                                lambda k: mv[:, k, HD * h:HD * h + HD], h, t)
                    return (z2[fr(h), 6 + h // 2, P * t:P * t + P], z2[fr(h), 9 + h // 2, 0:P * (t + 1)],
                            lambda k: vf[:, k, HD * h:HD * h + HD], h, t)

                pe.wait_ge(*v(("mla v", NT - 1)))
                pe.wait_ge(*v("kf"))
                for slot_n in range(AN + 3):
                    n = slot_n
                    if n < AN:
                        q, k, _, h, t = operands(n)
                        if n >= AN // 2 and t == 0:
                            if h:
                                pe.wait_ge(*s_(("fox row", h - 1)))
                            for b in range(NT):
                                m = pe.matmul(ps[:, 7, P * b:P * b + P],
                                              small[:, 24 + HEADS * b + h:25 + HEADS * b + h].to_broadcast([P, P]),
                                              ident, start=True, stop=True)
                            m.then_inc(*pe_t.tick(("fox row", h)))
                        if n >= 3:
                            pe.wait_ge(*v(("scores", n - 3)))
                        pe.matmul(ps[:, SB[n % 3], 0:P * (t + 1)], q, k, start=True, stop=True)\
                          .then_inc(*pe_t.tick(("scores", n)))
                    n = slot_n - 2
                    if 0 <= n < AN:
                        pe.wait_ge(*v(("weights", n)))
                        if n >= 2:
                            pe.wait_ge(*s_(("turned", n - 2)))
                        transposes(TB_[n % 2], asc(n), n % NT + 1, ("turned", n))
                    n = slot_n - 3
                    if 0 <= n < AN:
                        _, _, vals, h, t = operands(n)
                        pe.wait_ge(*s_(("turned", n)))
                        if n >= 2:
                            pe.wait_ge(*v(("out", n - 2)))
                        for k in range(t + 1):
                            m = pe.matmul(ps[fr(h), OB[n % 2], 0:P], vals(k), aturn(n)[:, P * k:P * k + P],
                                          start=(k == 0), stop=(k == t))
                        m.then_inc(*pe_t.tick(("out", n)))
                pe.wait_ge(*v(("low", 5)))
                for i in range(4):
                    rows_unit(Unit(V_WO + i, l), lambda k, i=i: xhi[:, 2 * i + k, :], lambda k, i=i: xlo[:, 2 * i + k, :],
                              i == 0, i == 3)
                xw_ready("n2", layer=l)
                total("n2", layer=l)
                ffn(V_UP2, "f2", l)
            total("fin2")
            for t in range(NT):
                for j in range(DC):
                    if t == 0:
                        pe.wait_ge(*ve_t(("y", j)))
                    if t and j % 4 == 0:
                        pe.wait_ge(*ve_t(("out half", t - 1, j // 4)))
                    m = pe.transpose(ps[:, j // 4, P * (j % 4):P * (j % 4) + P], xT[:, j, P * t:P * t + P], ident)
                    if j % 4 == 3:
                        m.then_inc(*pe_t.tick(("out half", t, j // 4)))


        @blk.scalar
        def _(sc):
            def high(u):
                sc.wait_ge(landed[u.slot], u.landed)
                if not u.early:
                    sc.wait_ge(consumed, u.before - 8)
                sc.activation(whi[u.slot][:, :], raw[u.slot][:, :], ACT.Copy).then_inc(high_ready, 1)

            def norm(tag, weight, x_of=None, reads=None, **at):
                x_of = x_of or (lambda j: ve_t(("x", tag, j), **at))
                for j in range(DC):
                    sc.wait_ge(*x_of(j))
                    if j == DC - 2 and reads is not None:
                        sc.wait_ge(consumed, reads.done)
                    if weight is not None:
                        sc.activation(xhi[:, j, :], xT[:, j, :], ACT.Copy, scale=weight(j))\
                          .then_inc(*sc_t.tick(("xw high", tag, j)))
                    if j >= 2:
                        sc.wait_ge(*po_t(("sum", tag, max(j - 2, 1)), **at))
                    sc.activation(tmp[j % 2][:, 0:T], xT[:, j, :], ACT.Square).then_inc(*sc_t.tick(("square", tag, j)))
                sc.wait_ge(*ve_t(("mean", tag), **at))
                sc.activation(rb[:, :], rb[:, :], ACT.Sqrt).then_inc(*sc_t.tick(("sqrt", tag)))

            def ffn(up, name, bias, layer=None):
                at = {} if layer is None else {"layer": layer}
                with loop(book, "sc", name, sc, "i", 11) as i:
                    high(Unit(up + 1, layer, i))
                    for c in range(2):
                        sc.wait_ge(*ve_t(("gate in" if bias else "gate", name, c), i=i, **at))
                        kw = {"bias": small[:, 12 + c:13 + c]} if bias else {}
                        sc.activation(tmp[c][:, 0:T], tmp[c][:, 0:T], ACT.Silu, **kw).then_inc(*sc_t.tick(("silu", name, c)))
                    high(Unit(up + 2, layer, i))
                    for c in range(2):
                        sc.wait_ge(*ve_t(("hidden", name, c), i=i, **at))
                        sc.activation(hhi[:, ds(i * 2 + c, 1), :].rearrange("p a t -> p (a t)"), tmp[4 + c][:, 0:T],
                                      ACT.Copy).then_inc(*sc_t.tick(("hidden high", name, c)))
                dn = up + 22
                high(Unit(dn + 1, layer))
                with loop(book, "sc", name + "d", sc, "i", 4) as i:
                    high(Unit(dn + 2, layer, i))
                    high(Unit(dn + 3, layer, i))
                high(Unit(dn + 10, layer))

            high(Unit(0))
            norm("attn", lambda j: pcol("attn", j))
            for u in range(1, U_SU + 2):
                high(Unit(u))
                if u == U_DV + 1:
                    sc.wait_ge(*ve_t("lambda sums"))
                    sc.activation(small[:, 22:24], small[:, 20:22], ACT.Exp).then_inc(*sc_t.tick("lambda"))
            for slot_n in range(DN + 2):
                n = slot_n
                if n < DN:
                    w, s0 = P * (n // 4 + 1), 26 + 8 * (n % 2)
                    for c in range(2):
                        sc.wait_ge(*ve_t(("diff max", n, c)))
                        x = dmap(n, c)[:, 0:w]
                        sc.activation(x, x, ACT.Exp, bias=small[:, s0 + c:s0 + c + 1],
                                      accum_out=small[:, s0 + 2 + c:s0 + 3 + c]).then_inc(*sc_t.tick(("diff exp", n, c)))
                n = slot_n - 2
                if 0 <= n < DN:
                    w = P * (n // 4 + 1)
                    sc.wait_ge(*pe_t(("diff turned", n)))
                    if n >= 2:
                        sc.wait_ge(*pe_t(("diff out", n - 2)))
                    sc.activation(dturn(n)[:, 0:w], ps[:, 4 + n % 2, 0:w], ACT.Copy).then_inc(*sc_t.tick(("diff turned", n)))
            for h in range(4):
                sc.wait_ge(*ve_t(("diff out", DN - 4 + h)))
                if h >= 2:
                    sc.wait_ge(*pe_t(("diff mean", h - 2)))
                elif h == 0:
                    sc.wait_ge(*pe_t(("diff turned", DN - 1)))
                sc.activation(tmp[h % 2][:, 0:T], osum[:, h, :], ACT.Square).then_inc(*sc_t.tick(("diff square", h)))
            for h in range(4):
                sc.wait_ge(*ve_t(("diff mean", h)))
                sc.activation(dx[0][:, :] if h == 3 else tmp[2 + h][:, 0:T], dx[0][:, :] if h == 3 else tmp[2 + h][:, 0:T],
                              ACT.Sqrt).then_inc(*sc_t.tick(("diff sqrt", h)))
            for h in range(4):
                sc.wait_ge(*ve_t(("diff normed", h)))
                sc.activation(mohi[:, 8 + h, :], osum[:, h, :], ACT.Copy, scale=1.0 - LAM_INIT)\
                  .then_inc(*sc_t.tick(("diff high", h)))
            sc.wait_ge(s5_in, 16 * 39)
            sc.activation(tmp[1][0:16, P:2 * P].rearrange("b (e p) -> b e p", e=2),
                          tmp[1][0:16, 0:2].unsqueeze(2).to_broadcast([16, 2, 64]), ACT.Exp).then_inc(*sc_t.tick("dt rows"))
            sc.wait_ge(*ve_t("s5 phase"))
            sc.activation(slot(5), slot(3), ACT.Exp).then_inc(*sc_t.tick("s5 size"))
            sc.activation(slot(7), slot(6), ACT.Sin).then_inc(*sc_t.tick("s5 sin"))
            sc.activation(slot(8), slot(6), ACT.Sin, scale=0.5).then_inc(*sc_t.tick("s5 half sin"))
            for j in range(STEP):
                for q in range(4):
                    sc.wait_ge(*pe_t(("s5 wbt", j, q)))
                    if 4 * j + q >= 2:
                        sc.wait_ge(*pe_t(("s5 add", (4 * j + q - 2) // 4, (q - 2) % 4)))
                    if j == 0 and q == 0:
                        sc.wait_ge(*ve_t("s5 bbar"))
                    sc.activation(tmp[4 + q % 2][:, 0:2 * P], ps[:, q % 2, 0:2 * P], ACT.Copy)\
                      .then_inc(*sc_t.tick(("s5 wbt", j, q)))
            for q in range(4):
                sc.wait_ge(*pe_t(("s5 kernel", q)))
                if q:
                    sc.wait_ge(*pe_t(("s5 y", q - 1)))
                else:
                    sc.wait_ge(*po_t("zero k"))
                for b in range(4):
                    r = slice(32 * b, 32 * b + 32)
                    sc.activation(kbd[r, :, 32 * b:32 * b + 32], ps[r, 2, 0:256].rearrange("p (t h) -> p t h", h=32),
                                  ACT.Copy).then_inc(*sc_t.tick(("s5 kernel", q, b)))
            high(Unit(U_GLU))
            for q in range(4):
                sc.wait_ge(*ve_t(("s5 y", q)))
                sc.activation(su[:, q, :], su[:, q, :], ACT.Gelu_apprx_tanh).then_inc(*sc_t.tick(("s5 gelu", q)))
            for q in range(4):
                sc.wait_ge(*sc_t(("s5 gelu", q)))
                sc.activation(mohi[:, 4 + q, :], su[:, q, :], ACT.Copy).then_inc(*sc_t.tick(("s5 high", q)))
            high(Unit(U_G))
            for j in range(4):
                sc.wait_ge(consumed, Unit(U_GLU).began + 2 * j + 2)
                sc.activation(tmp[j][:, 0:T], bank(3 + j), ACT.Sigmoid, bias=pcol("bglu", j))\
                  .then_inc(*sc_t.tick(("s5 sigmoid", j)))
            sc.wait_ge(*ve_t("s5 mean"))
            sc.activation(tmp[5][:, 0:T], tmp[5][:, 0:T], ACT.Sqrt).then_inc(*sc_t.tick("s5 sqrt"))
            for j in range(4):
                sc.wait_ge(*ve_t(("s5 out", j)))
                sc.activation(mohi[:, 4 + j, :], su[:, j, :], ACT.Copy).then_inc(*sc_t.tick(("s5 out high", j)))
            with loop(book, "sc", "g", sc, "i", 4) as i:
                high(Unit(U_G + 1, i=i))
                high(Unit(U_G + 2, i=i))
            sc.wait_ge(gate_in, 64)
            sc.activation(bah[:, :, :], baw[:, :, :], ACT.Copy).then_inc(*sc_t.tick("gate high"))
            for n in range(12):
                sc.wait_ge(*ve_t(("conv", n)))
                sc.activation(zg[:, n, 3:T + 3], tmp[2 + n % 2][:, 0:T], ACT.Silu).then_inc(*sc_t.tick(("conv silu", n)))
            for h in range(GH):
                sc.wait_ge(*ve_t(("zg", h), i=3))
                sc.activation(zg[:, 12 + h, 3:T + 3], zg[:, 12 + h, 3:T + 3], ACT.Silu)\
                  .then_inc(*sc_t.tick(("z silu", h)))
            for n in range(8):
                if n >= 2:
                    sc.wait_ge(*pe_t(("qk mean", n - 2)))
                sc.wait_ge(*sc_t(("conv silu", n)))
                sc.activation(tmp[4 + n % 2][:, 0:T], zg[:, n, 3:T + 3], ACT.Square)\
                  .then_inc(*sc_t.tick(("qk square", n)))
                sc.wait_ge(*ve_t(("qk mean", n)))
                sc.activation(tmp[n % 2][:, 0:T], tmp[n % 2][:, 0:T], ACT.Sqrt).then_inc(*sc_t.tick(("qk sqrt", n)))
            sc.wait_ge(*ve_t(("ba", NT - 1)))
            sc.activation(gates[:, 0:16].rearrange("p (t h) -> p t h", h=4),
                          small[:, 0:32].rearrange("p (t c) -> p t c", c=8)[:, :, 0:4], ACT.Sigmoid)\
              .then_inc(*sc_t.tick("beta"))
            sc.wait_ge(*ve_t("gate size"))
            sc.activation(small[:, 48:64], small[:, 48:64], ACT.Exp, scale=-1.0).then_inc(*sc_t.tick("gate exp"))
            sc.activation(gates[:, 48:52], gates[:, 48:52], ACT.Exp).then_inc(*sc_t.tick("a exp"))
            sc.wait_ge(*sc_t("gate exp"))
            sc.activation(small[:, 48:64], small[:, 48:64], ACT.Ln, bias=1.0).then_inc(*sc_t.tick("gate ln"))
            with loop(book, "sc", "blk", sc, "b", NT) as b:
                def blk_of(c0):
                    return zg[:, c0:c0 + 4, ds(b * P + 3, P)]

                def heads(x):
                    return x[:, 0:T].rearrange("p (h t) -> p h t", h=GH)

                sc.wait_ge(*ve_t("columns", b=b))
                for c0, dst in ((4, gb[0]), (0, gb[1])):
                    sc.activation(heads(dst), blk_of(c0), ACT.Copy).then_inc(*sc_t.tick(("block", c0)))
                sc.activation(heads(gb[10]), blk_of(8), ACT.Copy).then_inc(*sc_t.tick("blocks"))
                sc.activation(small[:, 68:72], small[:, 64:68], ACT.Exp).then_inc(*sc_t.tick("exp columns"))
                sc.wait_ge(*ve_t("row forms", b=b))
                sc.activation(tmp[0][:, 0:T], gb[2][:, :], ACT.Exp).then_inc(*sc_t.tick("exp rows"))
                sc.wait_ge(*ve_t("decay", b=b))
                sc.activation(gb[4][:, :], gb[4][:, :], ACT.Exp).then_inc(*sc_t.tick("decay"))
                sc.activation(small[:, 76:80], small[:, 76:80], ACT.Exp).then_inc(*sc_t.tick("to last"))
                sc.wait_ge(*pe_t("turned", b=b))
                sc.activation(gb[11][:, :], bank(4), ACT.Copy).then_inc(*sc_t.tick("kTok"))
                for s in range(7):
                    sc.wait_ge(*pe_t(("X", s), b=b))
                    sc.activation(gb[10][:, :], bank(6), ACT.Copy).then_inc(*sc_t.tick(("X", s)))
                sc.wait_ge(*pe_t("w", b=b))
                sc.activation(gb[15][:, :], bank(2), ACT.Copy, scale=-1.0).then_inc(*sc_t.tick("w"))
            for h in range(GH):
                if h >= 2:
                    sc.wait_ge(*pe_t(("delta mean", h - 2)))
                else:
                    sc.wait_ge(*ve_t("state", b=NT - 1))
                sc.activation(tmp[h % 2][:, 0:T], zg[:, h, 3:T + 3], ACT.Square).then_inc(*sc_t.tick(("delta square", h)))
                sc.wait_ge(*ve_t(("delta mean", h)))
                sc.activation(tmp[2 + h % 2][:, 0:T], tmp[2 + h % 2][:, 0:T], ACT.Sqrt)\
                  .then_inc(*sc_t.tick(("delta sqrt", h)))
                sc.wait_ge(*ve_t(("delta normed", h)))
                sc.activation(mohi[:, h, :], zg[:, h, 3:T + 3], ACT.Copy).then_inc(*sc_t.tick(("delta high", h)))
            for u in range(U_WO + 1, U_WO + 6):
                high(Unit(u))
            high(Unit(U_UP))
            norm("ffn", lambda j: pcol("ffn", j))
            ffn(U_UP, "f0", True)
            norm("fin1", None)

            with loop(book, "sc", "layer", sc, "layer", LAYERS) as l:
                def v(label):
                    return ve_t(label, layer=l)

                def p_(label):
                    return pe_t(label, layer=l)

                high(Unit(V_UP1, l))
                norm("n1", lambda j: lv[:, j:j + 1], layer=l)
                ffn(V_UP1, "f1", False, l)
                high(Unit(V_WIN, l))
                norm("nm", lambda j: lv[:, 8 + j:9 + j], layer=l)
                for u in range(V_WIN + 1, V_WIN + 7):
                    high(Unit(u, l))
                u = Unit(V_WIN + 7, l)
                sc.wait_ge(landed[u.slot], u.landed)
                sc.wait_ge(consumed, u.before - 8)
                sc.activation(whi[u.slot][:, :].rearrange("p (k c) -> p k c", k=DC)[:, :, 0:VF - COLS],
                              raw[u.slot][:, :].rearrange("p (k c) -> p k c", k=DC)[:, :, 0:VF - COLS],
                              ACT.Copy).then_inc(high_ready, 1)
                high(Unit(V_WO, l))
                for n in range(3):
                    sc.wait_ge(*v(("z", n)))
                    sc.activation(tmp[n][:, 0:T], z2[:, n, :], ACT.Square).then_inc(*sc_t.tick(("mla square", n)))
                sc.wait_ge(*v("mla means"))
                for n in range(2):
                    sc.activation(tmp[3 + n][:, 0:T], tmp[3 + n][:, 0:T], ACT.Sqrt).then_inc(*sc_t.tick(("mla sqrt", n)))
                for h in range(HEADS):
                    sc.wait_ge(*p_(("mla q", h)))
                    sc.activation(qf[0:QD, h, :], ps[0:QD, 4, :], ACT.Copy, scale=QD ** -0.5)\
                      .then_inc(*sc_t.tick(("mla q", h)))
                    sc.wait_ge(*p_(("mla k", h)))
                    sc.activation(kf[0:HD, h, :], ps[0:HD, 6, :], ACT.Copy).then_inc(*sc_t.tick(("mla k", h)))
                sc.wait_ge(*v("f size"))
                sc.activation(small[:, 24:48], small[:, 24:48], ACT.Exp, scale=-1.0).then_inc(*sc_t.tick("f exp"))
                sc.wait_ge(*sc_t("f exp", layer=l))
                sc.activation(small[:, 24:48], small[:, 24:48], ACT.Ln, bias=1.0).then_inc(*sc_t.tick("f ln"))
                for k in range(2):
                    sc.wait_ge(*v(("pool out", k)))
                    sc.activation(xhi[:, 3 + k, :], z2[:, 4 + k, :], ACT.Copy).then_inc(*sc_t.tick(("pool high", k)))

                for slot_n in range(AN + 3):
                    n = slot_n
                    if n < AN:
                        if n >= AN // 2 and n % NT == 0:
                            h = n // NT - HEADS
                            sc.wait_ge(*p_(("fox row", h)))
                            if h >= 2:
                                sc.wait_ge(*v(("scores", n - NT - 1)))
                            sc.activation(arow(h)[:, 0:T], bank(7), ACT.Copy).then_inc(*sc_t.tick(("fox row", h)))
                        s = asc(n)[:, 0:P * (n % NT + 1)]
                        sc.wait_ge(*v(("max", n)))
                        sc.activation(s, s, ACT.Exp, bias=small[:, 70 + n % 2:71 + n % 2],
                                      accum_out=small[:, 72 + n % 2:73 + n % 2]).then_inc(*sc_t.tick(("exp", n)))
                    n = slot_n - 2
                    if 0 <= n < AN:
                        w = P * (n % NT + 1)
                        sc.wait_ge(*p_(("turned", n)))
                        if n >= 2:
                            sc.wait_ge(*p_(("out", n - 2)))
                        sc.activation(aturn(n)[:, 0:w], ps[:, TB_[n % 2], 0:w], ACT.Copy).then_inc(*sc_t.tick(("turned", n)))
                    n = slot_n - 3
                    if n >= 0 and n % 8 == 7:
                        sc.wait_ge(*v(("out", n)))
                        sc.activation(xhi[:, CHUNKS[n // 8], :], tmp[3][:, 0:T], ACT.Copy)\
                          .then_inc(*sc_t.tick(("high", n // 8)))
                for u in range(V_WO + 1, V_WO + 4):
                    high(Unit(u, l))
                high(Unit(V_UP2, l))
                norm("n2", lambda j: lv[:, 16 + j:17 + j], reads=Unit(V_WO + 3, l), layer=l)
                ffn(V_UP2, "f2", False, l)
            norm("fin2", None, lambda j: ve_t(("x", "end", j), layer=LAYERS - 1))

        @blk.vector
        def _(ve):
            def own(**at):
                ve.wait_ge(*ve_t.last(**at))

            def mean(tag, n, dst, src, eps, sqrt_label, **at):
                ve.tensor_scalar(dst, src, 1.0 / n, eps, ALU.mult, ALU.add).then_inc(*ve_t.tick(tag))
                ve.wait_ge(*sc_t(sqrt_label, **at))
                ve.reciprocal(dst, dst).then_inc(*ve_t.tick(("root of", tag)))
                own(**at)

            def residual(tag, unit, scale, weight, x_tag=None, **at):
                for j in range(DC + 2):
                    if j < DC:
                        ve.wait_ge(consumed, unit.began + j + 1)
                        ve.scalar_tensor_tensor(out=xT[:, j, :], in0=bank((j + 4) % 8), scalar=scale, in1=xT[:, j, :],
                                                op0=ALU.mult, op1=ALU.add).then_inc(*ve_t.tick(("x", x_tag or tag, j)))
                    if j >= 2 and weight is not None:
                        low(tag, weight, j - 2, **at)

            def low(tag, weight, j, **at):
                ve.wait_ge(*sc_t(("xw high", tag, j), **at))
                ve.wait_ge(*ve_t(("x", tag, j), **at))
                ve.scalar_tensor_tensor(out=xlo[:, j, :], in0=xT[:, j, :], scalar=weight(j),
                                        in1=xhi[:, j, :].bitcast(F32), op0=ALU.mult, op1=ALU.subtract)\
                  .then_inc(*ve_t.tick(("xw low", tag, j)))

            def root(tag, column=False, wait=True, **at):
                ve.wait_ge(*pe_t(("total", tag), **at))
                ve.tensor_scalar(rb[:, :], bank(7), 1.0 / D, EPS, ALU.mult, ALU.add).then_inc(*ve_t.tick(("mean", tag)))
                ve.wait_ge(*sc_t(("sqrt", tag), **at))
                ve.reciprocal(rb[:, :], rb[:, :]).then_inc(*ve_t.tick(("root", tag)))
                if wait:
                    own(**at)
                if column:
                    ve.wait_ge(*pe_t(("root column", tag), **at))
                    ve.tensor_copy(rcol[:, :], ps[:, 6, 0:NT]).then_inc(*ve_t.tick(("rcol", tag)))
                    own(**at)

            def mul(dst, a, b, label, op=ALU.mult):
                ve.tensor_tensor(dst, a, b, op).then_inc(*ve_t.tick(label))

            def gated(up, name, tag, layer=None):
                at = {} if layer is None else {"layer": layer}
                with loop(book, "ve", name, ve, "i", 11) as i:
                    ve.wait_ge(*ve_t(("hidden", name, 1), i=i - 1, **at))
                    ve.wait_ge(*ve_t(("root", tag), **at))
                    for c in range(2):
                        ve.wait_ge(consumed, Unit(up, layer, i).began + 4 * c + 4)
                        mul(tmp[c][:, 0:T], bank(c), rb[:, :], ("gate", name, c))
                    for c in range(2):
                        ve.wait_ge(consumed, Unit(up + 1, layer, i).began + 4 * c + 4)
                        mul(tmp[2 + c][:, 0:T], bank(2 + c), rb[:, :], ("up", name, c))
                        own(i=i, **at)
                        ve.wait_ge(*sc_t(("silu", name, c), i=i, **at))
                        ve.wait_ge(*po_t(("hidden low", name, c), i=i - 1, **at))
                        mul(tmp[4 + c][:, 0:T], tmp[2 + c][:, 0:T], tmp[c][:, 0:T], ("hidden", name, c))

            def conv_gated(up, name):
                Z = (tmp[2], tmp[3])
                for z in Z:
                    ve.memset(z[:, 0:2], 0.0).then_inc(*ve_t.tick(("pad", z is Z[0])))
                wt = pv[:, PV["fconv"]:PV["fconv"] + 4 * 44].rearrange("p (k g f) -> p k g f", k=4, g=2)
                with loop(book, "ve", name, ve, "i", 11) as i:
                    ve.wait_ge(*ve_t(("hidden", name, 1), i=i - 1))
                    for g in range(2):
                        ve.tensor_copy(small[:, 0:16].rearrange("p (k g c) -> p k g c", k=4, g=2)[:, :, g, :],
                                       wt[:, :, g, ds(i * 2, 2)]).then_inc(*ve_t.tick(("taps", g)))
                    own(i=i)
                    for g in range(2):
                        for c in range(2):
                            n = 2 * g + c
                            ve.wait_ge(consumed, Unit(up + g, None, i).began + 4 * c + 4)
                            z = Z[c]
                            mul(z[:, 2:T + 2], bank(n), rb[:, :], (("gate", "up")[g], name, c))
                            own(i=i)
                            dst = tmp[4 * g + c][:, 0:T]
                            if g:
                                ve.wait_ge(*po_t(("hidden low", name, c), i=i - 1))
                            ve.tensor_scalar(dst, z[:, 0:T], small[:, n:n + 1], None, ALU.mult)\
                              .then_inc(*ve_t.tick(("tap", name, n, 0)))
                            for k in (1, 2):
                                own(i=i)
                                ve.scalar_tensor_tensor(out=dst, in0=z[:, k:T + k], scalar=small[:, 4 * k + n:4 * k + n + 1],
                                                        in1=dst, op0=ALU.mult, op1=ALU.add)\
                                  .then_inc(*ve_t.tick(("gate in", name, c) if k == 2 and g == 0 else ("tap", name, n, k)))
                            if g:
                                own(i=i)
                                ve.wait_ge(*sc_t(("silu", name, c), i=i))
                                ve.scalar_tensor_tensor(out=dst, in0=dst, scalar=small[:, 14 + c:15 + c],
                                                        in1=tmp[c][:, 0:T], op0=ALU.add, op1=ALU.mult)\
                                  .then_inc(*ve_t.tick(("hidden", name, c)))

            ve.wait_ge(*pe_t("parameters"))
            ve.tensor_copy(pv[:, 0:NPV], ps[:, 7, 0:NPV]).then_inc(*ve_t.tick("parameters"))
            for j in range(DC):
                ve.wait_ge(*pe_t(("x", j)))
                ve.tensor_copy(xT[:, j, :], bank(j)).then_inc(*ve_t.tick(("x", "attn", j)))
                if j >= 1:
                    low("attn", lambda j: pcol("attn", j), j - 1)
            low("attn", lambda j: pcol("attn", j), DC - 1)
            root("attn", column=True)
            for n in range(8):
                ve.wait_ge(consumed, Unit(U_DQK + n // 2).began + 4 * (n % 2) + 4)
                ve.scalar_tensor_tensor(out=dqk[:, n, :], in0=bank(n % 4), scalar=0.125 if n < 4 else 1.0, in1=rb[:, :],
                                        op0=ALU.mult, op1=ALU.mult).then_inc(*ve_t.tick(("dqk", n)))
            ve.wait_ge(lambda_in, 64)
            for k in range(2):
                mul(lamb[:, P * k:P * k + 64], lamb[:, P * k:P * k + 64], lamb[:, P * k + 64:P * k + P], ("lambda", k))
            own()
            ve.tensor_reduce(small[:, 20:22], lamb[:, :].rearrange("p (k d) -> p k d", k=2)[:, :, 0:64], AX, ALU.add)\
              .then_inc(*ve_t.tick("lambda sums"))
            for u in range(2):
                for t in range(NT):
                    ve.wait_ge(consumed, Unit(U_DV + u).began + 2 * t + 2)
                    ve.tensor_scalar(dv[:, t, COLS * u:COLS * u + COLS], ps[:, t, COLS * u:COLS * u + COLS],
                                     rcol[:, t:t + 1], None, ALU.mult).then_inc(*ve_t.tick(("dv", u, t)))
            ve.wait_ge(*sc_t("lambda"))
            mul(small[:, 24:25], small[:, 23:24], small[:, 22:23], "minus lambda", ALU.subtract)
            own()
            ve.tensor_scalar(small[:, 25:26], small[:, 24:25], -LAM_INIT, None, ALU.add).then_inc(*ve_t.tick("- lambda"))
            own()

            def scores(dst, src, t, label):
                n, o = P * (t + 1), P * t
                if t:
                    ve.tensor_copy(dst[:, 0:o], src[:, 0:o]).then_inc(*ve_t.tick((label, "copy")))
                mul(dst[:, o:n], src[:, o:n], causal, label, ALU.add)

            for slot_n in range(DN + 3):
                n = slot_n
                if n < DN:
                    t, s0 = n // 4, 26 + 8 * (n % 2)
                    if n >= 3:
                        ve.wait_ge(*pe_t(("diff turned", n - 3)))
                    for c in range(2):
                        ve.wait_ge(*pe_t(("diff scores", n, c)))
                        scores(dmap(n, c), bank(2 * (n % 2) + c), t, ("diff scores", n, c))
                    for c in range(2):
                        ve.wait_ge(*ve_t(("diff scores", n, c)))
                        ve.tensor_reduce(small[:, s0 + c:s0 + c + 1], dmap(n, c)[:, 0:P * (t + 1)], AX, ALU.max,
                                         negate=True).then_inc(*ve_t.tick(("diff max", n, c)))
                n = slot_n - 1
                if 0 <= n < DN:
                    w, s0 = P * (n // 4 + 1), 26 + 8 * (n % 2)
                    ve.wait_ge(*sc_t(("diff exp", n, 1)))
                    ve.reciprocal(small[:, s0 + 4:s0 + 6], small[:, s0 + 2:s0 + 4]).then_inc(*ve_t.tick(("diff inverse", n)))
                    own()
                    mul(small[:, s0 + 6:s0 + 7], small[:, s0 + 5:s0 + 6], small[:, 25:26], ("diff share", n))
                    x = dmap(n, 0)[:, 0:w]
                    ve.tensor_scalar(x, x, small[:, s0 + 4:s0 + 5], None, ALU.mult).then_inc(*ve_t.tick(("diff first", n)))
                    own()
                    ve.scalar_tensor_tensor(out=x, in0=dmap(n, 1)[:, 0:w], scalar=small[:, s0 + 6:s0 + 7], in1=x,
                                            op0=ALU.mult, op1=ALU.add).then_inc(*ve_t.tick(("diff weights", n)))
                    own()
                n = slot_n - 3
                if 0 <= n < DN:
                    t, h = divmod(n, 4)
                    ve.wait_ge(*pe_t(("diff out", n)))
                    ve.tensor_copy(osum[:, h, P * t:P * t + P], ps[:, 6 + n % 2, 0:P]).then_inc(*ve_t.tick(("diff out", n)))
            dr = [tmp[2][:, 0:T], tmp[3][:, 0:T], tmp[4][:, 0:T], dx[0][:, :]]
            for h in range(4):
                ve.wait_ge(*pe_t(("diff mean", h)))
                ve.tensor_scalar(dr[h], bank(4 + h % 2), 1.0 / P, EPS, ALU.mult, ALU.add).then_inc(*ve_t.tick(("diff mean", h)))
            for h in range(4):
                ve.wait_ge(*sc_t(("diff sqrt", h)))
                ve.reciprocal(dr[h], dr[h]).then_inc(*ve_t.tick(("diff root", h)))
                own()
                ve.scalar_tensor_tensor(out=osum[:, h, :], in0=osum[:, h, :], scalar=pcol("diffn", 0),
                                        in1=dr[h], op0=ALU.mult, op1=ALU.mult).then_inc(*ve_t.tick(("diff normed", h)))
            for h in range(4):
                ve.wait_ge(*sc_t(("diff high", h)))
                ve.wait_ge(*ve_t(("diff normed", h)))
                ve.scalar_tensor_tensor(out=molo[:, 8 + h, :], in0=osum[:, h, :], scalar=1.0 - LAM_INIT,
                                        in1=mohi[:, 8 + h, :].bitcast(F32), op0=ALU.mult, op1=ALU.subtract)\
                  .then_inc(*ve_t.tick(("diff low", h)))
            own()
            for c in range(2):
                for e in range(2):
                    ve.memset(bbd[c][64 * e:64 * e + 64, :, 16 * (1 - e):16 * (1 - e) + 16], 0.0)\
                      .then_inc(*ve_t.tick(("zero b", c, e)))
            for n in range(4):
                ve.wait_ge(consumed, Unit(U_SU + n // 2).began + 4 * (n % 2) + 4)
                mul(su[:, n, :], bank(n), rb[:, :], ("su", n))
            ve.wait_ge(*pe_t("s5 params"))
            ve.tensor_scalar(slot(0), ps[:, 4, 0:16], -1e-4, None, ALU.min).then_inc(*ve_t.tick("s5 lr"))
            ve.tensor_copy(slots(1, 3), ps[:, 4, 16:48]).then_inc(*ve_t.tick("s5 li dt"))
            own()
            mul(slot(3), slot(0), slot(2), "s5 zr")
            mul(slot(4), slot(1), slot(2), "s5 zi")
            own()
            ve.tensor_scalar(slot(9), slot(4), 1.0 / (2 * np.pi), ROUND, ALU.mult, ALU.add).then_inc(*ve_t.tick("turns"))
            own()
            ve.tensor_scalar(slot(9), slot(9), -ROUND, None, ALU.add).then_inc(*ve_t.tick("whole turns"))
            own()
            for n, part in enumerate(TWO_PI):
                ve.scalar_tensor_tensor(out=slot(4), in0=slot(9), scalar=-part, in1=slot(4), op0=ALU.mult, op1=ALU.add)\
                  .then_inc(*ve_t.tick(("phase", n)))
                own()
            ve.tensor_scalar(slot(6), slot(4), 3.1415925, -3.1415925, ALU.min, ALU.max).then_inc(*ve_t.tick("s5 phase"))
            for c in range(2):
                ve.wait_ge(*po_t(("zero c", c)))
                for e in range(2):
                    r = slice(64 * e, 64 * e + 64)
                    ve.tensor_scalar(cbd[c][r, :, 16 * e:16 * e + 16],
                                     ps[r, 5, 256 * c:256 * c + 256].rearrange("p (b h) -> p b h", h=16),
                                     -1.0 if c else 1.0, None, ALU.mult).then_inc(*ve_t.tick(("s5 c", c, e)))
            ve.wait_ge(*sc_t("s5 half sin"))
            mul(slot(8), slot(8), slot(8), "s5 sin2")
            own()
            ve.tensor_scalar(slot(8), slot(8), -2.0, 1.0, ALU.mult, ALU.add).then_inc(*ve_t.tick("s5 cos"))
            ve.memset(pw[0][:, 0, :], 1.0).then_inc(*ve_t.tick("s5 one"))
            ve.memset(pw[1][:, 0, :], 0.0).then_inc(*ve_t.tick("s5 zero"))
            own()
            mul(pw[0][:, 1, :], slot(5), slot(8), "s5 p1r")
            mul(pw[1][:, 1, :], slot(5), slot(7), "s5 p1i")
            own()

            def cmul(dst, a, b, label, s=(40, 41), n=1, dims=None):
                t0, t1 = (slots(x, x + n) if dims is None else slots(x, x + n).rearrange(dims[0], **dims[1])
                          for x in (s[0], s[0] + n))
                mul(t0, a[0], b[0], (label, 0))
                mul(t1, a[1], b[1], (label, 1))
                own()
                mul(t0, t0, t1, (label, 2), ALU.subtract)
                own()
                mul(t1, a[0], b[1], (label, 3))
                t2 = slots(s[0] + 2 * n, s[0] + 3 * n)
                t2 = t2 if dims is None else t2.rearrange(dims[0], **dims[1])
                mul(t2, a[1], b[0], (label, 4))
                own()
                mul(dst[1], t1, t2, (label, 5), ALU.add)
                ve.tensor_copy(dst[0], t0).then_inc(*ve_t.tick((label, 6)))
                own()

            def powers(a, b):
                return [pw[c][:, a:b, :] for c in range(2)]

            for m in (1, 2, 4):
                cmul(powers(m + 1, 2 * m + 1), powers(1, m + 1),
                     [pw[c][:, m:m + 1, :].to_broadcast([P, m, PAIRS]) for c in range(2)], ("s5 power", m), n=m,
                     dims=("p (m b) -> p m b", {"m": m}))
            for k in range(6):
                if k == 0:
                    for c in range(2):
                        ve.tensor_copy(lvp[c][:, 0, :], pw[c][:, STEP, :]).then_inc(*ve_t.tick(("s5 level", 0, c)))
                    own()
                else:
                    cmul([lvp[c][:, k, :] for c in range(2)], [lvp[c][:, k - 1, :] for c in range(2)],
                         [lvp[c][:, k - 1, :] for c in range(2)], ("s5 level", k))
            ve.tensor_scalar(slot(10), pw[0][:, 1, :], -1.0, None, ALU.add).then_inc(*ve_t.tick("s5 nr"))
            mul(slot(14), slot(0), slot(0), "s5 lr2")
            mul(slot(15), slot(1), slot(1), "s5 li2")
            own()
            mul(slot(14), slot(14), slot(15), "s5 l2", ALU.add)
            own()
            ve.reciprocal(slot(14), slot(14)).then_inc(*ve_t.tick("s5 1/l2"))
            mul(slot(12), slot(10), slot(0), "s5 w0")
            mul(slot(13), pw[1][:, 1, :], slot(1), "s5 w1")
            mul(slot(15), pw[1][:, 1, :], slot(0), "s5 w2")
            mul(slot(16), slot(10), slot(1), "s5 w3")
            own()
            mul(slot(12), slot(12), slot(13), "s5 w4", ALU.add)
            mul(slot(15), slot(15), slot(16), "s5 w5", ALU.subtract)
            own()
            mul(slot(12), slot(12), slot(14), "s5 w6")
            mul(slot(13), slot(15), slot(14), "s5 w7")
            own()

            def wide(x):
                return x.unsqueeze(2).to_broadcast([P, PAIRS, 32])

            def flat(x):
                return x[:, 0:T].rearrange("p (b h) -> p b h", h=32)

            t4, t5 = flat(tmp[4]), flat(tmp[5])
            B, w_ = [bbd[c][:, :, :] for c in range(2)], [slot(12), slot(13)]
            mul(t4, B[0], wide(w_[0]), "bb0")
            mul(t5, B[1], wide(w_[1]), "bb1")
            own()
            mul(t4, t4, t5, "bb2", ALU.subtract)
            own()
            mul(t5, B[0], wide(w_[1]), "bb3")
            mul(B[1], B[1], wide(w_[0]), "bb4")
            own()
            mul(B[1], B[1], t5, "bb5", ALU.add)
            ve.tensor_copy(B[0], t4).then_inc(*ve_t.tick("s5 bbar"))
            own()
            for j in range(STEP):
                m = STEP - 1 - j
                if j:
                    ve.wait_ge(*pe_t(("s5 wbt", j - 1, 3)))
                Pr, Pi = (wide(pw[c][:, m, :]) for c in range(2))
                t0, t1 = flat(tmp[0]), flat(tmp[1])
                mul(t0, B[0], Pr, ("wb", j, 0))
                mul(t1, B[1], Pi, ("wb", j, 1))
                own()
                mul(flat(tmp[2]), t0, t1, ("wb", j, 2), ALU.subtract)
                own()
                mul(t0, B[0], Pi, ("wb", j, 3))
                mul(t1, B[1], Pr, ("wb", j, 4))
                own()
                mul(flat(tmp[3]), t0, t1, ("s5 wb", j), ALU.add)
            ve.wait_ge(*pe_t(("s5 add", STEP - 1, 3)))
            for c in range(2):
                for b in range(4):
                    ve.tensor_copy(st[c][:, b:PAIRS:4, :],
                                   ps[:, 4 + b, 256 * c:256 * c + 256].rearrange("p (q n) -> p q n", q=4))\
                      .then_inc(*ve_t.tick(("s5 moved", c, b)))
            own()
            for k in range(6):
                d = 1 << k
                for half in range(2):
                    hp = slice(8 * half, 8 * half + 8)
                    w = NSTEP - d
                    tt = [tmp[x][:, 0:8 * w].rearrange("p (b n) -> p b n", b=8) for x in range(4)]
                    ar, ai = (lvp[c][:, k, hp].unsqueeze(2).to_broadcast([P, 8, w]) for c in range(2))
                    Sr, Si = (st[c][:, hp, 0:w] for c in range(2))
                    mul(tt[0], Sr, ar, ("scan", k, half, 0))
                    mul(tt[1], Si, ai, ("scan", k, half, 1))
                    mul(tt[2], Si, ar, ("scan", k, half, 2))
                    mul(tt[3], Sr, ai, ("scan", k, half, 3))
                    own()
                    mul(tt[0], tt[0], tt[1], ("scan", k, half, 4), ALU.subtract)
                    mul(tt[2], tt[2], tt[3], ("scan", k, half, 5), ALU.add)
                    own()
                    for c in range(2):
                        mul(st[c][:, hp, d:NSTEP], st[c][:, hp, d:NSTEP], tt[2 * c], ("scan", k, half, 6 + c), ALU.add)
                    own()
            ve.memset(small[:, 89:90], 0.0).then_inc(*ve_t.tick("s5 scanned"))
            for q in range(4):
                if q:
                    ve.wait_ge(*pe_t(("s5 y", q - 1)))
                    ve.scalar_tensor_tensor(out=su[:, q - 1, :], in0=su[:, q - 1, :], scalar=pcol("s5d", q - 1),
                                            in1=bank((q - 1) % 2), op0=ALU.mult, op1=ALU.add)\
                      .then_inc(*ve_t.tick(("s5 y", q - 1)))
                for b in range(4):
                    pair = 4 * q + b
                    Cr, Ci = (cbd[c][:, pair:pair + 1, :].to_broadcast([P, STEP + 1, 32]) for c in range(2))
                    Pr, Pi = (pw[c][:, :, pair:pair + 1].to_broadcast([P, STEP + 1, 32]) for c in range(2))
                    t4, t5, t3, t2 = (tmp[x][:, 0:288].rearrange("p (t h) -> p t h", h=32) for x in (4, 5, 3, 2))
                    mul(t4, Cr, Pr, ("cp", q, b, 0))
                    mul(t5, Ci, Pi, ("cp", q, b, 1))
                    mul(t3, Ci, Pr, ("cp", q, b, 2))
                    mul(t2, Cr, Pi, ("cp", q, b, 3))
                    own()
                    mul(cp[0][:, b, :, :], t4, t5, ("cp", q, b, 4), ALU.add)
                    mul(cp[1][:, b, :, :], t3, t2, ("s5 cp", q) if b == 3 else ("cp", q, b, 5), ALU.subtract)
                    own()
            ve.wait_ge(*pe_t(("s5 y", 3)))
            ve.scalar_tensor_tensor(out=su[:, 3, :], in0=su[:, 3, :], scalar=pcol("s5d", 3), in1=bank(1),
                                    op0=ALU.mult, op1=ALU.add).then_inc(*ve_t.tick(("s5 y", 3)))
            for q in range(4):
                ve.wait_ge(*sc_t(("s5 high", q)))
                mul(molo[:, 4 + q, :], su[:, q, :], mohi[:, 4 + q, :].bitcast(F32), ("s5 gelu low", q), ALU.subtract)
            for j in range(4):
                ve.wait_ge(*sc_t(("s5 sigmoid", j)))
                mul(su[:, j, :], su[:, j, :], tmp[j][:, 0:T], ("s5 gated", j))
                own()
                mul(tmp[5 if j else 4][:, 0:T], su[:, j, :], su[:, j, :], ("s5 sq", j))
                if j:
                    own()
                    mul(tmp[4][:, 0:T], tmp[4][:, 0:T], tmp[5][:, 0:T], "s5 squares" if j == 3 else ("s5 sum", j), ALU.add)
                    own()
            ve.wait_ge(*pe_t("s5 mean"))
            mean("s5 mean", 512, tmp[5][:, 0:T], bank(7), EPS, "s5 sqrt")
            for j in range(4):
                ve.scalar_tensor_tensor(out=su[:, j, :], in0=su[:, j, :], scalar=pcol("s5n", j), in1=tmp[5][:, 0:T],
                                        op0=ALU.mult, op1=ALU.mult).then_inc(*ve_t.tick(("s5 out", j)))
            for j in range(4):
                ve.wait_ge(*sc_t(("s5 out high", j)))
                mul(molo[:, 4 + j, :], su[:, j, :], mohi[:, 4 + j, :].bitcast(F32), ("s5 out low", j), ALU.subtract)
            own()
            ve.memset(zg[:, 0:12, 0:3], 0.0).then_inc(*ve_t.tick("zg pad"))
            with loop(book, "ve", "g", ve, "i", 4) as i:
                for n in range(4):
                    ve.wait_ge(consumed, Unit(U_G + n // 2, i=i).began + 4 * (n % 2) + 4)
                    mul(zg[:, ds(i * 4 + n, 1), 3:T + 3].rearrange("p a t -> p (a t)"), bank(n), rb[:, :], ("zg", n))
            ve.wait_ge(*sc_t("gate high"))
            mul(bal[:, :, :], baw[:, :, :], bah[:, :, :].bitcast(F32), "gate weights", ALU.subtract)
            own()
            for n in range(12):
                dst = tmp[2 + n % 2][:, 0:T]
                if n >= 2:
                    ve.wait_ge(*sc_t(("conv silu", n - 2)))
                for k in range(4):
                    w = pcol("gconv", 12 * k + n)
                    if k == 0:
                        ve.tensor_scalar(dst, zg[:, n, 0:T], w, None, ALU.mult).then_inc(*ve_t.tick(("gtap", n, 0)))
                    else:
                        own()
                        ve.scalar_tensor_tensor(out=dst, in0=zg[:, n, k:T + k], scalar=w, in1=dst, op0=ALU.mult,
                                                op1=ALU.add).then_inc(*ve_t.tick(("conv", n) if k == 3 else ("gtap", n, k)))
            ve.wait_ge(*pe_t("gates"))
            for t in range(NT):
                ve.tensor_scalar(small[:, 8 * t:8 * t + 8], ps[:, 4, 8 * t:8 * t + 8], rcol[:, t:t + 1], None, ALU.mult)\
                  .then_inc(*ve_t.tick(("ba", t)))
            own()
            sm = small[:, 0:32].rearrange("p (t c) -> p t c", c=8)
            x16 = small[:, 32:48].rearrange("p (t c) -> p t c", c=4)
            mul(x16, sm[:, :, 4:8], gates[:, 52:56].unsqueeze(1).to_broadcast([P, 4, 4]), "gate x", ALU.add)
            own()
            ve.scalar_tensor_tensor(out=small[:, 48:64], in0=small[:, 32:48], scalar=-1.0, in1=small[:, 32:48],
                                    op0=ALU.mult, op1=ALU.max).then_inc(*ve_t.tick("gate size"))
            for n in range(8):
                ve.wait_ge(*pe_t(("qk mean", n)))
                if n < 2:
                    ve.wait_ge(*sc_t(("s5 sigmoid", 3)))
                mean(("qk mean", n), 1.0, tmp[n % 2][:, 0:T], bank(5 + n % 2), EPS, ("qk sqrt", n))
                ve.scalar_tensor_tensor(out=zg[:, n, 3:T + 3], in0=zg[:, n, 3:T + 3],
                                        scalar=GD ** -0.5 if n < 4 else 1.0, in1=tmp[n % 2][:, 0:T], op0=ALU.mult,
                                        op1=ALU.mult).then_inc(*ve_t.tick(("qk normed", n)))
            ve.wait_ge(*sc_t("gate ln"))
            ve.scalar_tensor_tensor(out=small[:, 32:48], in0=small[:, 32:48], scalar=0.0, in1=small[:, 48:64],
                                    op0=ALU.max, op1=ALU.add).then_inc(*ve_t.tick("softplus"))
            own()
            ve.scalar_tensor_tensor(out=gates[:, 16:32].rearrange("p (t c) -> p t c", c=4), in0=x16, scalar=-1.0,
                                    in1=gates[:, 48:52].unsqueeze(1).to_broadcast([P, 4, 4]), op0=ALU.mult,
                                    op1=ALU.mult).then_inc(*ve_t.tick("log decay"))
            ve.wait_ge(*pe_t("cumulated"))
            ve.tensor_copy(gates[:, 32:48], ps[:, 4, 64:80]).then_inc(*ve_t.tick("cumulated"))
            ve.memset(tmp[5][:, 0:T], 0.0).then_inc(*ve_t.tick("state 0"))
            own()
            kb, qb, gcR, beR, decT, LT, atT, CT, Dm, DT, X, kTok, vbT, kbe, kl, nwT = gb
            vn, qe, S = tmp[3], tmp[4], tmp[5]

            def heads(x):
                return x[:, 0:T].rearrange("p (h t) -> p h t", h=GH)

            def per_head(c):
                return small[:, c:c + 4].unsqueeze(2).to_broadcast([P, GH, P])

            def mask(m):
                return m.unsqueeze(1).to_broadcast([P, GH, P])

            with loop(book, "ve", "blk", ve, "b", NT) as b:
                ve.tensor_copy(gates[:, 56:60], gates[:, ds(b * 4 + 16, 4)]).then_inc(*ve_t.tick("col g"))
                ve.tensor_copy(gates[:, 60:64], gates[:, ds(b * 4, 4)]).then_inc(*ve_t.tick("col beta"))
                ve.tensor_copy(small[:, 64:68], gates[:, ds(b * 4 + 32, 4)]).then_inc(*ve_t.tick("columns"))
                ve.wait_ge(*pe_t("row forms", b=b))
                ve.tensor_copy(beR[:, :], bank(1)).then_inc(*ve_t.tick("beta rows"))
                ve.tensor_copy(gcR[:, :], bank(0)).then_inc(*ve_t.tick("row forms"))
                own(b=b)
                mul(small[:, 76:80], heads(gcR)[:, :, P - 1], small[:, 64:68], "to last", ALU.subtract)
                for h in range(GH):
                    ve.tensor_scalar(decT[:, P * h:P * h + P], gcR[:, P * h:P * h + P], small[:, 64 + h:65 + h], 0.0,
                                     ALU.subtract, ALU.min).then_inc(*ve_t.tick("decay" if h == 3 else ("decay", h)))
                ve.wait_ge(*sc_t("decay", b=b))
                mul(heads(decT), heads(decT), mask(tri), "decay masked")
                ve.wait_ge(*pe_t("kk", b=b))
                own(b=b)
                mul(LT[:, :], bank(2), decT[:, :], "L0")
                own(b=b)
                mul(heads(LT), heads(LT), mask(strict), "L1")
                own(b=b)
                mul(LT[:, :], LT[:, :], beR[:, :], "L2")
                mul(atT[:, :], bank(3), decT[:, :], "kk used")
                for n, x in enumerate((Dm, DT)):
                    ve.tensor_copy(heads(x), mask(ident)).then_inc(*ve_t.tick(("eye", n)))
                own(b=b)
                for s in range(7):
                    mul(heads(CT), heads(LT), mask(lvl[:, s, :]), ("level", s))
                    if s == 0:
                        ve.wait_ge(*pe_t("turned", b=b))
                        ve.wait_ge(*sc_t("kTok", b=b))
                        mul(small[:, 72:76], small[:, 68:72], gates[:, 60:64], "beta exp g")
                        mul(heads(vbT), heads(bank(5)), gates[:, 60:64].unsqueeze(2).to_broadcast([P, GH, P]), "vb")
                        own(b=b)
                        mul(heads(kbe), heads(kTok), per_head(72), "kbe")
                        mul(heads(kl), heads(kTok), per_head(76), "kl0")
                        ve.wait_ge(*sc_t("exp rows", b=b))
                        ve.wait_ge(*sc_t("blocks", b=b))
                        mul(qe[:, 0:T], qb[:, :], tmp[0][:, 0:T], "kl")
                    ve.wait_ge(*pe_t(("DD", s), b=b))
                    if s < 6:
                        mul(Dm[:, :], Dm[:, :], bank(0), ("D", s), ALU.subtract)
                    mul(DT[:, :], DT[:, :], bank(1), ("DT", s), ALU.subtract)
                    own(b=b)
                ve.wait_ge(*pe_t("v new", b=b))
                ve.tensor_copy(vn[:, 0:T], bank(3)).then_inc(*ve_t.tick("v new"))
                ve.wait_ge(*pe_t("delta out", b=b))
                ve.tensor_scalar(zg[:, 0:4, ds(b * P + 3, P)], heads(bank(4)), 1.0, None, ALU.mult)\
                  .then_inc(*ve_t.tick("delta out"))
                for h in range(GH):
                    hs = slice(P * h, P * h + P)
                    ve.scalar_tensor_tensor(out=S[:, hs], in0=S[:, hs], scalar=tmp[0][:, P * h + P - 1:P * h + P],
                                            in1=ps[:, 5, hs], op0=ALU.mult, op1=ALU.add)\
                      .then_inc(*ve_t.tick("state" if h == 3 else ("state", h)))
                own(b=b)
            for h in range(GH):
                ve.wait_ge(*pe_t(("delta mean", h)))
                r = tmp[2 + h % 2][:, 0:T]
                mean(("delta mean", h), GD, r, bank(6 + h % 2), EPS, ("delta sqrt", h))
                o = zg[:, h, 3:T + 3]
                ve.scalar_tensor_tensor(out=o, in0=o, scalar=pcol("gdnn", 0), in1=r, op0=ALU.mult, op1=ALU.mult)\
                  .then_inc(*ve_t.tick(("delta root", h)))
                own()
                mul(o, o, zg[:, 12 + h, 3:T + 3], ("delta normed", h))
                ve.wait_ge(*sc_t(("delta high", h)))
                own()
                mul(molo[:, h, :], o, mohi[:, h, :].bitcast(F32), ("delta low", h), ALU.subtract)
            residual("ffn", Unit(U_WO + 5), 1.0, lambda j: pcol("ffn", j))
            root("ffn")
            conv_gated(U_UP, "f0")
            residual("fin1", Unit(U_DN + 10), 1.0, None)
            root("fin1")
            for j in range(DC):
                ve.scalar_tensor_tensor(out=xT[:, j, :], in0=xT[:, j, :], scalar=pcol("fin1", j), in1=rb[:, :],
                                        op0=ALU.mult, op1=ALU.mult).then_inc(*ve_t.tick(("fin1", j)))
            own()

            with loop(book, "ve", "layer", ve, "layer", LAYERS) as l:
                at = {"layer": l}

                def p_(label):
                    return pe_t(label, layer=l)

                def s_(label):
                    return sc_t(label, layer=l)

                ve.tensor_copy(lv[:, :], pv[:, ds(l * LW + PV["layer"], LW)]).then_inc(*ve_t.tick("layer columns"))
                own(**at)
                for j in range(DC):
                    ve.memset(small[:, 80 + j:81 + j], 0.0).then_inc(*ve_t.tick(("x", "n1", j)))
                for j in range(DC):
                    low("n1", lambda j: lv[:, j:j + 1], j, **at)
                root("n1", wait=False, **at)
                gated(V_UP1, "f1", "n1", l)
                residual("nm", Unit(V_DN1 + 10, l), 0.5, lambda j: lv[:, 8 + j:9 + j], **at)
                root("nm", column=True, **at)
                for n in range(12):
                    ve.wait_ge(consumed, Unit(V_WIN + n // 2, l).began + 4 * (n % 2) + 4)
                    ve.scalar_tensor_tensor(out=z2[:, n, :], in0=bank(n % 4), scalar=0.125 if 6 <= n < 9 else 1.0,
                                            in1=rb[:, :], op0=ALU.mult, op1=ALU.mult).then_inc(*ve_t.tick(("z", n)))
                for u in range(2):
                    for t in range(NT):
                        c = slice(COLS * u, COLS if u == 0 else VF)
                        ve.wait_ge(consumed, Unit(V_WIN + 6 + u, l).began + 2 * t + 2)
                        ve.tensor_scalar(vf[:, t, c], ps[:, t, c], rcol[:, t:t + 1], None, ALU.mult)\
                          .then_inc(*ve_t.tick(("vf", u, t)))
                for g in range(2):
                    ve.memset(poolw[HD * g:HD * g + HD, :, HD - HD * g:P - HD * g], 0.0).then_inc(*ve_t.tick(("pool zero", g)))
                ve.wait_ge(*p_("q_a mean"))
                ve.tensor_scalar(tmp[3][:, 0:T], bank(4), 1.0 / 256, EPS, ALU.mult, ALU.add).then_inc(*ve_t.tick("q_a mean"))
                ve.wait_ge(*p_("kv_a mean"))
                ve.tensor_scalar(tmp[4][:, 0:T], bank(5), 1.0 / 128, EPS, ALU.mult, ALU.add).then_inc(*ve_t.tick("mla means"))
                for n in range(2):
                    ve.wait_ge(*s_(("mla sqrt", n)))
                    ve.reciprocal(tmp[3 + n][:, 0:T], tmp[3 + n][:, 0:T]).then_inc(*ve_t.tick(("mla root", n)))
                own(**at)
                for n in range(3):
                    ve.scalar_tensor_tensor(out=z2[:, n, :], in0=z2[:, n, :], scalar=lv[:, 24 + n:25 + n],
                                            in1=tmp[3 + n // 2][:, 0:T], op0=ALU.mult, op1=ALU.mult)\
                      .then_inc(*ve_t.tick("kv_a" if n == 2 else ("q_a", n)))
                ve.wait_ge(layer_in, l * 128 + 128)
                for h in range(HEADS):
                    ve.wait_ge(*p_(("mla q turned", h)))
                    own(**at)
                    mul(tmp[3][0:QD, 0:T], ps[0:QD, 5, :], ropet[0:QD, 1, :], ("mla sin", h))
                    mul(qf[0:QD, h, :], qf[0:QD, h, :], ropet[0:QD, 0, :], ("mla cos", h))
                    own(**at)
                    mul(qf[0:QD, h, :], qf[0:QD, h, :], tmp[3][0:QD, 0:T], ("mla q", h), ALU.add)
                ve.wait_ge(*p_("k rope"))
                own(**at)
                kr = slice(HD, QD)
                mul(tmp[3][kr, 0:T], ps[kr, 7, :], ropet[kr, 1, :], "k sin")
                mul(z2[kr, 3, :], z2[kr, 3, :], ropet[kr, 0, :], "k cos")
                own(**at)
                mul(z2[kr, 3, :], z2[kr, 3, :], tmp[3][kr, 0:T], "k rope", ALU.add)
                own(**at)
                ve.tensor_copy(kf[kr, :, :], z2[kr, 3:4, :].to_broadcast([ROPE, HEADS, T])).then_inc(*ve_t.tick("kf"))
                for t in range(NT):
                    ve.wait_ge(*p_(("mla v", t)))
                    ve.tensor_copy(mv[:, t, :], ps[:, t, 0:HEADS * HD]).then_inc(*ve_t.tick(("mla v", t)))
                x24 = small[:, 0:24].rearrange("p (t h) -> p t h", h=HEADS)
                mul(x24, vf[:, :, 384:390], small[:, 64:70].unsqueeze(1).to_broadcast([P, NT, HEADS]), "f x", ALU.add)
                own(**at)
                ve.scalar_tensor_tensor(out=small[:, 24:48], in0=small[:, 0:24], scalar=-1.0, in1=small[:, 0:24],
                                        op0=ALU.mult, op1=ALU.max).then_inc(*ve_t.tick("f size"))
                ve.wait_ge(*s_("f ln"))
                ve.scalar_tensor_tensor(out=small[:, 0:24], in0=small[:, 0:24], scalar=0.0, in1=small[:, 24:48],
                                        op0=ALU.min, op1=ALU.subtract).then_inc(*ve_t.tick("log f"))
                ve.wait_ge(*p_("fox sum"))
                ve.tensor_copy(small[:, 24:48], ps[:, 4, 0:24]).then_inc(*ve_t.tick("fox columns"))
                for k in range(2):
                    z, src, d, done = z2[:, 4 + k, :], z2[:, 4 + k, :], 1, []
                    for n in range(2 + 2 * k):
                        dst = tmp[3 + n % 2][:, 0:T]
                        own(**at)
                        ve.tensor_copy(dst[:, 0:d], src[:, 0:d]).then_inc(*ve_t.tick(("pool", k, n, 0)))
                        mul(dst[:, d:T], src[:, d:T], src[:, 0:T - d], ("pool", k, n, 1), ALU.add)
                        src, d = dst, 2 * d
                    own(**at)
                    for g in range(2):
                        r = slice(64 * g, 64 * g + 64)
                        w = tmp[3 + g][r, 0:T]
                        mul(w, w, poolt[r, k, :], ("pool mean", k, g))
                        own(**at)
                        mul(z[r, :], w, z[r, :], "pooled" if k and g else ("pooled", k, g), ALU.subtract)
                ve.wait_ge(*p_("pool out"))
                for k in range(2):
                    ve.tensor_scalar(z2[:, 4 + k, :], bank(4 + k), lv[:, 27 + k:28 + k], None, ALU.mult)\
                      .then_inc(*ve_t.tick(("pool out", k)))
                for k in range(2):
                    ve.wait_ge(*s_(("pool high", k)))
                    own(**at)
                    mul(xlo[:, 3 + k, :], z2[:, 4 + k, :], xhi[:, 3 + k, :].bitcast(F32), ("pool low", k), ALU.subtract)

                for slot_n in range(AN + 4):
                    n = slot_n
                    if n < AN:
                        t, s = n % NT, asc(n)
                        w = P * (t + 1)
                        ve.wait_ge(*p_(("scores", n)))
                        if n >= 4:
                            ve.wait_ge(*p_(("turned", n - 4)))
                        if n >= AN // 2:
                            h = n // NT - HEADS
                            ve.wait_ge(*s_(("fox row", h)))
                            c = 24 + HEADS * t + h
                            ve.scalar_tensor_tensor(out=s[:, 0:w], in0=ps[:, SB[n % 3], 0:w], scalar=small[:, c:c + 1],
                                                    in1=arow(h)[:, 0:w], op0=ALU.add, op1=ALU.subtract)\
                              .then_inc(*ve_t.tick(("shift", n)))
                            own(**at)
                            mul(s[:, P * t:w], s[:, P * t:w], causal, ("scores", n), ALU.add)
                        else:
                            scores(s, ps[:, SB[n % 3], :], t, ("scores", n))
                        own(**at)
                        ve.tensor_reduce(small[:, 70 + n % 2:71 + n % 2], s[:, 0:w], AX, ALU.max, negate=True)\
                          .then_inc(*ve_t.tick(("max", n)))
                    n = slot_n - 1
                    if 0 <= n < AN:
                        s, c = asc(n)[:, 0:P * (n % NT + 1)], 74 + n % 2
                        ve.wait_ge(*s_(("exp", n)))
                        ve.reciprocal(small[:, c:c + 1], small[:, c - 2:c - 1]).then_inc(*ve_t.tick(("inverse", n)))
                        own(**at)
                        ve.tensor_scalar(s, s, small[:, c:c + 1], None, ALU.mult).then_inc(*ve_t.tick(("weights", n)))
                    n = slot_n - 4
                    if n >= 0 and n % 8 == 7:
                        ve.wait_ge(*s_(("high", n // 8)))
                        ch = CHUNKS[n // 8]
                        mul(xlo[:, ch, :], tmp[3][:, 0:T], xhi[:, ch, :].bitcast(F32), ("low", n // 8), ALU.subtract)
                        own(**at)
                    n = slot_n - 3
                    if 0 <= n < AN:
                        o = slice(64 * (n // NT % 2), 64 * (n // NT % 2) + 64)
                        ve.wait_ge(*p_(("out", n)))
                        ve.tensor_copy(tmp[3][o, P * (n % NT):P * (n % NT) + P], ps[o, OB[n % 2], 0:P])\
                          .then_inc(*ve_t.tick(("out", n)))
                residual("n2", Unit(V_WO + 3, l), 1.0, lambda j: lv[:, 16 + j:17 + j], **at)
                root("n2", wait=False, **at)
                gated(V_UP2, "f2", "n2", l)
                residual("end", Unit(V_DN2 + 10, l), 0.5, None)
                own(**at)
            root("fin2")
            for j in range(DC):
                ve.scalar_tensor_tensor(out=xT[:, j, :], in0=xT[:, j, :], scalar=pcol("fin2", j), in1=rb[:, :],
                                        op0=ALU.mult, op1=ALU.mult).then_inc(*ve_t.tick(("y", j)))
            for t in range(NT):
                for k in range(2):
                    ve.wait_ge(*pe_t(("out half", t, k)))
                    ve.tensor_copy(raw_out(t)[:, T * k:T * k + T], bank(k)).then_inc(*ve_t.tick(("out half", t, k)))


def constants():
    i, j = np.arange(P)[:, None], np.arange(P)[None, :]
    cst = np.stack([i == j, i <= j, i < j, np.where(j > i, NEG, 0.0), np.ones((P, P))], 1).astype(np.float32)
    lev = np.stack([(i // (2 * s) == j // (2 * s)) & (j // s % 2 == 1) & (i // s % 2 == 0)
                    for s in (1, 2, 4, 8, 16, 32, 64)], 1).astype(np.float32)
    half = ROPE // 2
    inv = np.float32(10000.0) ** (-np.arange(0, ROPE, 2, dtype=np.float32) / np.float32(ROPE))
    ang = np.arange(T, dtype=np.float32)[None, :] * inv[:, None].astype(np.float32)
    rope = np.zeros((QD, 2, T), np.float32)
    rope[0:HD, 0] = 1.0
    rope[HD:QD, 0] = np.tile(np.cos(ang.astype(np.float64)), (2, 1))
    rope[HD:QD, 1] = np.tile(np.sin(ang.astype(np.float64)), (2, 1))
    turn = np.zeros((QD, QD), np.float32)
    for k in range(half):
        turn[HD + half + k, HD + k] = -1.0
        turn[HD + k, HD + half + k] = 1.0
    counts = np.zeros((P, 2, T), np.float32)
    for g, w in enumerate((2, 4, 8, 16)):
        counts[64 * (g % 2):64 * (g % 2) + 64, g // 2] = 1.0 / np.minimum(np.arange(1, T + 1), w)
    return {"constants": cst, "levels": lev, "rope": rope, "turn": turn, "counts": counts}


def kernel(**inputs):
    import concourse.bacc as bacc
    from concourse.bass_utils import run_bass_kernel_spmd

    def program(known):
        nc = bacc.Bacc("TRN2", target_bir_lowering=False, num_devices=1)
        dram = {n: nc.dram_tensor(f"in_{n}", a.shape, F32, kind="ExternalInput").ap() for n, a in arrays.items()}
        out = nc.dram_tensor("out", (1, T, D), F32, kind="ExternalOutput").ap()
        book = Book(known)
        build(nc, dram, out, book)
        return nc, book

    arrays = {n: np.ascontiguousarray(a) for n, a in inputs.items()} | constants()
    _, counts = program(None)
    nc, _ = program(counts)
    r = run_bass_kernel_spmd(nc, [{f"in_{n}": a for n, a in arrays.items()}], core_ids=[0])
    return r.results[0]["out"]
```

```python
from contextlib import ExitStack, contextmanager

import numpy as np
import concourse.bass as bass
from concourse import mybir

F32 = mybir.dt.float32
F32R = mybir.dt.float32r
I32 = mybir.dt.int32
ALU = mybir.AluOpType
ACT = mybir.ActivationFunctionType
AX = mybir.AxisListType.X
ds = bass.ds

P = 128
T = 512
NT = T // P
D = 1024
DC = D // P
FF = 2816
FC = FF // P
EPS = 1e-6
LAYERS = 2
COLS = 256
NEG = -1.0e30

GH, GD = 4, 128
G_Q, G_Z, G_BA, S_U, D_Q, D_V = 0, 1536, 2048, 2056, 2568, 3592
QA, KVA, POOL, FOX_Q, FOX_V = 0, 256, 416, 672, 1440
IN2 = 1830
HEADS, HD, ROPE, QD = 6, 64, 32, 96
VF = IN2 - FOX_V
S5G, S5H, S5P = 32, 16, 64
PAIRS = S5G // 2
STEP = 8
NSTEP = T // STEP

U_DQK, U_DV, U_SU, U_GLU, U_G, U_WO, U_UP, U_DN, U_FIRST = 0, 4, 6, 8, 9, 17, 23, 45, 56
V_UP1, V_DN1, V_WIN, V_WO, V_UP2, V_DN2, U_LAYER = 0, 22, 33, 41, 45, 67, 78

PV = {}
_at = 0
for _n, _k in (("attn", 8), ("ffn", 8), ("fin1", 8), ("s5d", 4), ("bglu", 4), ("s5n", 4), ("gdnn", 1), ("diffn", 1),
               ("gconv", 48), ("fconv", 132), ("fbias", 44), ("fin2", 8), ("layer", 58)):
    PV[_n] = _at
    _at += _k
NPV = _at
LW = 29
PVT = -(-NPV // P)


LAM_INIT = 0.8 - 0.6 * float(np.exp(0.0))
ROUND = 1.5 * 2.0 ** 23
TWO_PI = (6.28125, 0.0019350051879882812, 2 * np.pi - 6.28125 - 0.0019350051879882812)


class Book:

    def __init__(self, known=None):
        self.known, self.places, self.pers, self.frames = known, {}, {}, {}


class Tally:

    def __init__(self, book, sem, name, engine):
        self.book, self.sem, self.name, self.cursor = book, sem, name, 0
        self.frames = book.frames.setdefault(engine, [])

    def tick(self, label, n=1):
        for f in self.frames:
            f["starts"].setdefault(self, self.cursor)
        self.cursor += n
        key = (self.name, label)
        assert key not in self.book.places, key
        self.book.places[key] = (self.cursor, [f["key"] for f in self.frames])
        self.newest = label
        return self.sem, n

    def __call__(self, label, **at):
        known = self.book.known
        if known is None:
            return self.sem, 1
        count, loops = known.places[(self.name, label)]
        for key in loops:
            count = count + at[key[0]] * known.pers[(self.name, key)]
        if isinstance(count, int):
            assert count >= 0
        return self.sem, count

    def last(self, **at):
        return self(self.newest, **at)


@contextmanager
def loop(book, engine, name, eng, key, n):
    frame = {"key": (key, name), "starts": {}}
    book.frames.setdefault(engine, []).append(frame)
    with eng.Fori(0, n) as i:
        yield i
    book.frames[engine].pop()
    for tally, start in frame["starts"].items():
        per = tally.cursor - start
        book.pers[(tally.name, frame["key"])] = per
        tally.cursor = start + per * n


class Unit:

    def __init__(self, const, layer=None, i=None):
        self.slot, self.first = const % 2, const == 0
        n, half = const, const // 2
        if layer is not None:
            n, half = n + U_FIRST + layer * U_LAYER, half + U_FIRST // 2 + layer * (U_LAYER // 2)
        if i is not None:
            n, half = n + i * 2, half + i
        self.n, self.half = n, half
        self.early = layer is None and i is None and const < 2
        self.landed = (half + 1) * 32
        self.split = n + 1
        self.done = (n + 1) * 8
        self.before = n * 8
        self.began = n * 8


def build(nc, A, out, book):
    with ExitStack() as ctx:
        def sb(name, shape, dt=F32):
            return ctx.enter_context(nc.sbuf_tensor(name, shape, dt))

        def sem(name):
            return ctx.enter_context(nc.semaphore(name))

        xT = sb("xT", [P, DC, T])
        raw = [sb(f"raw{s}", [P, 2048]) for s in range(2)]
        whi = [sb(f"weight_high{s}", [P, 2048], F32R) for s in range(2)]
        wlo = [sb(f"weight_low{s}", [P, 2048], F32R) for s in range(2)]
        cst = sb("constants", [P, 5, P])
        ident, tri, strict, causal, ones = (cst[:, i, :] for i in range(5))
        pv = sb("parameters", [P, PVT * P])
        lv = sb("layer_parameters", [P, LW])
        rb = sb("root", [P, T])
        rcol = sb("root_column", [P, NT])
        tmp = [sb(f"tmp{i}", [P, T + 2]) for i in range(6)]
        small = sb("small", [P, 96])
        xa = ExitStack()
        gb = [xa.enter_context(nc.sbuf_tensor(f"delta{i}", [P, T], F32)) for i in range(16)]
        xa.close()
        xhi = sb("xw_high", [P, DC, T], F32R)
        xlo = sb("xw_low", [P, DC, T], F32R)
        region = ExitStack()

        def tb(name, shape, dt=F32):
            return region.enter_context(nc.sbuf_tensor(name, shape, dt))

        xc = ExitStack()
        cpe = [xc.enter_context(nc.sbuf_tensor(f"s5_cp_even{c}", [P, 4, STEP + 1, 32], F32)) for c in "ri"]
        xc.close()
        mohi = tb("mixed_high", [P, 12, T], F32R)
        molo = tb("mixed_low", [P, 12, T], F32R)
        sub = ExitStack()

        def ub(name, shape, dt=F32):
            return sub.enter_context(nc.sbuf_tensor(name, shape, dt))

        xin = ub("x_in", [P, NT, D])
        rows = ub("parameter_rows", [P, PVT, P])
        sub.close()
        sub = ExitStack()
        dqk = ub("diff_qk", [P, 8, T])
        dv = ub("diff_v", [P, NT, T])
        osum = ub("diff_out", [P, 4, T])
        lamb = ub("lambda_rows", [P, 4 * 64])
        dx = [ub(f"diff_turn{i}", [P, T]) for i in range(3)]
        sub.close()
        sub = ExitStack()
        su = ub("s5_u", [P, 4, T])
        bbd = [ub(f"s5_b{c}", [P, PAIRS, 32]) for c in "ri"]
        cbd = [ub(f"s5_c{c}", [P, PAIRS, 32]) for c in "ri"]
        lvp = [ub(f"s5_level{c}", [P, 6, PAIRS]) for c in "ri"]
        pw = [ub(f"s5_power{c}", [P, STEP + 1, PAIRS]) for c in "ri"]
        st = [ub(f"s5_state{c}", [P, PAIRS, NSTEP]) for c in "ri"]
        cp = [ub(f"s5_cp{c}", [P, 4, STEP + 1, 32]) for c in "ri"]
        kbd = ub("s5_kernel", [P, STEP, P])
        sub.close()
        sub = ExitStack()
        zg = ub("delta_z", [P, 16, T + 3])
        lvl = ub("level_masks", [P, 7, P])
        baw = ub("gate_weights", [P, DC, 8])
        bah = ub("gate_weights_high", [P, DC, 8], F32R)
        bal = ub("gate_weights_low", [P, DC, 8], F32R)
        gates = ub("gates", [P, 64])
        sub.close()
        region.close()
        region = ExitStack()
        z2 = tb("z", [P, 12, T])
        vf = tb("fox_v_gates", [P, NT, VF + 2])
        qf = tb("mla_q", [P, HEADS, T])
        kf = tb("mla_k", [P, HEADS, T])
        mv = tb("mla_v", [P, NT, HEADS * HD])
        wqb = tb("w_q_b", [P, 2, HEADS * QD])
        wkvb = tb("w_kv_b", [P, HEADS, 2 * HD])
        ropet = tb("rope_tables", [P, 2, T])
        poolt = tb("pool_counts", [P, 2, T])
        poolw = tb("pool_w", [P, 2, P])
        turn = tb("rope_turn", [P, QD])
        ax = [tb(f"attention_turn{i}", [P, T]) for i in range(3)]
        region.close()
        hhi = sb("hidden_high", [P, FC, T], F32R)
        hlo = sb("hidden_low", [P, FC, T], F32R)

        ps = ctx.enter_context(nc.psum_tensor("psum", [P, 8, T], F32))

        landed = [sem(f"unit_landed{s}") for s in range(2)]
        high_ready, low_ready, consumed = sem("high_ready"), sem("low_ready"), sem("units_consumed")
        params_in, x_in, mixer_in, lambda_in, gate_in = (sem(n) for n in
                                                          ("params_in", "x_in_landed", "mixer_in", "lambda_in", "gate_in"))
        s5_in, layer_in, stored = sem("s5_in"), sem("layer_in"), sem("output_stored")
        pe_t = Tally(book, sem("products_ready"), "pe", "pe")
        ve_t = Tally(book, sem("vector_ready"), "ve", "ve")
        sc_t = Tally(book, sem("scalar_ready"), "sc", "sc")
        po_t = Tally(book, sem("pool_ready"), "po", "po")
        dm_t = Tally(book, mixer_in, "dm", "sp")
        blk = ctx.enter_context(nc.Block())

        def prow(name, k):
            r = PV[name] + k
            return r % P, r // P

        def pcol(name, k):
            return pv[:, PV[name] + k:PV[name] + k + 1]

        def bank(i):
            return ps[:, i, :]

        dmap = lambda n, c: (tmp[0], tmp[1], dx[0])[n % 3] if c == 0 else tmp[2 + n % 2]
        dturn = lambda n: (tmp[4], dx[1])[n % 2]
        asc = lambda n: (tmp[0], tmp[1], ax[0], ax[1])[n % 4]
        aturn = lambda n: (tmp[2], ax[2])[n % 2]
        arow = lambda h: tmp[4 + h % 2]
        CHUNKS = (0, 1, 2, 5, 6, 7)
        WO_ORDER = (2, 3, 4, 5, 0, 1)
        DN = NT * 4
        AN = 2 * HEADS * NT
        SB, TB_, OB = (0, 1, 4), (2, 5), (3, 6)

        def slots(a, b):
            return st[0][:, :, :].rearrange("p b n -> p (b n)")[:, 16 * a:16 * b]

        def slot(a):
            return slots(a, a + 1)

        def raw_out(t):
            return raw[t // 2][:, D * (t % 2):D * (t % 2) + D]

        def wbj(c, j):
            return tmp[2 + c][:, 0:T] if j % 2 == 0 else cp[c][:, :, :, :].rearrange("p b t h -> p (b t h)")[:, 0:T]

        def s5_cp(q):
            return [(cp if q % 2 else cpe)[c][:, :, :, :] for c in range(2)]

        def cp_factors(q, b):
            pair = 4 * q + b
            return [cbd[c][:, pair:pair + 1, :].to_broadcast([P, STEP + 1, 32]) for c in range(2)] + \
                   [pw[c][:, :, pair:pair + 1].to_broadcast([P, STEP + 1, 32]) for c in range(2)]

        @blk.sync
        def _(sp):
            nparam = 0

            def rows_in(name, src, k):
                nonlocal nparam
                at = PV[name]
                done = 0
                while done < k:
                    m = min(k - done, P - (at + done) % P)
                    sp.dma_start(rows[(at + done) % P:(at + done) % P + m, (at + done) // P, :],
                                 src[done:done + m, :]).then_inc(params_in, 16)
                    done += m
                    nparam += 1

            def of128(ap):
                return ap.rearrange("a (k p) -> (a k) p", p=P)

            sp.dma_start(xin[:, :, :], A["x"][0].rearrange("(t p) d -> p t d", p=P)).then_inc(x_in, 16)
            sp.dma_start(cst[:, :, :], A["constants"]).then_inc(x_in, 16)
            for name, src, k in (("attn", "attn_norm_w", 8), ("ffn", "ffn_norm_w", 8), ("s5d", "s5_d", 4),
                                 ("bglu", "s5_b_glu", 4), ("s5n", "s5_norm_w", 4), ("gdnn", "gdn_norm_w", 1),
                                 ("diffn", "diff_norm_w", 1), ("fbias", "ffn_conv_b", 44)):
                rows_in(name, of128(A[src]), k)
            for name, src in (("fin1", "final_norm_w"), ("fin2", "final_norm_2")):
                rows_in(name, A[src].rearrange("(k p) -> k p", p=P), 8)
            rows_in("gconv", of128(A["gdn_conv_w"][0]), 48)
            rows_in("fconv", of128(A["ffn_conv_w"][0]), 132)
            for l in range(LAYERS):
                at = 29 * l
                for src, k in (("ffn1_norm_2", 8), ("mix_norm_2", 8), ("ffn2_norm_2", 8), ("q_a_norm_2", 2),
                               ("kv_a_norm_2", 1), ("pool_scale_2", 2)):
                    PV["_"] = PV["layer"] + at
                    rows_in("_", A[src][l:l + 1, :].rearrange("a (k p) -> (a k) p", p=P), k)
                    at += k
            book.nparam = nparam

            def free(u):
                if not u.early:
                    sp.wait_ge(high_ready, u.split - 2)
                    sp.wait_ge(low_ready, u.split - 2)

            def load_cols(u, w, c0, c1=None):
                free(u)
                dst = raw[u.slot][:, :].rearrange("p (k c) -> p k c", k=DC)
                src = w.rearrange("(k p) c -> p k c", p=P)
                if c1 is None:
                    for h in range(2):
                        sp.dma_start(dst[:, 4 * h:4 * h + 4, :], src[:, 4 * h:4 * h + 4, ds(c0, COLS)])\
                          .then_inc(landed[u.slot], 16)
                else:
                    for h, c in enumerate((c0, c1)):
                        sp.dma_start(dst[:, :, P * h:P * h + P], src[:, :, ds(c, P)]).then_inc(landed[u.slot], 16)

            def load_rows(u, w, r0):
                free(u)
                for h in range(2):
                    sp.dma_start(raw[u.slot][:, 1024 * h:1024 * h + 1024], w[ds(r0 + P * h, P), :])\
                      .then_inc(landed[u.slot], 16)

            w_in = A["w_in"][0]
            for i in range(4):
                load_cols(Unit(U_DQK + i), w_in, D_Q + COLS * i)
                if i == 1:
                    for n, v in enumerate(("q1", "k1", "q2", "k2")):
                        sp.dma_start(lamb[:, 64 * n:64 * n + 64],
                                     A["diff_lambda_" + v][0:1, :].to_broadcast([P, 64])).then_inc(lambda_in, 16)
            for i in range(2):
                load_cols(Unit(U_DV + i), w_in, D_V + COLS * i)
            for i in range(2):
                load_cols(Unit(U_SU + i), w_in, S_U + COLS * i)
            sp.wait_ge(*ve_t(("diff low", 3)))
            sp.wait_ge(*sc_t(("diff high", 3)))
            for c, n in enumerate(("re", "im")):
                sp.dma_start(tmp[0][0:16, P * c:P * c + P],
                             A[f"s5_lambda_{n}"][0].rearrange("(b e) p -> b (e p)", e=2)).then_inc(s5_in, 16)
                for e in range(2):
                    sp.dma_start(bbd[c][64 * e:64 * e + 64, :, 16 * e:16 * e + 16],
                                 A[f"s5_b_{n}"][0].rearrange("(b e) p h -> e p b h", e=2)[e]).then_inc(s5_in, 16)
                for q in range(2):
                    for b in range(8):
                        sp.dma_start(tmp[2 + c][16 * b:16 * b + 16, P * q:P * q + P].rearrange("h (e p) -> h e p", e=2),
                                     A[f"s5_c_{n}"][0].rearrange("(b e) h p -> b h e p", e=2)[8 * q + b])\
                          .then_inc(s5_in, 16)
            sp.dma_start(tmp[1][0:16, 0:2], A["s5_log_dt"][0].rearrange("(b e) -> b e", e=2)).then_inc(s5_in, 16)
            free(Unit(U_GLU))
            for h in range(2):
                sp.dma_start(raw[Unit(U_GLU).slot][:, 1024 * h:1024 * h + 1024].rearrange("p (k c) -> p k c", k=2),
                             A["s5_w_glu"][0][256 * h:256 * h + 256, :].rearrange("(k p) c -> p k c", p=P))\
                  .then_inc(landed[Unit(U_GLU).slot], 16)
            for i in range(2):
                load_cols(Unit(U_G + i), w_in, COLS * i)
            sp.wait_ge(*ve_t(("s5 out low", 3)))
            sp.wait_ge(*po_t("s5 free"))
            sp.dma_start(lvl[:, :, :], A["levels"]).then_inc(gate_in, 16)
            with nc.allow_non_contiguous_dma(reason="eight columns"):
                sp.dma_start(baw[:, :, :], w_in[:, G_BA:G_BA + 8].rearrange("(k p) c -> p k c", p=P))\
                  .then_inc(gate_in, 16)
            sp.dma_start(gates[:, 48:52], A["gdn_a_log"][0:1, :].to_broadcast([P, 4])).then_inc(gate_in, 16)
            sp.dma_start(gates[:, 52:56], A["gdn_dt_bias"][0:1, :].to_broadcast([P, 4])).then_inc(gate_in, 16)
            for i in range(2, 8):
                load_cols(Unit(U_G + i), w_in, COLS * i)
            for i in range(6):
                load_rows(Unit(U_WO + i), A["w_out"][0], 2 * P * WO_ORDER[i])

            def load_ffn(up, down, w_up, w_down, name, layer=None):
                with loop(book, "sp", name, sp, "i", 11) as i:
                    load_cols(Unit(up, layer, i), w_up, i * COLS)
                    load_cols(Unit(up + 1, layer, i), w_up, i * COLS + FF)
                load_rows(Unit(down, layer), w_down, 0)
                with loop(book, "sp", name + "d", sp, "i", 4) as i:
                    load_rows(Unit(down + 1, layer, i), w_down, i * (4 * P) + 2 * P)
                    load_rows(Unit(down + 2, layer, i), w_down, i * (4 * P) + 4 * P)
                for k in range(2):
                    load_rows(Unit(down + 9 + k, layer), w_down, (9 + k) * 2 * P)

            load_ffn(U_UP, U_DN, A["ffn_w_up"][0], A["ffn_w_down"][0], "f0")
            with loop(book, "sp", "layer", sp, "layer", LAYERS) as l:
                def of(name):
                    a = A[name]
                    return a[ds(l, 1)].rearrange("a r c -> (a r) c")

                load_ffn(V_UP1, V_DN1, of("ffn1_w_gu_2"), of("ffn1_w_down_2"), "f1", l)
                win2 = of("w_in_2")
                load_cols(Unit(V_WIN, l), win2, QA)
                load_cols(Unit(V_WIN + 1, l), win2, KVA, KVA + 64)
                sp.wait_ge(consumed, Unit(V_WIN, l).before)
                sp.dma_start(wqb[:, :, :], of("w_q_b_2").rearrange("(k p) c -> p k c", p=P)).then_inc(layer_in, 16)
                sp.dma_start(wkvb[:, :, :].rearrange("p h c -> p (h c)"), of("w_kv_b_2")).then_inc(layer_in, 16)
                sp.dma_start(ropet[0:QD, :, :], A["rope"]).then_inc(layer_in, 16)
                sp.dma_start(poolt[:, :, :], A["counts"]).then_inc(layer_in, 16)
                sp.dma_start(turn[0:QD, :], A["turn"]).then_inc(layer_in, 16)
                pwl = A["pool_w_2"][ds(l, 1)].rearrange("a (k g) c d -> g (a c) k d", g=2)
                for g in range(2):
                    r = slice(HD * g, HD * g + HD)
                    sp.dma_start(poolw[r, :, r], pwl[g]).then_inc(layer_in, 16)
                sp.dma_start(small[:, 64:70], A["fox_b_f_2"][ds(l, 1), :].to_broadcast([P, HEADS]))\
                  .then_inc(layer_in, 16)
                for k in range(4):
                    load_cols(Unit(V_WIN + 2 + k, l), win2, POOL + COLS * k)
                load_cols(Unit(V_WIN + 6, l), win2, FOX_V)
                u = Unit(V_WIN + 7, l)
                free(u)
                dst = raw[u.slot][:, :].rearrange("p (k c) -> p k c", k=DC)
                src = win2.rearrange("(k p) c -> p k c", p=P)
                for h in range(2):
                    sp.dma_start(dst[:, 4 * h:4 * h + 4, 0:VF - COLS], src[:, 4 * h:4 * h + 4, FOX_V + COLS:IN2])\
                      .then_inc(landed[u.slot], 16)
                for k in range(4):
                    load_rows(Unit(V_WO + k, l), of("w_out_2"), 2 * P * k)
                load_ffn(V_UP2, V_DN2, of("ffn2_w_gu_2"), of("ffn2_w_down_2"), "f2", l)
            for t in range(NT):
                sp.wait_ge(*ve_t(("out half", t, 1)))
                sp.dma_start(out[0, P * t:P * t + P, :], raw_out(t)).then_inc(stored, 16)
            sp.wait_ge(stored, 16 * NT)

        @blk.gpsimd
        def _(po):
            def low(u, n=2048):
                po.wait_ge(high_ready, u.split)
                po.tensor_tensor(wlo[u.slot][:, 0:n], raw[u.slot][:, 0:n], whi[u.slot][:, 0:n].bitcast(F32),
                                 ALU.subtract).then_inc(low_ready, 1)

            def sum_squares(tag, **at):
                for j in range(1, DC):
                    po.wait_ge(*sc_t(("square", tag, j), **at))
                    if j > 1:
                        po.wait_ge(*po_t.last(**at))
                    po.tensor_tensor(tmp[2][:, 0:T], tmp[2 if j > 1 else 0][:, 0:T], tmp[j % 2][:, 0:T], ALU.add)\
                      .then_inc(*po_t.tick(("sum", tag, j)))

            def ffn(up, name, layer=None):
                at = {} if layer is None else {"layer": layer}
                with loop(book, "po", name, po, "i", 11) as i:
                    for h in range(2):
                        low(Unit(up + 1 + h, layer, i))
                    for c in range(2):
                        po.wait_ge(*sc_t(("hidden high", name, c), i=i, **at))
                        po.tensor_tensor(hlo[:, ds(i * 2 + c, 1), :].rearrange("p a t -> p (a t)"), tmp[4 + c][:, 0:T],
                                         hhi[:, ds(i * 2 + c, 1), :].rearrange("p a t -> p (a t)").bitcast(F32),
                                         ALU.subtract).then_inc(*po_t.tick(("hidden low", name, c)))
                dn = up + 22
                low(Unit(dn + 1, layer))
                with loop(book, "po", name + "d", po, "i", 4) as i:
                    low(Unit(dn + 2, layer, i))
                    low(Unit(dn + 3, layer, i))
                low(Unit(dn + 10, layer))

            po.memset(small[:, 95:96], 0.0).then_inc(*po_t.tick("start"))
            low(Unit(0))
            sum_squares("attn")
            for u in range(1, U_SU + 2):
                low(Unit(u))
            po.wait_ge(*ve_t(("diff low", 3)))
            po.wait_ge(*sc_t(("diff high", 3)))
            for c in range(2):
                po.memset(cbd[c][:, :, :], 0.0).then_inc(*po_t.tick(("zero c", c)))
            po.memset(kbd[:, :, :], 0.0).then_inc(*po_t.tick("zero k"))
            po.wait_ge(*pe_t(("s5 add", 4 * STEP - 1)))
            po.wait_ge(*ve_t(("s5 wb", STEP - 1)))
            for q in range(2):
                for b in range(4):
                    Cr, Ci, Pr, Pi = cp_factors(q, b)
                    t4, t5 = (tmp[x][:, 0:288].rearrange("p (t h) -> p t h", h=32) for x in (4, 5))
                    for c in range(2):
                        if q or b or c:
                            po.wait_ge(*po_t.last())
                        po.tensor_tensor(t4, Ci if c else Cr, Pr, ALU.mult).then_inc(*po_t.tick(("cp", q, b, 3 * c)))
                        po.tensor_tensor(t5, Cr if c else Ci, Pi, ALU.mult).then_inc(*po_t.tick(("cp", q, b, 3 * c + 1)))
                        po.wait_ge(*po_t.last())
                        po.tensor_tensor(s5_cp(q)[c][:, b, :, :], t4, t5, ALU.subtract if c else ALU.add)\
                          .then_inc(*po_t.tick(("s5 cp", q) if b == 3 and c else ("cp", q, b, 3 * c + 2)))
            low(Unit(U_GLU))
            low(Unit(U_G))
            po.memset(small[:, 94:95], 0.0).then_inc(*po_t.tick("s5 free"))
            for i in range(8):
                low(Unit(U_G + 1 + i))
            for u in range(U_WO + 1, U_WO + 6):
                low(Unit(u))
            low(Unit(U_UP))
            sum_squares("ffn")
            ffn(U_UP, "f0")
            sum_squares("fin1")
            with loop(book, "po", "layer", po, "layer", LAYERS) as l:
                low(Unit(V_UP1, l))
                sum_squares("n1", layer=l)
                ffn(V_UP1, "f1", l)
                low(Unit(V_WIN, l))
                sum_squares("nm", layer=l)
                for u in range(V_WIN + 1, V_WIN + 7):
                    low(Unit(u, l))
                u = Unit(V_WIN + 7, l)
                po.wait_ge(high_ready, u.split)
                lo_part = wlo[u.slot][:, :].rearrange("p (k c) -> p k c", k=DC)[:, :, 0:VF - COLS]
                po.tensor_tensor(lo_part, raw[u.slot][:, :].rearrange("p (k c) -> p k c", k=DC)[:, :, 0:VF - COLS],
                                 whi[u.slot][:, :].rearrange("p (k c) -> p k c", k=DC)[:, :, 0:VF - COLS].bitcast(F32),
                                 ALU.subtract).then_inc(low_ready, 1)
                for u in range(V_WO, V_WO + 4):
                    low(Unit(u, l))
                low(Unit(V_UP2, l))
                sum_squares("n2", layer=l)
                ffn(V_UP2, "f2", l)
            sum_squares("fin2")

        @blk.tensor
        def _(pe):
            def three(dst, lh, ll, rh, rl, start, stop):
                pe.matmul(dst, lh, rh, start=start, stop=False, skip_group_check=True)
                pe.matmul(dst, ll, rh, start=False, stop=False, skip_group_check=True)
                return pe.matmul(dst, lh, rl, start=False, stop=stop, skip_group_check=True)

            def cols_unit(u, banks, waits=()):
                pe.wait_ge(low_ready, u.split)
                for c in range(2):
                    if waits:
                        pe.wait_ge(*waits[c])
                    for k in range(DC):
                        w = slice(COLS * k + P * c, COLS * k + P * c + P)
                        m = three(bank(banks[c]), whi[u.slot][:, w], wlo[u.slot][:, w], xhi[:, k, :], xlo[:, k, :],
                                  k == 0, k == DC - 1)
                    m.then_inc(consumed, 4)

            def tokens_unit(u, n, c0, waits=None, after=None):
                pe.wait_ge(low_ready, u.split)
                for t in range(NT):
                    if waits:
                        pe.wait_ge(*waits[t])
                    for k in range(DC):
                        w = slice(COLS * k, COLS * k + n)
                        x = slice(P * t, P * t + P)
                        m = three(ps[:, t, c0:c0 + n], xhi[:, k, x], xlo[:, k, x], whi[u.slot][:, w],
                                  wlo[u.slot][:, w], k == 0, k == DC - 1)
                    m.then_inc(consumed, 2)
                    if after:
                        after(t)

            def rows_unit(u, rh, rl, start, stop, first_wait=None):
                pe.wait_ge(low_ready, u.split)
                for j in range(DC):
                    if first_wait and j in first_wait:
                        pe.wait_ge(*first_wait[j])
                    for k in range(2):
                        w = slice(1024 * k + P * j, 1024 * k + P * j + P)
                        m = three(bank((j + 4) % 8), whi[u.slot][:, w], wlo[u.slot][:, w], rh(k), rl(k),
                                  start and k == 0, stop and k == 1)
                    if stop:
                        m.then_inc(consumed, 1)
                if not stop:
                    m.then_inc(consumed, 8)

            def total(tag, **at):
                pe.wait_ge(*po_t(("sum", tag, DC - 1), **at))
                pe.matmul(bank(7), ones, tmp[2][:, 0:T], start=True, stop=True).then_inc(*pe_t.tick(("total", tag)))

            def root_column(tag, **at):
                pe.wait_ge(*ve_t(("root", tag), **at))
                for t in range(NT):
                    m = pe.matmul(ps[:, 6, t:t + 1], rb[:, P * t:P * t + P], ident[:, 0:1], start=True, stop=True)
                m.then_inc(*pe_t.tick(("root column", tag)))

            def first_unit(u, tag, column=False, then=None, **at):
                pe.wait_ge(low_ready, u.split)
                pe.wait_ge(*ve_t(("x", tag, 5), **at))
                for k in range(DC):
                    pe.wait_ge(*ve_t(("xw low", tag, k), **at))
                    for c in range(2):
                        w = slice(COLS * k + P * c, COLS * k + P * c + P)
                        m = three(bank(c), whi[u.slot][:, w], wlo[u.slot][:, w], xhi[:, k, :], xlo[:, k, :],
                                  k == 0, k == DC - 1)
                        if k == DC - 1:
                            m.then_inc(consumed, 4)
                total(tag, **at)
                cols_unit(then, (2, 3))
                if column:
                    root_column(tag, **at)

            def ffn(up, name, tag, layer=None):
                at = {} if layer is None else {"layer": layer}
                first_unit(Unit(up, layer), tag, then=Unit(up + 1, layer), **at)
                with loop(book, "pe", name, pe, "i", 10) as i:
                    cols_unit(Unit(up + 2, layer, i), (0, 1), [ve_t(("gate", name, c), i=i, **at) for c in range(2)])
                    cols_unit(Unit(up + 3, layer, i), (2, 3), [ve_t(("up", name, c), i=i, **at) for c in range(2)])
                dn = up + 22

                def hid(hc):
                    return (lambda k: hhi[:, ds(hc + k, 1), :].rearrange("p a t -> p (a t)"),
                            lambda k: hlo[:, ds(hc + k, 1), :].rearrange("p a t -> p (a t)"))

                def ready(i):
                    return po_t(("hidden low", name, 1), i=i, **at)

                last = {4 + c: ve_t(("gate", name, c), i=10, **at) for c in range(2)}
                last |= {6 + c: ve_t(("up", name, c), i=10, **at) for c in range(2)}
                pe.wait_ge(*ready(0))
                rows_unit(Unit(dn, layer), *hid(0), True, False, last)
                with loop(book, "pe", name + "d", pe, "i", 4) as i:
                    pe.wait_ge(*ready(i * 2 + 1))
                    rows_unit(Unit(dn + 1, layer, i), *hid(i * 4 + 2), False, False)
                    pe.wait_ge(*ready(i * 2 + 2))
                    rows_unit(Unit(dn + 2, layer, i), *hid(i * 4 + 4), False, False)
                pe.wait_ge(*ready(9))
                rows_unit(Unit(dn + 9, layer), *hid(18), False, False)
                pe.wait_ge(*ready(10))
                rows_unit(Unit(dn + 10, layer), *hid(20), False, True)

            pe.wait_ge(params_in, 16 * book.nparam)
            pe.wait_ge(x_in, 32)
            for t in range(PVT):
                n = min(P, NPV - P * t)
                m = pe.transpose(ps[:, 7, P * t:P * t + n], rows[0:n, t, :], ident[0:n, 0:n])
            m.then_inc(*pe_t.tick("parameters"))
            for j in range(DC):
                if j == 7:
                    pe.wait_ge(*ve_t("parameters"))
                for t in range(NT):
                    m = pe.transpose(ps[:, j, P * t:P * t + P], xin[:, t, P * j:P * j + P], ident)
                m.then_inc(*pe_t.tick(("x", j)))

            first_unit(Unit(U_DQK), "attn", column=True, then=Unit(U_DQK + 1))
            for i in range(2, 4):
                w = [ve_t(("dqk", 2 * i + c - 4)) for c in range(2)]
                cols_unit(Unit(U_DQK + i), (2 * i % 4, 2 * i % 4 + 1), w)
            tokens_unit(Unit(U_DV), COLS, 0, [ve_t(("dqk", 4 + t)) for t in range(NT)])
            tokens_unit(Unit(U_DV + 1), COLS, COLS, [ve_t(("dv", 0, t)) for t in range(NT)])

            def transposes(dst, src, n, label):
                for k in range(n):
                    m = pe.transpose(bank(dst)[:, P * k:P * k + P], src[:, P * k:P * k + P], ident)
                m.then_inc(*pe_t.tick(label))

            for slot_n in range(DN + 3):
                n = slot_n
                if n < DN:
                    t, h = divmod(n, 4)
                    if n < 4:
                        pe.wait_ge(*ve_t(("dqk", 4 + n)))
                    if n < 2:
                        for k in range(2):
                            pe.wait_ge(*ve_t(("dv", 1, 2 * n + k)))
                    else:
                        pe.wait_ge(*ve_t(("diff scores", n - 2, 1)))
                    for c in range(2):
                        r = slice(64 * c, 64 * c + 64)
                        pe.matmul(ps[:, 2 * (n % 2) + c, 0:P * (t + 1)], dqk[r, h, P * t:P * t + P],
                                  dqk[r, 4 + h, 0:P * (t + 1)], start=True, stop=True)\
                          .then_inc(*pe_t.tick(("diff scores", n, c)))
                n = slot_n - 2
                if 0 <= n < DN:
                    pe.wait_ge(*ve_t(("diff weights", n)))
                    if n >= 2:
                        pe.wait_ge(*sc_t(("diff turned", n - 2)))
                    transposes(4 + n % 2, dmap(n, 0), n // 4 + 1, ("diff turned", n))
                n = slot_n - 3
                if 0 <= n < DN:
                    t, h = divmod(n, 4)
                    pe.wait_ge(*sc_t(("diff turned", n)))
                    if n >= 2:
                        pe.wait_ge(*ve_t(("diff out", n - 2)))
                    for k in range(t + 1):
                        m = pe.matmul(ps[:, 6 + n % 2, 0:P], dv[:, k, P * h:P * h + P], dturn(n)[:, P * k:P * k + P],
                                      start=(k == 0), stop=(k == t))
                    m.then_inc(*pe_t.tick(("diff out", n)))
            for h in range(4):
                pe.wait_ge(*sc_t(("diff square", h)))
                if h >= 2:
                    pe.wait_ge(*ve_t(("diff mean", h - 2)))
                pe.matmul(bank(4 + h % 2), ones, tmp[h % 2][:, 0:T], start=True, stop=True)\
                  .then_inc(*pe_t.tick(("diff mean", h)))

            for i in range(2):
                cols_unit(Unit(U_SU + i), (2 * i, 2 * i + 1), [ve_t(("diff scores", DN - 2 + i, c)) for c in range(2)])
            pe.wait_ge(s5_in, 16 * 39)
            pe.wait_ge(*sc_t("dt rows"))
            pe.wait_ge(*ve_t(("diff mean", 3)))
            pe.wait_ge(*ve_t(("diff out", DN - 1)))
            for c in range(2):
                pe.transpose(ps[:, 4, 16 * c:16 * c + 16], tmp[0][0:16, P * c:P * c + P], ident[0:16, 0:16])
                for q in range(2):
                    pe.transpose(ps[:, 5, 256 * c + P * q:256 * c + P * q + P], tmp[2 + c][:, P * q:P * q + P], ident)
            pe.transpose(ps[:, 4, 32:48], tmp[1][0:16, P:2 * P], ident[0:16, 0:16]).then_inc(*pe_t.tick("s5 params"))
            for n in range(4 * STEP + 1):
                if n < 4 * STEP:
                    j, q = divmod(n, 4)
                    if q == 0:
                        pe.wait_ge(*ve_t(("s5 wb", j)))
                    if n >= 2:
                        pe.wait_ge(*sc_t(("s5 wbt", n - 2)))
                    else:
                        pe.wait_ge(*ve_t(("su", 3)))
                    for c in range(2):
                        m = pe.transpose(ps[:, n % 2, P * c:P * c + P], wbj(c, j)[:, P * q:P * q + P], ident)
                    m.then_inc(*pe_t.tick(("s5 wbt", n)))
                if n:
                    j, q = divmod(n - 1, 4)
                    pe.wait_ge(*sc_t(("s5 wbt", n - 1)))
                    for b in range(4):
                        for c in range(2):
                            r = slice(32 * b, 32 * b + 32)
                            o = NSTEP * (4 * c + q)
                            m = pe.matmul(ps[:, 4 + b, o:o + NSTEP], tmp[4 + q % 2][r, P * c:P * c + P],
                                          su[r, q, j:T:STEP], start=(j == 0 and q == 0 and c == 0),
                                          stop=(j == STEP - 1), skip_group_check=True)
                    m.then_inc(*pe_t.tick(("s5 add", n - 1)))
            def s5_kernel(q):
                pe.wait_ge(*(po_t if q < 2 else ve_t)(("s5 cp", q)))
                for b in range(4):
                    pair = 4 * q + b
                    for c in range(2):
                        m = pe.matmul(ps[32 * b:32 * b + 32, 2, 0:256],
                                      bbd[c][:, pair, :], s5_cp(q)[c][:, b, 0:STEP, :].rearrange("p t h -> p (t h)"),
                                      start=(c == 0), stop=(c == 1))
                m.then_inc(*pe_t.tick(("s5 kernel", q)))

            pe.wait_ge(*sc_t(("s5 wbt", 4 * STEP - 1)))
            s5_kernel(0)
            for q in range(4):
                pe.wait_ge(*sc_t(("s5 kernel", q, 3)))
                if q >= 2:
                    pe.wait_ge(*ve_t(("s5 y", q - 2)))
                o = ps[:, q % 2, :].rearrange("p (c t) -> p c t", t=STEP)
                uu = su[:, q, :].rearrange("p (c t) -> p c t", t=STEP)
                for lag in range(STEP):
                    m = pe.matmul(o[:, :, lag:STEP], kbd[:, lag, :], uu[:, :, 0:STEP - lag], start=(lag == 0),
                                  stop=False, skip_group_check=True)
                m.then_inc(*pe_t.tick(("s5 lags", q)))
                if q == 0:
                    s5_kernel(1)
                    pe.wait_ge(*ve_t("s5 scanned"))
                for t in range(STEP):
                    for b in range(4):
                        for c in range(2):
                            m = pe.matmul(o[32 * b:32 * b + 32, 1:NSTEP, t], s5_cp(q)[c][:, b, t + 1, :],
                                          st[c][:, 4 * q + b, 0:NSTEP - 1], start=False, stop=False,
                                          skip_group_check=True)
                m.then_inc(*pe_t.tick(("s5 y", q)))
                if q in (1, 2):
                    s5_kernel(q + 1)
            u = Unit(U_GLU)
            pe.wait_ge(low_ready, u.split)
            pe.wait_ge(*ve_t(("s5 gelu low", 3)))
            pe.wait_ge(*ve_t("s5 scanned"))
            for j in range(4):
                for k in range(4):
                    w = slice(512 * k + P * j, 512 * k + P * j + P)
                    m = three(bank(3 + j), whi[u.slot][:, w], wlo[u.slot][:, w], mohi[:, 4 + k, :], molo[:, 4 + k, :],
                              k == 0, k == 3)
                m.then_inc(consumed, 2)
            pe.wait_ge(*ve_t("s5 squares"))
            pe.matmul(bank(7), ones, tmp[4][:, 0:T], start=True, stop=True).then_inc(*pe_t.tick("s5 mean"))

            pe.wait_ge(*ve_t(("s5 out low", 3)))
            def qk_mean(n):
                pe.wait_ge(*sc_t(("qk square", n)))
                if n >= 2:
                    pe.wait_ge(*ve_t(("qk mean", n - 2)))
                pe.matmul(bank(5 + n % 2), ones, tmp[n % 2][:, 0:T], start=True, stop=True)\
                  .then_inc(*pe_t.tick(("qk mean", n)))

            for i in range(8):
                cols_unit(Unit(U_G + i), (2 * i % 4, 2 * i % 4 + 1),
                          [ve_t(("zg", 2 * i + c - 4)) for c in range(2)] if i >= 2 else ())
                if 1 <= i <= 4:
                    qk_mean(2 * i - 2)
                    qk_mean(2 * i - 1)
                if i == 6:
                    pe.wait_ge(*ve_t("gate weights"))
                    for t in range(NT):
                        x = slice(P * t, P * t + P)
                        for k in range(DC):
                            m = three(ps[:, 4, 8 * t:8 * t + 8], xhi[:, k, x], xlo[:, k, x], bah[:, k, :], bal[:, k, :],
                                      k == 0, k == DC - 1)
                    m.then_inc(*pe_t.tick("gates"))
            pe.wait_ge(*ve_t("log decay"))
            for t in range(NT):
                m = pe.matmul(ps[:, 4, 64 + 4 * t:68 + 4 * t], tri, gates[:, 4 * t + 16:4 * t + 20], start=True, stop=True)
            m.then_inc(*pe_t.tick("cumulated"))
            pe.wait_ge(*ve_t("cumulated"))
            kb, qb, gcR, beR, decT, LT, atT, CT, Dm, DT, X, kTok, vbT, kbe, kl, nwT = gb
            vn, qe, S = tmp[3], tmp[4], tmp[5]
            with loop(book, "pe", "blk", pe, "b", NT) as b:
                def v(label):
                    return ve_t(label, b=b)

                def hs(h):
                    return slice(P * h, P * h + P)

                pe.wait_ge(*v("columns"))
                for h in range(GH):
                    pe.matmul(ps[:, 0, hs(h)], gates[:, 56 + h:57 + h].to_broadcast([P, P]), tri, start=True, stop=True)
                    m = pe.matmul(ps[:, 1, hs(h)], gates[:, 60 + h:61 + h].to_broadcast([P, P]), ident, start=True,
                                  stop=True)
                m.then_inc(*pe_t.tick("row forms"))
                pe.wait_ge(*sc_t("blocks", b=b))
                for h in range(GH):
                    pe.matmul(ps[:, 2, hs(h)], kb[:, hs(h)], kb[:, hs(h)], start=True, stop=True)
                    m = pe.matmul(ps[:, 3, hs(h)], kb[:, hs(h)], qb[:, hs(h)], start=True, stop=True)
                m.then_inc(*pe_t.tick("kk"))
                for h in range(GH):
                    pe.transpose(ps[:, 4, hs(h)], kb[:, hs(h)], ident)
                    m = pe.transpose(ps[:, 5, hs(h)], X[:, hs(h)], ident)
                m.then_inc(*pe_t.tick("turned"))
                for s in range(7):
                    for g in range(2):
                        pe.wait_ge(*v(("level", s, g)))
                        if s >= 2:
                            pe.wait_ge(*v(("D", s - 1, g)))
                        elif s == 1:
                            pe.wait_ge(*v(("DT", 0, g)))
                        for h in (2 * g, 2 * g + 1):
                            m = pe.matmul(ps[:, 6 + g, hs(h)], CT[:, hs(h)], ident if s == 0 else Dm[:, hs(h)],
                                          start=True, stop=True)
                        m.then_inc(*pe_t.tick(("X", s, g)))
                    for g in range(2):
                        if s == 0:
                            continue
                        pe.wait_ge(*sc_t(("X", s, g), b=b))
                        if s == 1:
                            pe.wait_ge(*v("kk used"))
                        for h in (2 * g, 2 * g + 1):
                            m = pe.matmul(ps[:, 2 * g + 1, hs(h)], X[:, hs(h)], DT[:, hs(h)], start=True, stop=True)
                        if s < 6:
                            for h in (2 * g, 2 * g + 1):
                                m = pe.matmul(ps[:, 2 * g, hs(h)], DT[:, hs(h)], X[:, hs(h)], start=True, stop=True)
                        m.then_inc(*pe_t.tick(("DD", s, g)))
                pe.wait_ge(*v(("DT", 6, 1)))
                pe.wait_ge(*v("kbe"))
                for h in range(GH):
                    m = pe.matmul(ps[:, 2, hs(h)], kbe[:, hs(h)], DT[:, hs(h)], start=True, stop=True)
                m.then_inc(*pe_t.tick("w"))
                pe.wait_ge(*sc_t("w", b=b))
                for h in range(GH):
                    pe.matmul(ps[:, 3, hs(h)], DT[:, hs(h)], vbT[:, hs(h)], start=True, stop=False)
                    m = pe.matmul(ps[:, 3, hs(h)], nwT[:, hs(h)], S[:, hs(h)], start=False, stop=True)
                m.then_inc(*pe_t.tick("v new"))
                pe.wait_ge(*v("v new"))
                pe.wait_ge(*v("kl"))
                for h in range(GH):
                    pe.matmul(ps[:, 4, hs(h)], S[:, hs(h)], qe[:, hs(h)], start=True, stop=False)
                    pe.matmul(ps[:, 4, hs(h)], vn[:, hs(h)], atT[:, hs(h)], start=False, stop=True)
                    m = pe.matmul(ps[:, 5, hs(h)], kl[:, hs(h)], vn[:, hs(h)], start=True, stop=True)
                m.then_inc(*pe_t.tick("delta out"))
            pe.wait_ge(*ve_t("state", b=NT - 1))
            for h in range(GH):
                pe.wait_ge(*sc_t(("delta square", h)))
                pe.matmul(bank((6 + h) % 8), ones, tmp[h % 2][:, 0:T], start=True, stop=True)\
                  .then_inc(*pe_t.tick(("delta mean", h)))
            means = {2 + h: ve_t(("delta mean", h)) for h in range(GH)}
            for i, pair in enumerate(WO_ORDER):
                if pair < 2:
                    pe.wait_ge(*ve_t(("delta low", 2 * pair + 1)))
                rows_unit(Unit(U_WO + i), lambda k, pair=pair: mohi[:, 2 * pair + k, :],
                          lambda k, pair=pair: molo[:, 2 * pair + k, :], i == 0, i == 5, None if i else means)
            ffn(U_UP, "f0", "ffn")
            total("fin1")

            with loop(book, "pe", "layer", pe, "layer", LAYERS) as l:
                ffn(V_UP1, "f1", "n1", l)
                first_unit(Unit(V_WIN, l), "nm", column=True, then=Unit(V_WIN + 1, l), layer=l)

                def v(label):
                    return ve_t(label, layer=l)

                def s_(label):
                    return sc_t(label, layer=l)

                def mla_means():
                    pe.wait_ge(*s_(("mla square", 1)))
                    pe.matmul(bank(4), ones, tmp[0][:, 0:T], start=True, stop=False)
                    pe.matmul(bank(4), ones, tmp[1][:, 0:T], start=False, stop=True).then_inc(*pe_t.tick("q_a mean"))
                    pe.wait_ge(*s_(("mla square", 2)))
                    pe.matmul(bank(5), ones, tmp[2][:, 0:T], start=True, stop=True).then_inc(*pe_t.tick("kv_a mean"))

                def mla_q(h):
                    for k in range(2):
                        m = pe.matmul(ps[0:QD, 4, :], wqb[:, k, QD * h:QD * h + QD], z2[:, k, :], start=(k == 0),
                                      stop=(k == 1))
                    m.then_inc(*pe_t.tick(("mla q", h)))

                def mla_k(h):
                    pe.wait_ge(*s_(("mla q", h)))
                    pe.wait_ge(*v(("mla sin", h - 1) if h else ("pool out", 1)))
                    pe.matmul(ps[0:QD, 5, :], turn[0:QD, :], qf[0:QD, h, :], start=True, stop=True)\
                      .then_inc(*pe_t.tick(("mla q turned", h)))
                    if h:
                        pe.wait_ge(*s_(("mla k", h - 1)))
                    pe.matmul(ps[0:HD, 6, :], wkvb[:, h, 0:HD], z2[:, 2, :], start=True, stop=True)\
                      .then_inc(*pe_t.tick(("mla k", h)))

                def between(unit):
                    def after(t):
                        h = NT * unit + t
                        if h < HEADS:
                            mla_k(h)
                            if h + 1 < HEADS:
                                mla_q(h + 1)
                        if h == HEADS:
                            pe.matmul(ps[0:QD, 7, :], turn[0:QD, :], z2[0:QD, 3, :], start=True, stop=True)\
                              .then_inc(*pe_t.tick("k rope"))
                    return after

                for i in range(2, 6):
                    w = [v(("z", 2 * i + c - 4)) for c in range(2)]
                    cols_unit(Unit(V_WIN + i, l), (2 * i % 4, 2 * i % 4 + 1), w)
                    if i == 2:
                        mla_means()
                    if i == 4:
                        pe.wait_ge(layer_in, l * 128 + 128)
                        pe.wait_ge(*v("kv_a"))
                        mla_q(0)
                pe.wait_ge(*v("pooled"))
                for k in range(2):
                    m = pe.matmul(bank(7 - 2 * k), poolw[:, k, :], z2[:, 4 + k, :], start=True, stop=True)
                m.then_inc(*pe_t.tick("pool out"))
                tokens_unit(Unit(V_WIN + 6, l), COLS, 0, [v(("z", 8 + t)) for t in range(NT)], between(0))
                tokens_unit(Unit(V_WIN + 7, l), VF - COLS, COLS, [v(("vf", 0, t)) for t in range(NT)], between(1))
                for t in range(NT):
                    pe.wait_ge(*v(("vf", 1, t)))
                    m = pe.matmul(ps[:, t, 0:HEADS * HD], z2[:, 2, P * t:P * t + P],
                                  wkvb[:, :, HD:2 * HD], start=True, stop=True)
                    m.then_inc(*pe_t.tick(("mla v", t)))
                pe.wait_ge(*v("log f"))
                pe.wait_ge(*s_(("mla q", HEADS - 1)))
                for t in range(NT):
                    for k in range(t + 1):
                        m = pe.matmul(ps[:, 4, HEADS * t:HEADS * t + HEADS], tri if k == t else ones,
                                      small[:, HEADS * k:HEADS * k + HEADS], start=(k == 0), stop=(k == t))
                m.then_inc(*pe_t.tick("fox sum"))
                pe.wait_ge(*v("fox columns"))
                pe.wait_ge(*s_(("mla k", HEADS - 1)))

                def fr(h):
                    return slice(64 * (h % 2), 64 * (h % 2) + 64)

                def operands(n):
                    kind, h, t = n // (HEADS * NT), n // NT % HEADS, n % NT
                    if kind == 0:
                        return (qf[0:QD, h, P * t:P * t + P], kf[0:QD, h, 0:P * (t + 1)],
                                lambda k: mv[:, k, HD * h:HD * h + HD], h, t)
                    return (z2[fr(h), 6 + h // 2, P * t:P * t + P], z2[fr(h), 9 + h // 2, 0:P * (t + 1)],
                            lambda k: vf[:, k, HD * h:HD * h + HD], h, t)

                pe.wait_ge(*v(("mla v", NT - 1)))
                pe.wait_ge(*v("kf"))
                for slot_n in range(AN + 3):
                    n = slot_n
                    if n < AN:
                        q, k, _, h, t = operands(n)
                        if n >= AN // 2 and t == 0:
                            if h:
                                pe.wait_ge(*s_(("fox row", h - 1)))
                            for b in range(NT):
                                m = pe.matmul(ps[:, 7, P * b:P * b + P],
                                              small[:, 24 + HEADS * b + h:25 + HEADS * b + h].to_broadcast([P, P]),
                                              ident, start=True, stop=True)
                            m.then_inc(*pe_t.tick(("fox row", h)))
                        if n >= 3:
                            pe.wait_ge(*v(("scores", n - 3)))
                        pe.matmul(ps[:, SB[n % 3], 0:P * (t + 1)], q, k, start=True, stop=True)\
                          .then_inc(*pe_t.tick(("scores", n)))
                    n = slot_n - 2
                    if 0 <= n < AN:
                        pe.wait_ge(*v(("weights", n)))
                        if n >= 2:
                            pe.wait_ge(*s_(("turned", n - 2)))
                        transposes(TB_[n % 2], asc(n), n % NT + 1, ("turned", n))
                    n = slot_n - 3
                    if 0 <= n < AN:
                        _, _, vals, h, t = operands(n)
                        pe.wait_ge(*s_(("turned", n)))
                        if n >= 2:
                            pe.wait_ge(*v(("out", n - 2)))
                        for k in range(t + 1):
                            m = pe.matmul(ps[fr(h), OB[n % 2], 0:P], vals(k), aturn(n)[:, P * k:P * k + P],
                                          start=(k == 0), stop=(k == t))
                        m.then_inc(*pe_t.tick(("out", n)))
                pe.wait_ge(*v(("low", 5)))
                for i in range(4):
                    rows_unit(Unit(V_WO + i, l), lambda k, i=i: xhi[:, 2 * i + k, :], lambda k, i=i: xlo[:, 2 * i + k, :],
                              i == 0, i == 3)
                ffn(V_UP2, "f2", "n2", l)
            total("fin2")
            for t in range(NT):
                for j in range(DC):
                    if t == 0:
                        pe.wait_ge(*ve_t(("y", j)))
                    if t and j % 4 == 0:
                        pe.wait_ge(*ve_t(("out half", t - 1, j // 4)))
                    m = pe.transpose(ps[:, j // 4, P * (j % 4):P * (j % 4) + P], xT[:, j, P * t:P * t + P], ident)
                    if j % 4 == 3:
                        m.then_inc(*pe_t.tick(("out half", t, j // 4)))


        @blk.scalar
        def _(sc):
            def high(u):
                sc.wait_ge(landed[u.slot], u.landed)
                if not u.early:
                    sc.wait_ge(consumed, u.before - 8)
                sc.activation(whi[u.slot][:, :], raw[u.slot][:, :], ACT.Copy).then_inc(high_ready, 1)

            def norm(tag, weight, x_of=None, reads=None, then=None, **at):
                x_of = x_of or (lambda j: ve_t(("x", tag, j), **at))
                for j in range(DC):
                    sc.wait_ge(*x_of(j))
                    if j == DC - 2 and reads is not None:
                        sc.wait_ge(consumed, reads.done)
                    if weight is not None:
                        sc.activation(xhi[:, j, :], xT[:, j, :], ACT.Copy, scale=weight(j))\
                          .then_inc(*sc_t.tick(("xw high", tag, j)))
                    if j >= 2:
                        sc.wait_ge(*po_t(("sum", tag, max(j - 2, 1)), **at))
                    sc.activation(tmp[j % 2][:, 0:T], xT[:, j, :], ACT.Square).then_inc(*sc_t.tick(("square", tag, j)))
                if then is not None:
                    high(then)
                sc.wait_ge(*ve_t(("mean", tag), **at))
                sc.activation(rb[:, :], rb[:, :], ACT.Sqrt).then_inc(*sc_t.tick(("sqrt", tag)))

            def ffn(up, name, bias, layer=None):
                at = {} if layer is None else {"layer": layer}
                with loop(book, "sc", name, sc, "i", 11) as i:
                    for c in range(2):
                        sc.wait_ge(*ve_t(("gate in" if bias else "gate", name, c), i=i, **at))
                        kw = {"bias": small[:, 12 + c:13 + c]} if bias else {}
                        sc.activation(tmp[c][:, 0:T], tmp[c][:, 0:T], ACT.Silu, **kw).then_inc(*sc_t.tick(("silu", name, c)))
                    high(Unit(up + 2, layer, i))
                    for c in range(2):
                        sc.wait_ge(*ve_t(("hidden", name, c), i=i, **at))
                        sc.activation(hhi[:, ds(i * 2 + c, 1), :].rearrange("p a t -> p (a t)"), tmp[4 + c][:, 0:T],
                                      ACT.Copy).then_inc(*sc_t.tick(("hidden high", name, c)))
                    high(Unit(up + 3, layer, i))
                dn = up + 22
                with loop(book, "sc", name + "d", sc, "i", 4) as i:
                    high(Unit(dn + 2, layer, i))
                    high(Unit(dn + 3, layer, i))
                high(Unit(dn + 10, layer))

            high(Unit(0))
            norm("attn", lambda j: pcol("attn", j), then=Unit(1))
            for u in range(2, U_SU + 2):
                high(Unit(u))
                if u == U_DV + 1:
                    sc.wait_ge(*ve_t("lambda sums"))
                    sc.activation(small[:, 22:24], small[:, 20:22], ACT.Exp).then_inc(*sc_t.tick("lambda"))
            for slot_n in range(DN + 2):
                n = slot_n
                if n < DN:
                    w, s0 = P * (n // 4 + 1), 26 + 8 * (n % 2)
                    for c in range(2):
                        sc.wait_ge(*ve_t(("diff max", n, c)))
                        x = dmap(n, c)[:, 0:w]
                        sc.activation(x, x, ACT.Exp, bias=small[:, s0 + c:s0 + c + 1],
                                      accum_out=small[:, s0 + 2 + c:s0 + 3 + c]).then_inc(*sc_t.tick(("diff exp", n, c)))
                n = slot_n - 2
                if 0 <= n < DN:
                    w = P * (n // 4 + 1)
                    sc.wait_ge(*pe_t(("diff turned", n)))
                    if n >= 2:
                        sc.wait_ge(*pe_t(("diff out", n - 2)))
                    sc.activation(dturn(n)[:, 0:w], ps[:, 4 + n % 2, 0:w], ACT.Copy).then_inc(*sc_t.tick(("diff turned", n)))
            for h in range(4):
                sc.wait_ge(*ve_t(("diff out", DN - 4 + h)))
                if h >= 2:
                    sc.wait_ge(*pe_t(("diff mean", h - 2)))
                elif h == 0:
                    sc.wait_ge(*pe_t(("diff turned", DN - 1)))
                sc.activation(tmp[h % 2][:, 0:T], osum[:, h, :], ACT.Square).then_inc(*sc_t.tick(("diff square", h)))
            for h in range(4):
                sc.wait_ge(*ve_t(("diff mean", h)))
                sc.activation(dx[0][:, :] if h == 3 else tmp[2 + h][:, 0:T], dx[0][:, :] if h == 3 else tmp[2 + h][:, 0:T],
                              ACT.Sqrt).then_inc(*sc_t.tick(("diff sqrt", h)))
            for h in range(4):
                sc.wait_ge(*ve_t(("diff normed", h)))
                sc.activation(mohi[:, 8 + h, :], osum[:, h, :], ACT.Copy, scale=1.0 - LAM_INIT)\
                  .then_inc(*sc_t.tick(("diff high", h)))
            sc.wait_ge(s5_in, 16 * 39)
            sc.activation(tmp[1][0:16, P:2 * P].rearrange("b (e p) -> b e p", e=2),
                          tmp[1][0:16, 0:2].unsqueeze(2).to_broadcast([16, 2, 64]), ACT.Exp).then_inc(*sc_t.tick("dt rows"))
            sc.wait_ge(*ve_t("s5 phase"))
            sc.activation(slot(5), slot(3), ACT.Exp).then_inc(*sc_t.tick("s5 size"))
            sc.activation(slot(7), slot(6), ACT.Sin).then_inc(*sc_t.tick("s5 sin"))
            sc.activation(slot(8), slot(6), ACT.Sin, scale=0.5).then_inc(*sc_t.tick("s5 half sin"))
            for n in range(4 * STEP):
                sc.wait_ge(*pe_t(("s5 wbt", n)))
                if n >= 2:
                    sc.wait_ge(*pe_t(("s5 add", n - 2)))
                else:
                    sc.wait_ge(*ve_t("s5 bbar"))
                sc.activation(tmp[4 + n % 2][:, 0:2 * P], ps[:, n % 2, 0:2 * P], ACT.Copy)\
                  .then_inc(*sc_t.tick(("s5 wbt", n)))
            for q in range(4):
                sc.wait_ge(*pe_t(("s5 kernel", q)))
                if q:
                    sc.wait_ge(*pe_t(("s5 lags", q - 1)))
                else:
                    sc.wait_ge(*po_t("zero k"))
                for b in range(4):
                    r = slice(32 * b, 32 * b + 32)
                    sc.activation(kbd[r, :, 32 * b:32 * b + 32], ps[r, 2, 0:256].rearrange("p (t h) -> p t h", h=32),
                                  ACT.Copy).then_inc(*sc_t.tick(("s5 kernel", q, b)))
            high(Unit(U_GLU))
            for q in range(4):
                sc.wait_ge(*ve_t(("s5 y", q)))
                sc.activation(su[:, q, :], su[:, q, :], ACT.Gelu_apprx_tanh).then_inc(*sc_t.tick(("s5 gelu", q)))
            for q in range(4):
                sc.wait_ge(*sc_t(("s5 gelu", q)))
                sc.activation(mohi[:, 4 + q, :], su[:, q, :], ACT.Copy).then_inc(*sc_t.tick(("s5 high", q)))
            high(Unit(U_G))
            for j in range(4):
                sc.wait_ge(consumed, Unit(U_GLU).began + 2 * j + 2)
                sc.activation(tmp[j][:, 0:T], bank(3 + j), ACT.Sigmoid, bias=pcol("bglu", j))\
                  .then_inc(*sc_t.tick(("s5 sigmoid", j)))
            sc.wait_ge(*ve_t("s5 mean"))
            sc.activation(tmp[5][:, 0:T], tmp[5][:, 0:T], ACT.Sqrt).then_inc(*sc_t.tick("s5 sqrt"))
            for j in range(4):
                sc.wait_ge(*ve_t(("s5 out", j)))
                sc.activation(mohi[:, 4 + j, :], su[:, j, :], ACT.Copy).then_inc(*sc_t.tick(("s5 out high", j)))
            high(Unit(U_G + 1))
            for n in range(16 + 2):
                if n < 12:
                    sc.wait_ge(*ve_t(("conv", n)))
                    sc.activation(zg[:, n, 3:T + 3], tmp[2 + n % 2][:, 0:T], ACT.Silu).then_inc(*sc_t.tick(("conv silu", n)))
                elif n < 16:
                    sc.wait_ge(*ve_t(("zg", n)))
                    sc.activation(zg[:, n, 3:T + 3], zg[:, n, 3:T + 3], ACT.Silu).then_inc(*sc_t.tick(("z silu", n - 12)))
                if n < 8:
                    if n >= 2:
                        sc.wait_ge(*pe_t(("qk mean", n - 2)))
                    sc.wait_ge(*sc_t(("conv silu", n)))
                    sc.activation(tmp[n % 2][:, 0:T], zg[:, n, 3:T + 3], ACT.Square)\
                      .then_inc(*sc_t.tick(("qk square", n)))
                if n % 2 and n // 2 + 2 < 9:
                    high(Unit(U_G + 2 + n // 2))
                if n == 9:
                    sc.wait_ge(gate_in, 64)
                    sc.activation(bah[:, :, :], baw[:, :, :], ACT.Copy).then_inc(*sc_t.tick("gate high"))
                for k in (2 * n - 10, 2 * n - 9) if 5 <= n < 9 else ():
                    sc.wait_ge(*ve_t(("qk mean", k)))
                    sc.activation(tmp[4 + k % 2][:, 0:T], tmp[4 + k % 2][:, 0:T], ACT.Sqrt).then_inc(*sc_t.tick(("qk sqrt", k)))
            sc.wait_ge(*ve_t(("ba", NT - 1)))
            sc.activation(gates[:, 0:16].rearrange("p (t h) -> p t h", h=4),
                          small[:, 0:32].rearrange("p (t c) -> p t c", c=8)[:, :, 0:4], ACT.Sigmoid)\
              .then_inc(*sc_t.tick("beta"))
            sc.wait_ge(*ve_t("gate size"))
            sc.activation(small[:, 48:64], small[:, 48:64], ACT.Exp, scale=-1.0).then_inc(*sc_t.tick("gate exp"))
            sc.activation(gates[:, 48:52], gates[:, 48:52], ACT.Exp).then_inc(*sc_t.tick("a exp"))
            sc.wait_ge(*sc_t("gate exp"))
            sc.activation(small[:, 48:64], small[:, 48:64], ACT.Ln, bias=1.0).then_inc(*sc_t.tick("gate ln"))
            with loop(book, "sc", "blk", sc, "b", NT) as b:
                def blk_of(c0):
                    return zg[:, c0:c0 + 4, ds(b * P + 3, P)]

                def heads(x):
                    return x[:, 0:T].rearrange("p (h t) -> p h t", h=GH)

                sc.wait_ge(*ve_t("columns", b=b))
                for c0, dst in ((4, gb[0]), (0, gb[1])):
                    sc.activation(heads(dst), blk_of(c0), ACT.Copy).then_inc(*sc_t.tick(("block", c0)))
                sc.activation(heads(gb[10]), blk_of(8), ACT.Copy).then_inc(*sc_t.tick("blocks"))
                sc.activation(small[:, 68:72], small[:, 64:68], ACT.Exp).then_inc(*sc_t.tick("exp columns"))
                sc.wait_ge(*ve_t("row forms", b=b))
                sc.activation(tmp[0][:, 0:T], gb[2][:, :], ACT.Exp).then_inc(*sc_t.tick("exp rows"))
                sc.wait_ge(*ve_t("decay", b=b))
                sc.activation(gb[4][:, :], gb[4][:, :], ACT.Exp).then_inc(*sc_t.tick("decay"))
                sc.activation(small[:, 76:80], small[:, 76:80], ACT.Exp).then_inc(*sc_t.tick("to last"))
                sc.wait_ge(*pe_t("turned", b=b))
                sc.activation(gb[11][:, :], bank(4), ACT.Copy).then_inc(*sc_t.tick("kTok"))
                for s in range(1, 7):
                    for g in range(2):
                        hs = slice(2 * P * g, 2 * P * g + 2 * P)
                        sc.wait_ge(*pe_t(("X", s, g), b=b))
                        sc.activation(gb[10][:, hs], ps[:, 6 + g, hs], ACT.Copy).then_inc(*sc_t.tick(("X", s, g)))
                sc.wait_ge(*pe_t("w", b=b))
                sc.activation(gb[15][:, :], bank(2), ACT.Copy, scale=-1.0).then_inc(*sc_t.tick("w"))
            for h in range(GH):
                if h >= 2:
                    sc.wait_ge(*pe_t(("delta mean", h - 2)))
                else:
                    sc.wait_ge(*ve_t("state", b=NT - 1))
                sc.activation(tmp[h % 2][:, 0:T], zg[:, h, 3:T + 3], ACT.Square).then_inc(*sc_t.tick(("delta square", h)))
            for h in range(GH):
                sc.wait_ge(*ve_t(("delta mean", h)))
                sc.activation(tmp[2 + h][:, 0:T], tmp[2 + h][:, 0:T], ACT.Sqrt).then_inc(*sc_t.tick(("delta sqrt", h)))
            high(Unit(U_WO + 1))
            for h in range(GH):
                if h in (2, 3):
                    high(Unit(U_WO + h))
                sc.wait_ge(*ve_t(("delta normed", h)))
                sc.activation(mohi[:, h, :], zg[:, h, 3:T + 3], ACT.Copy).then_inc(*sc_t.tick(("delta high", h)))
            for u in range(U_WO + 4, U_WO + 6):
                high(Unit(u))
            high(Unit(U_UP))
            norm("ffn", lambda j: pcol("ffn", j), then=Unit(U_UP + 1))
            ffn(U_UP, "f0", True)
            norm("fin1", None)

            with loop(book, "sc", "layer", sc, "layer", LAYERS) as l:
                def v(label):
                    return ve_t(label, layer=l)

                def p_(label):
                    return pe_t(label, layer=l)

                high(Unit(V_UP1, l))
                norm("n1", lambda j: lv[:, j:j + 1], then=Unit(V_UP1 + 1, l), layer=l)
                ffn(V_UP1, "f1", False, l)
                high(Unit(V_WIN, l))
                norm("nm", lambda j: lv[:, 8 + j:9 + j], then=Unit(V_WIN + 1, l), layer=l)
                for u in range(V_WIN + 2, V_WIN + 4):
                    high(Unit(u, l))
                for n in range(3):
                    sc.wait_ge(*v(("z", n)))
                    sc.activation(tmp[n][:, 0:T], z2[:, n, :], ACT.Square).then_inc(*sc_t.tick(("mla square", n)))
                high(Unit(V_WIN + 4, l))
                sc.wait_ge(*v("mla means"))
                for n in range(2):
                    sc.activation(tmp[3 + n][:, 0:T], tmp[3 + n][:, 0:T], ACT.Sqrt).then_inc(*sc_t.tick(("mla sqrt", n)))
                for u in range(V_WIN + 5, V_WIN + 7):
                    high(Unit(u, l))

                def mla_q(h):
                    sc.wait_ge(*p_(("mla q", h)))
                    sc.activation(qf[0:QD, h, :], ps[0:QD, 4, :], ACT.Copy, scale=QD ** -0.5)\
                      .then_inc(*sc_t.tick(("mla q", h)))

                mla_q(0)
                u = Unit(V_WIN + 7, l)
                sc.wait_ge(landed[u.slot], u.landed)
                sc.wait_ge(consumed, u.before - 8)
                sc.activation(whi[u.slot][:, :].rearrange("p (k c) -> p k c", k=DC)[:, :, 0:VF - COLS],
                              raw[u.slot][:, :].rearrange("p (k c) -> p k c", k=DC)[:, :, 0:VF - COLS],
                              ACT.Copy).then_inc(high_ready, 1)
                for h in range(HEADS):
                    if h == NT + 1:
                        high(Unit(V_WO, l))
                    sc.wait_ge(*p_(("mla k", h)))
                    sc.activation(kf[0:HD, h, :], ps[0:HD, 6, :], ACT.Copy).then_inc(*sc_t.tick(("mla k", h)))
                    if h + 1 < HEADS:
                        mla_q(h + 1)
                sc.wait_ge(*v("f size"))
                sc.activation(small[:, 24:48], small[:, 24:48], ACT.Exp, scale=-1.0).then_inc(*sc_t.tick("f exp"))
                sc.wait_ge(*sc_t("f exp", layer=l))
                sc.activation(small[:, 24:48], small[:, 24:48], ACT.Ln, bias=1.0).then_inc(*sc_t.tick("f ln"))
                sc.wait_ge(consumed, Unit(V_WIN + 7, l).done)
                for k in range(2):
                    sc.wait_ge(*v(("pool out", k)))
                    sc.activation(xhi[:, 3 + k, :], z2[:, 4 + k, :], ACT.Copy).then_inc(*sc_t.tick(("pool high", k)))

                for slot_n in range(AN + 3):
                    n = slot_n
                    if n < AN:
                        if n >= AN // 2 and n % NT == 0:
                            h = n // NT - HEADS
                            sc.wait_ge(*p_(("fox row", h)))
                            if h >= 2:
                                sc.wait_ge(*v(("scores", n - NT - 1)))
                            sc.activation(arow(h)[:, 0:T], bank(7), ACT.Copy).then_inc(*sc_t.tick(("fox row", h)))
                        s = asc(n)[:, 0:P * (n % NT + 1)]
                        sc.wait_ge(*v(("max", n)))
                        sc.activation(s, s, ACT.Exp, bias=small[:, 70 + n % 2:71 + n % 2],
                                      accum_out=small[:, 72 + n % 2:73 + n % 2]).then_inc(*sc_t.tick(("exp", n)))
                    n = slot_n - 2
                    if 0 <= n < AN:
                        w = P * (n % NT + 1)
                        sc.wait_ge(*p_(("turned", n)))
                        if n >= 2:
                            sc.wait_ge(*p_(("out", n - 2)))
                        sc.activation(aturn(n)[:, 0:w], ps[:, TB_[n % 2], 0:w], ACT.Copy).then_inc(*sc_t.tick(("turned", n)))
                    n = slot_n - 3
                    if n >= 0 and n % 8 == 7:
                        sc.wait_ge(*v(("out", n)))
                        sc.activation(xhi[:, CHUNKS[n // 8], :], tmp[3][:, 0:T], ACT.Copy)\
                          .then_inc(*sc_t.tick(("high", n // 8)))
                for u in range(V_WO + 1, V_WO + 4):
                    high(Unit(u, l))
                high(Unit(V_UP2, l))
                norm("n2", lambda j: lv[:, 16 + j:17 + j], reads=Unit(V_WO + 3, l), then=Unit(V_UP2 + 1, l),
                     layer=l)
                ffn(V_UP2, "f2", False, l)
            norm("fin2", None, lambda j: ve_t(("x", "end", j), layer=LAYERS - 1))

        @blk.vector
        def _(ve):
            def own(**at):
                ve.wait_ge(*ve_t.last(**at))

            def mean(tag, n, dst, src, eps, sqrt_label, **at):
                ve.tensor_scalar(dst, src, 1.0 / n, eps, ALU.mult, ALU.add).then_inc(*ve_t.tick(tag))
                ve.wait_ge(*sc_t(sqrt_label, **at))
                ve.reciprocal(dst, dst).then_inc(*ve_t.tick(("root of", tag)))
                own(**at)

            def residual(tag, unit, scale, weight, x_tag=None, **at):
                for j in range(DC + 2):
                    if j < DC:
                        ve.wait_ge(consumed, unit.began + j + 1)
                        ve.scalar_tensor_tensor(out=xT[:, j, :], in0=bank((j + 4) % 8), scalar=scale, in1=xT[:, j, :],
                                                op0=ALU.mult, op1=ALU.add).then_inc(*ve_t.tick(("x", x_tag or tag, j)))
                    if j >= 2 and weight is not None:
                        low(tag, weight, j - 2, **at)

            def low(tag, weight, j, **at):
                ve.wait_ge(*sc_t(("xw high", tag, j), **at))
                ve.wait_ge(*ve_t(("x", tag, j), **at))
                ve.scalar_tensor_tensor(out=xlo[:, j, :], in0=xT[:, j, :], scalar=weight(j),
                                        in1=xhi[:, j, :].bitcast(F32), op0=ALU.mult, op1=ALU.subtract)\
                  .then_inc(*ve_t.tick(("xw low", tag, j)))

            def root(tag, wait=True, **at):
                ve.wait_ge(*pe_t(("total", tag), **at))
                ve.tensor_scalar(rb[:, :], bank(7), 1.0 / D, EPS, ALU.mult, ALU.add).then_inc(*ve_t.tick(("mean", tag)))
                ve.wait_ge(*sc_t(("sqrt", tag), **at))
                ve.reciprocal(rb[:, :], rb[:, :]).then_inc(*ve_t.tick(("root", tag)))
                if wait:
                    own(**at)

            def root_column(tag, **at):
                ve.wait_ge(*pe_t(("root column", tag), **at))
                ve.tensor_copy(rcol[:, :], ps[:, 6, 0:NT]).then_inc(*ve_t.tick(("rcol", tag)))
                own(**at)

            def mul(dst, a, b, label, op=ALU.mult):
                ve.tensor_tensor(dst, a, b, op).then_inc(*ve_t.tick(label))

            def gated(up, name, tag, layer=None):
                at = {} if layer is None else {"layer": layer}
                with loop(book, "ve", name, ve, "i", 11) as i:
                    ve.wait_ge(*ve_t(("hidden", name, 1), i=i - 1, **at))
                    ve.wait_ge(*ve_t(("root", tag), **at))
                    for c in range(2):
                        ve.wait_ge(consumed, Unit(up, layer, i).began + 4 * c + 4)
                        mul(tmp[c][:, 0:T], bank(c), rb[:, :], ("gate", name, c))
                    for c in range(2):
                        ve.wait_ge(consumed, Unit(up + 1, layer, i).began + 4 * c + 4)
                        mul(tmp[2 + c][:, 0:T], bank(2 + c), rb[:, :], ("up", name, c))
                        own(i=i, **at)
                        ve.wait_ge(*sc_t(("silu", name, c), i=i, **at))
                        ve.wait_ge(*po_t(("hidden low", name, c), i=i - 1, **at))
                        mul(tmp[4 + c][:, 0:T], tmp[2 + c][:, 0:T], tmp[c][:, 0:T], ("hidden", name, c))

            def conv_gated(up, name):
                Z = (tmp[2], tmp[3])
                for z in Z:
                    ve.memset(z[:, 0:2], 0.0).then_inc(*ve_t.tick(("pad", z is Z[0])))
                wt = pv[:, PV["fconv"]:PV["fconv"] + 4 * 44].rearrange("p (k g f) -> p k g f", k=4, g=2)
                with loop(book, "ve", name, ve, "i", 11) as i:
                    ve.wait_ge(*ve_t(("hidden", name, 1), i=i - 1))
                    for g in range(2):
                        ve.tensor_copy(small[:, 0:16].rearrange("p (k g c) -> p k g c", k=4, g=2)[:, :, g, :],
                                       wt[:, :, g, ds(i * 2, 2)]).then_inc(*ve_t.tick(("taps", g)))
                    own(i=i)
                    for g in range(2):
                        for c in range(2):
                            n = 2 * g + c
                            ve.wait_ge(consumed, Unit(up + g, None, i).began + 4 * c + 4)
                            z = Z[c]
                            mul(z[:, 2:T + 2], bank(n), rb[:, :], (("gate", "up")[g], name, c))
                            own(i=i)
                            dst = tmp[4 * g + c][:, 0:T]
                            if g:
                                ve.wait_ge(*po_t(("hidden low", name, c), i=i - 1))
                            ve.tensor_scalar(dst, z[:, 0:T], small[:, n:n + 1], None, ALU.mult)\
                              .then_inc(*ve_t.tick(("tap", name, n, 0)))
                            for k in (1, 2):
                                own(i=i)
                                ve.scalar_tensor_tensor(out=dst, in0=z[:, k:T + k], scalar=small[:, 4 * k + n:4 * k + n + 1],
                                                        in1=dst, op0=ALU.mult, op1=ALU.add)\
                                  .then_inc(*ve_t.tick(("gate in", name, c) if k == 2 and g == 0 else ("tap", name, n, k)))
                            if g:
                                own(i=i)
                                ve.wait_ge(*sc_t(("silu", name, c), i=i))
                                ve.scalar_tensor_tensor(out=dst, in0=dst, scalar=small[:, 14 + c:15 + c],
                                                        in1=tmp[c][:, 0:T], op0=ALU.add, op1=ALU.mult)\
                                  .then_inc(*ve_t.tick(("hidden", name, c)))

            ve.wait_ge(*pe_t("parameters"))
            ve.tensor_copy(pv[:, 0:NPV], ps[:, 7, 0:NPV]).then_inc(*ve_t.tick("parameters"))
            for j in range(DC):
                ve.wait_ge(*pe_t(("x", j)))
                ve.tensor_copy(xT[:, j, :], bank(j)).then_inc(*ve_t.tick(("x", "attn", j)))
                if j >= 1:
                    low("attn", lambda j: pcol("attn", j), j - 1)
            low("attn", lambda j: pcol("attn", j), DC - 1)
            root("attn")
            for n in range(8):
                ve.wait_ge(consumed, Unit(U_DQK + n // 2).began + 4 * (n % 2) + 4)
                ve.scalar_tensor_tensor(out=dqk[:, n, :], in0=bank(n % 4), scalar=0.125 if n < 4 else 1.0, in1=rb[:, :],
                                        op0=ALU.mult, op1=ALU.mult).then_inc(*ve_t.tick(("dqk", n)))
            root_column("attn")
            ve.wait_ge(lambda_in, 64)
            for k in range(2):
                mul(lamb[:, P * k:P * k + 64], lamb[:, P * k:P * k + 64], lamb[:, P * k + 64:P * k + P], ("lambda", k))
            own()
            ve.tensor_reduce(small[:, 20:22], lamb[:, :].rearrange("p (k d) -> p k d", k=2)[:, :, 0:64], AX, ALU.add)\
              .then_inc(*ve_t.tick("lambda sums"))
            for u in range(2):
                for t in range(NT):
                    ve.wait_ge(consumed, Unit(U_DV + u).began + 2 * t + 2)
                    ve.tensor_scalar(dv[:, t, COLS * u:COLS * u + COLS], ps[:, t, COLS * u:COLS * u + COLS],
                                     rcol[:, t:t + 1], None, ALU.mult).then_inc(*ve_t.tick(("dv", u, t)))
            ve.wait_ge(*sc_t("lambda"))
            mul(small[:, 24:25], small[:, 23:24], small[:, 22:23], "minus lambda", ALU.subtract)
            own()
            ve.tensor_scalar(small[:, 25:26], small[:, 24:25], -LAM_INIT, None, ALU.add).then_inc(*ve_t.tick("- lambda"))
            own()

            def scores(dst, src, t, label):
                n, o = P * (t + 1), P * t
                if t:
                    ve.tensor_copy(dst[:, 0:o], src[:, 0:o]).then_inc(*ve_t.tick((label, "copy")))
                mul(dst[:, o:n], src[:, o:n], causal, label, ALU.add)

            for slot_n in range(DN + 3):
                n = slot_n
                if n < DN:
                    t, s0 = n // 4, 26 + 8 * (n % 2)
                    if n >= 3:
                        ve.wait_ge(*pe_t(("diff turned", n - 3)))
                    for c in range(2):
                        ve.wait_ge(*pe_t(("diff scores", n, c)))
                        scores(dmap(n, c), bank(2 * (n % 2) + c), t, ("diff scores", n, c))
                    for c in range(2):
                        ve.wait_ge(*ve_t(("diff scores", n, c)))
                        ve.tensor_reduce(small[:, s0 + c:s0 + c + 1], dmap(n, c)[:, 0:P * (t + 1)], AX, ALU.max,
                                         negate=True).then_inc(*ve_t.tick(("diff max", n, c)))
                n = slot_n - 1
                if 0 <= n < DN:
                    w, s0 = P * (n // 4 + 1), 26 + 8 * (n % 2)
                    ve.wait_ge(*sc_t(("diff exp", n, 1)))
                    ve.reciprocal(small[:, s0 + 4:s0 + 6], small[:, s0 + 2:s0 + 4]).then_inc(*ve_t.tick(("diff inverse", n)))
                    own()
                    mul(small[:, s0 + 6:s0 + 7], small[:, s0 + 5:s0 + 6], small[:, 25:26], ("diff share", n))
                    x = dmap(n, 0)[:, 0:w]
                    ve.tensor_scalar(x, x, small[:, s0 + 4:s0 + 5], None, ALU.mult).then_inc(*ve_t.tick(("diff first", n)))
                    own()
                    ve.scalar_tensor_tensor(out=x, in0=dmap(n, 1)[:, 0:w], scalar=small[:, s0 + 6:s0 + 7], in1=x,
                                            op0=ALU.mult, op1=ALU.add).then_inc(*ve_t.tick(("diff weights", n)))
                    own()
                n = slot_n - 3
                if 0 <= n < DN:
                    t, h = divmod(n, 4)
                    ve.wait_ge(*pe_t(("diff out", n)))
                    ve.tensor_copy(osum[:, h, P * t:P * t + P], ps[:, 6 + n % 2, 0:P]).then_inc(*ve_t.tick(("diff out", n)))
            dr = [tmp[2][:, 0:T], tmp[3][:, 0:T], tmp[4][:, 0:T], dx[0][:, :]]
            for h in range(4):
                ve.wait_ge(*pe_t(("diff mean", h)))
                ve.tensor_scalar(dr[h], bank(4 + h % 2), 1.0 / P, EPS, ALU.mult, ALU.add).then_inc(*ve_t.tick(("diff mean", h)))
            for h in range(4):
                ve.wait_ge(*sc_t(("diff sqrt", h)))
                ve.reciprocal(dr[h], dr[h]).then_inc(*ve_t.tick(("diff root", h)))
                own()
                ve.scalar_tensor_tensor(out=osum[:, h, :], in0=osum[:, h, :], scalar=pcol("diffn", 0),
                                        in1=dr[h], op0=ALU.mult, op1=ALU.mult).then_inc(*ve_t.tick(("diff normed", h)))
            for h in range(4):
                ve.wait_ge(*sc_t(("diff high", h)))
                ve.wait_ge(*ve_t(("diff normed", h)))
                ve.scalar_tensor_tensor(out=molo[:, 8 + h, :], in0=osum[:, h, :], scalar=1.0 - LAM_INIT,
                                        in1=mohi[:, 8 + h, :].bitcast(F32), op0=ALU.mult, op1=ALU.subtract)\
                  .then_inc(*ve_t.tick(("diff low", h)))
            own()
            for c in range(2):
                for e in range(2):
                    ve.memset(bbd[c][64 * e:64 * e + 64, :, 16 * (1 - e):16 * (1 - e) + 16], 0.0)\
                      .then_inc(*ve_t.tick(("zero b", c, e)))
            for n in range(4):
                ve.wait_ge(consumed, Unit(U_SU + n // 2).began + 4 * (n % 2) + 4)
                mul(su[:, n, :], bank(n), rb[:, :], ("su", n))
            ve.wait_ge(*pe_t("s5 params"))
            ve.tensor_scalar(slot(0), ps[:, 4, 0:16], -1e-4, None, ALU.min).then_inc(*ve_t.tick("s5 lr"))
            ve.tensor_copy(slots(1, 3), ps[:, 4, 16:48]).then_inc(*ve_t.tick("s5 li dt"))
            own()
            mul(slot(3), slot(0), slot(2), "s5 zr")
            mul(slot(4), slot(1), slot(2), "s5 zi")
            own()
            ve.tensor_scalar(slot(9), slot(4), 1.0 / (2 * np.pi), ROUND, ALU.mult, ALU.add).then_inc(*ve_t.tick("turns"))
            own()
            ve.tensor_scalar(slot(9), slot(9), -ROUND, None, ALU.add).then_inc(*ve_t.tick("whole turns"))
            own()
            for n, part in enumerate(TWO_PI):
                ve.scalar_tensor_tensor(out=slot(4), in0=slot(9), scalar=-part, in1=slot(4), op0=ALU.mult, op1=ALU.add)\
                  .then_inc(*ve_t.tick(("phase", n)))
                own()
            ve.tensor_scalar(slot(6), slot(4), 3.1415925, -3.1415925, ALU.min, ALU.max).then_inc(*ve_t.tick("s5 phase"))
            for c in range(2):
                ve.wait_ge(*po_t(("zero c", c)))
                for e in range(2):
                    r = slice(64 * e, 64 * e + 64)
                    ve.tensor_scalar(cbd[c][r, :, 16 * e:16 * e + 16],
                                     ps[r, 5, 256 * c:256 * c + 256].rearrange("p (b h) -> p b h", h=16),
                                     -1.0 if c else 1.0, None, ALU.mult).then_inc(*ve_t.tick(("s5 c", c, e)))
            ve.wait_ge(*sc_t("s5 half sin"))
            mul(slot(8), slot(8), slot(8), "s5 sin2")
            own()
            ve.tensor_scalar(slot(8), slot(8), -2.0, 1.0, ALU.mult, ALU.add).then_inc(*ve_t.tick("s5 cos"))
            ve.memset(pw[0][:, 0, :], 1.0).then_inc(*ve_t.tick("s5 one"))
            ve.memset(pw[1][:, 0, :], 0.0).then_inc(*ve_t.tick("s5 zero"))
            own()
            mul(pw[0][:, 1, :], slot(5), slot(8), "s5 p1r")
            mul(pw[1][:, 1, :], slot(5), slot(7), "s5 p1i")
            own()

            def cmul(dst, a, b, label, s=(40, 41), n=1, dims=None):
                t0, t1 = (slots(x, x + n) if dims is None else slots(x, x + n).rearrange(dims[0], **dims[1])
                          for x in (s[0], s[0] + n))
                mul(t0, a[0], b[0], (label, 0))
                mul(t1, a[1], b[1], (label, 1))
                own()
                mul(t0, t0, t1, (label, 2), ALU.subtract)
                own()
                mul(t1, a[0], b[1], (label, 3))
                t2 = slots(s[0] + 2 * n, s[0] + 3 * n)
                t2 = t2 if dims is None else t2.rearrange(dims[0], **dims[1])
                mul(t2, a[1], b[0], (label, 4))
                own()
                mul(dst[1], t1, t2, (label, 5), ALU.add)
                ve.tensor_copy(dst[0], t0).then_inc(*ve_t.tick((label, 6)))
                own()

            def powers(a, b):
                return [pw[c][:, a:b, :] for c in range(2)]

            for m in (1, 2, 4):
                cmul(powers(m + 1, 2 * m + 1), powers(1, m + 1),
                     [pw[c][:, m:m + 1, :].to_broadcast([P, m, PAIRS]) for c in range(2)], ("s5 power", m), n=m,
                     dims=("p (m b) -> p m b", {"m": m}))
            for k in range(6):
                if k == 0:
                    for c in range(2):
                        ve.tensor_copy(lvp[c][:, 0, :], pw[c][:, STEP, :]).then_inc(*ve_t.tick(("s5 level", 0, c)))
                    own()
                else:
                    cmul([lvp[c][:, k, :] for c in range(2)], [lvp[c][:, k - 1, :] for c in range(2)],
                         [lvp[c][:, k - 1, :] for c in range(2)], ("s5 level", k))
            ve.tensor_scalar(slot(10), pw[0][:, 1, :], -1.0, None, ALU.add).then_inc(*ve_t.tick("s5 nr"))
            mul(slot(14), slot(0), slot(0), "s5 lr2")
            mul(slot(15), slot(1), slot(1), "s5 li2")
            own()
            mul(slot(14), slot(14), slot(15), "s5 l2", ALU.add)
            own()
            ve.reciprocal(slot(14), slot(14)).then_inc(*ve_t.tick("s5 1/l2"))
            mul(slot(12), slot(10), slot(0), "s5 w0")
            mul(slot(13), pw[1][:, 1, :], slot(1), "s5 w1")
            mul(slot(15), pw[1][:, 1, :], slot(0), "s5 w2")
            mul(slot(16), slot(10), slot(1), "s5 w3")
            own()
            mul(slot(12), slot(12), slot(13), "s5 w4", ALU.add)
            mul(slot(15), slot(15), slot(16), "s5 w5", ALU.subtract)
            own()
            mul(slot(12), slot(12), slot(14), "s5 w6")
            mul(slot(13), slot(15), slot(14), "s5 w7")
            own()

            def wide(x):
                return x.unsqueeze(2).to_broadcast([P, PAIRS, 32])

            def flat(x):
                return x[:, 0:T].rearrange("p (b h) -> p b h", h=32)

            t4, t5 = flat(tmp[4]), flat(tmp[5])
            B, w_ = [bbd[c][:, :, :] for c in range(2)], [slot(12), slot(13)]
            mul(t4, B[0], wide(w_[0]), "bb0")
            mul(t5, B[1], wide(w_[1]), "bb1")
            own()
            mul(t4, t4, t5, "bb2", ALU.subtract)
            own()
            mul(t5, B[0], wide(w_[1]), "bb3")
            mul(B[1], B[1], wide(w_[0]), "bb4")
            own()
            mul(B[1], B[1], t5, "bb5", ALU.add)
            ve.tensor_copy(B[0], t4).then_inc(*ve_t.tick("s5 bbar"))
            own()
            for j in range(STEP):
                m = STEP - 1 - j
                if j >= 2:
                    ve.wait_ge(*pe_t(("s5 wbt", 4 * (j - 2) + 3)))
                if j:
                    own()
                Pr, Pi = (wide(pw[c][:, m, :]) for c in range(2))
                t0, t1 = flat(tmp[0]), flat(tmp[1])
                mul(t0, B[0], Pr, ("wb", j, 0))
                mul(t1, B[1], Pi, ("wb", j, 1))
                own()
                mul(wbj(0, j).rearrange("p (b h) -> p b h", h=32), t0, t1, ("wb", j, 2), ALU.subtract)
                own()
                mul(t0, B[0], Pi, ("wb", j, 3))
                mul(t1, B[1], Pr, ("wb", j, 4))
                own()
                mul(wbj(1, j).rearrange("p (b h) -> p b h", h=32), t0, t1, ("s5 wb", j), ALU.add)
            ve.wait_ge(*pe_t(("s5 add", 4 * STEP - 1)))
            for c in range(2):
                for b in range(4):
                    ve.tensor_copy(st[c][:, b:PAIRS:4, :],
                                   ps[:, 4 + b, 256 * c:256 * c + 256].rearrange("p (q n) -> p q n", q=4))\
                      .then_inc(*ve_t.tick(("s5 moved", c, b)))
            own()
            for k in range(6):
                d = 1 << k
                for half in range(2):
                    hp = slice(8 * half, 8 * half + 8)
                    w = NSTEP - d
                    tt = [tmp[x][:, 0:8 * w].rearrange("p (b n) -> p b n", b=8) for x in range(4)]
                    ar, ai = (lvp[c][:, k, hp].unsqueeze(2).to_broadcast([P, 8, w]) for c in range(2))
                    Sr, Si = (st[c][:, hp, 0:w] for c in range(2))
                    mul(tt[0], Sr, ar, ("scan", k, half, 0))
                    mul(tt[1], Si, ai, ("scan", k, half, 1))
                    mul(tt[2], Si, ar, ("scan", k, half, 2))
                    mul(tt[3], Sr, ai, ("scan", k, half, 3))
                    own()
                    mul(tt[0], tt[0], tt[1], ("scan", k, half, 4), ALU.subtract)
                    mul(tt[2], tt[2], tt[3], ("scan", k, half, 5), ALU.add)
                    own()
                    for c in range(2):
                        mul(st[c][:, hp, d:NSTEP], st[c][:, hp, d:NSTEP], tt[2 * c], ("scan", k, half, 6 + c), ALU.add)
                    own()
            ve.memset(small[:, 89:90], 0.0).then_inc(*ve_t.tick("s5 scanned"))
            ve.wait_ge(*po_t(("s5 cp", 1)))
            for q in range(2, 5):
                ve.wait_ge(*pe_t(("s5 y", q - 2)))
                ve.scalar_tensor_tensor(out=su[:, q - 2, :], in0=su[:, q - 2, :], scalar=pcol("s5d", q - 2),
                                        in1=bank((q - 2) % 2), op0=ALU.mult, op1=ALU.add)\
                  .then_inc(*ve_t.tick(("s5 y", q - 2)))
                for b in range(4 if q < 4 else 0):
                    Cr, Ci, Pr, Pi = cp_factors(q, b)
                    t4, t5, t3, t2 = (tmp[x][:, 0:288].rearrange("p (t h) -> p t h", h=32) for x in (4, 5, 3, 2))
                    mul(t4, Cr, Pr, ("cp", q, b, 0))
                    mul(t5, Ci, Pi, ("cp", q, b, 1))
                    mul(t3, Ci, Pr, ("cp", q, b, 2))
                    mul(t2, Cr, Pi, ("cp", q, b, 3))
                    own()
                    mul(s5_cp(q)[0][:, b, :, :], t4, t5, ("cp", q, b, 4), ALU.add)
                    mul(s5_cp(q)[1][:, b, :, :], t3, t2, ("s5 cp", q) if b == 3 else ("cp", q, b, 5), ALU.subtract)
                    own()
            ve.wait_ge(*pe_t(("s5 y", 3)))
            ve.scalar_tensor_tensor(out=su[:, 3, :], in0=su[:, 3, :], scalar=pcol("s5d", 3), in1=bank(1),
                                    op0=ALU.mult, op1=ALU.add).then_inc(*ve_t.tick(("s5 y", 3)))
            for q in range(4):
                ve.wait_ge(*sc_t(("s5 high", q)))
                mul(molo[:, 4 + q, :], su[:, q, :], mohi[:, 4 + q, :].bitcast(F32), ("s5 gelu low", q), ALU.subtract)
            for j in range(4):
                ve.wait_ge(*sc_t(("s5 sigmoid", j)))
                mul(su[:, j, :], su[:, j, :], tmp[j][:, 0:T], ("s5 gated", j))
                own()
                mul(tmp[5 if j else 4][:, 0:T], su[:, j, :], su[:, j, :], ("s5 sq", j))
                if j:
                    own()
                    mul(tmp[4][:, 0:T], tmp[4][:, 0:T], tmp[5][:, 0:T], "s5 squares" if j == 3 else ("s5 sum", j), ALU.add)
                    own()
            ve.wait_ge(*pe_t("s5 mean"))
            mean("s5 mean", 512, tmp[5][:, 0:T], bank(7), EPS, "s5 sqrt")
            for j in range(4):
                ve.scalar_tensor_tensor(out=su[:, j, :], in0=su[:, j, :], scalar=pcol("s5n", j), in1=tmp[5][:, 0:T],
                                        op0=ALU.mult, op1=ALU.mult).then_inc(*ve_t.tick(("s5 out", j)))
            for j in range(4):
                ve.wait_ge(*sc_t(("s5 out high", j)))
                mul(molo[:, 4 + j, :], su[:, j, :], mohi[:, 4 + j, :].bitcast(F32), ("s5 out low", j), ALU.subtract)
            own()
            ve.memset(zg[:, 0:12, 0:3], 0.0).then_inc(*ve_t.tick("zg pad"))
            own()

            def qk_mean(n):
                ve.wait_ge(*pe_t(("qk mean", n)))
                ve.tensor_scalar(tmp[4 + n % 2][:, 0:T], bank(5 + n % 2), EPS, None, ALU.add)\
                  .then_inc(*ve_t.tick(("qk mean", n)))

            def qk_norm(n):
                ve.wait_ge(*sc_t(("qk sqrt", n)))
                ve.reciprocal(tmp[4 + n % 2][:, 0:T], tmp[4 + n % 2][:, 0:T]).then_inc(*ve_t.tick(("qk root", n)))
                own()
                ve.scalar_tensor_tensor(out=zg[:, n, 3:T + 3], in0=zg[:, n, 3:T + 3],
                                        scalar=GD ** -0.5 if n < 4 else 1.0, in1=tmp[4 + n % 2][:, 0:T], op0=ALU.mult,
                                        op1=ALU.mult).then_inc(*ve_t.tick(("qk normed", n)))
                own()

            for n in range(16):
                ve.wait_ge(consumed, Unit(U_G + n // 2).began + 4 * (n % 2) + 4)
                mul(zg[:, n, 3:T + 3], bank(n % 4), rb[:, :], ("zg", n))
                own()
                if 5 <= n < 9:
                    for k in (2 * n - 10, 2 * n - 9):
                        if k >= 2:
                            qk_norm(k - 2)
                        qk_mean(k)
                if n == 9:
                    qk_norm(6)
                    qk_norm(7)
                if n == 10:
                    ve.wait_ge(*sc_t("gate high"))
                    mul(bal[:, :, :], baw[:, :, :], bah[:, :, :].bitcast(F32), "gate weights", ALU.subtract)
                if n >= 12:
                    continue
                dst = tmp[2 + n % 2][:, 0:T]
                if n >= 2:
                    ve.wait_ge(*sc_t(("conv silu", n - 2)))
                for k in range(4):
                    w = pcol("gconv", 12 * k + n)
                    if k == 0:
                        ve.tensor_scalar(dst, zg[:, n, 0:T], w, None, ALU.mult).then_inc(*ve_t.tick(("gtap", n, 0)))
                    else:
                        own()
                        ve.scalar_tensor_tensor(out=dst, in0=zg[:, n, k:T + k], scalar=w, in1=dst, op0=ALU.mult,
                                                op1=ALU.add).then_inc(*ve_t.tick(("conv", n) if k == 3 else ("gtap", n, k)))
            ve.wait_ge(*pe_t("gates"))
            for t in range(NT):
                ve.tensor_scalar(small[:, 8 * t:8 * t + 8], ps[:, 4, 8 * t:8 * t + 8], rcol[:, t:t + 1], None, ALU.mult)\
                  .then_inc(*ve_t.tick(("ba", t)))
            own()
            sm = small[:, 0:32].rearrange("p (t c) -> p t c", c=8)
            x16 = small[:, 32:48].rearrange("p (t c) -> p t c", c=4)
            mul(x16, sm[:, :, 4:8], gates[:, 52:56].unsqueeze(1).to_broadcast([P, 4, 4]), "gate x", ALU.add)
            own()
            ve.scalar_tensor_tensor(out=small[:, 48:64], in0=small[:, 32:48], scalar=-1.0, in1=small[:, 32:48],
                                    op0=ALU.mult, op1=ALU.max).then_inc(*ve_t.tick("gate size"))
            ve.wait_ge(*sc_t("gate ln"))
            ve.scalar_tensor_tensor(out=small[:, 32:48], in0=small[:, 32:48], scalar=0.0, in1=small[:, 48:64],
                                    op0=ALU.max, op1=ALU.add).then_inc(*ve_t.tick("softplus"))
            own()
            ve.scalar_tensor_tensor(out=gates[:, 16:32].rearrange("p (t c) -> p t c", c=4), in0=x16, scalar=-1.0,
                                    in1=gates[:, 48:52].unsqueeze(1).to_broadcast([P, 4, 4]), op0=ALU.mult,
                                    op1=ALU.mult).then_inc(*ve_t.tick("log decay"))
            ve.wait_ge(*pe_t("cumulated"))
            ve.tensor_copy(gates[:, 32:48], ps[:, 4, 64:80]).then_inc(*ve_t.tick("cumulated"))
            ve.memset(tmp[5][:, 0:T], 0.0).then_inc(*ve_t.tick("state 0"))
            own()
            kb, qb, gcR, beR, decT, LT, atT, CT, Dm, DT, X, kTok, vbT, kbe, kl, nwT = gb
            vn, qe, S = tmp[3], tmp[4], tmp[5]

            def heads(x):
                return x[:, 0:T].rearrange("p (h t) -> p h t", h=GH)

            def per_head(c):
                return small[:, c:c + 4].unsqueeze(2).to_broadcast([P, GH, P])

            def mask(m):
                return m.unsqueeze(1).to_broadcast([P, GH, P])

            with loop(book, "ve", "blk", ve, "b", NT) as b:
                ve.tensor_copy(gates[:, 56:60], gates[:, ds(b * 4 + 16, 4)]).then_inc(*ve_t.tick("col g"))
                ve.tensor_copy(gates[:, 60:64], gates[:, ds(b * 4, 4)]).then_inc(*ve_t.tick("col beta"))
                ve.tensor_copy(small[:, 64:68], gates[:, ds(b * 4 + 32, 4)]).then_inc(*ve_t.tick("columns"))
                ve.wait_ge(*pe_t("row forms", b=b))
                ve.tensor_copy(beR[:, :], bank(1)).then_inc(*ve_t.tick("beta rows"))
                ve.tensor_copy(gcR[:, :], bank(0)).then_inc(*ve_t.tick("row forms"))
                own(b=b)
                mul(small[:, 76:80], heads(gcR)[:, :, P - 1], small[:, 64:68], "to last", ALU.subtract)
                for h in range(GH):
                    ve.tensor_scalar(decT[:, P * h:P * h + P], gcR[:, P * h:P * h + P], small[:, 64 + h:65 + h], 0.0,
                                     ALU.subtract, ALU.min).then_inc(*ve_t.tick("decay" if h == 3 else ("decay", h)))
                ve.wait_ge(*sc_t("decay", b=b))
                mul(heads(decT), heads(decT), mask(tri), "decay masked")
                ve.wait_ge(*pe_t("kk", b=b))
                own(b=b)
                mul(LT[:, :], bank(2), decT[:, :], "L0")
                own(b=b)
                mul(heads(LT), heads(LT), mask(strict), "L1")
                own(b=b)
                mul(LT[:, :], LT[:, :], beR[:, :], "L2")
                mul(atT[:, :], bank(3), decT[:, :], "kk used")
                own(b=b)

                def level(s, g):
                    mul(pair(CT, g), pair(LT, g), lvl[:, s, :].unsqueeze(1).to_broadcast([P, 2, P]), ("level", s, g))

                def pair(x, g):
                    return x[:, 2 * P * g:2 * P * g + 2 * P].rearrange("p (h t) -> p h t", h=2)

                for g in range(2):
                    level(0, g)
                for g in range(2):
                    ve.wait_ge(*pe_t(("X", 0, g), b=b))
                    eye = ident.unsqueeze(1).to_broadcast([P, 2, P])
                    ve.wait_ge(*ve_t(("level", 0, g), b=b))
                    mul(pair(Dm, g), eye, pair(bank(6 + g), g), ("D", 0, g), ALU.subtract)
                    mul(pair(DT, g), eye, pair(CT, g), ("DT", 0, g), ALU.subtract)
                    own(b=b)
                    level(1, g)
                ve.wait_ge(*pe_t("turned", b=b))
                ve.wait_ge(*sc_t("kTok", b=b))
                mul(small[:, 72:76], small[:, 68:72], gates[:, 60:64], "beta exp g")
                mul(heads(vbT), heads(bank(5)), gates[:, 60:64].unsqueeze(2).to_broadcast([P, GH, P]), "vb")
                own(b=b)
                mul(heads(kbe), heads(kTok), per_head(72), "kbe")
                mul(heads(kl), heads(kTok), per_head(76), "kl0")
                ve.wait_ge(*sc_t("exp rows", b=b))
                ve.wait_ge(*sc_t("blocks", b=b))
                mul(qe[:, 0:T], qb[:, :], tmp[0][:, 0:T], "kl")
                for s in range(1, 7):
                    for g in range(2):
                        ve.wait_ge(*pe_t(("DD", s, g), b=b))
                        mul(pair(DT, g), pair(DT, g), pair(bank(2 * g + 1), g), ("DT", s, g), ALU.subtract)
                        if s < 6:
                            mul(pair(Dm, g), pair(Dm, g), pair(bank(2 * g), g), ("D", s, g), ALU.subtract)
                            level(s + 1, g)
                own(b=b)
                ve.wait_ge(*pe_t("v new", b=b))
                ve.tensor_copy(vn[:, 0:T], bank(3)).then_inc(*ve_t.tick("v new"))
                ve.wait_ge(*pe_t("delta out", b=b))
                ve.tensor_scalar(zg[:, 0:4, ds(b * P + 3, P)], heads(bank(4)), 1.0, None, ALU.mult)\
                  .then_inc(*ve_t.tick("delta out"))
                for h in range(GH):
                    hs = slice(P * h, P * h + P)
                    ve.scalar_tensor_tensor(out=S[:, hs], in0=S[:, hs], scalar=tmp[0][:, P * h + P - 1:P * h + P],
                                            in1=ps[:, 5, hs], op0=ALU.mult, op1=ALU.add)\
                      .then_inc(*ve_t.tick("state" if h == 3 else ("state", h)))
                own(b=b)
            for h in range(GH):
                ve.wait_ge(*pe_t(("delta mean", h)))
                ve.tensor_scalar(tmp[2 + h][:, 0:T], bank((6 + h) % 8), 1.0 / GD, EPS, ALU.mult, ALU.add)\
                  .then_inc(*ve_t.tick(("delta mean", h)))
            for h in range(GH):
                r, o = tmp[2 + h][:, 0:T], zg[:, h, 3:T + 3]
                ve.wait_ge(*sc_t(("delta sqrt", h)))
                ve.reciprocal(r, r).then_inc(*ve_t.tick(("delta inverse", h)))
                own()
                ve.scalar_tensor_tensor(out=o, in0=o, scalar=pcol("gdnn", 0), in1=r, op0=ALU.mult, op1=ALU.mult)\
                  .then_inc(*ve_t.tick(("delta root", h)))
                own()
                mul(o, o, zg[:, 12 + h, 3:T + 3], ("delta normed", h))
                ve.wait_ge(*sc_t(("delta high", h)))
                own()
                mul(molo[:, h, :], o, mohi[:, h, :].bitcast(F32), ("delta low", h), ALU.subtract)
            residual("ffn", Unit(U_WO + 5), 1.0, lambda j: pcol("ffn", j))
            root("ffn")
            conv_gated(U_UP, "f0")
            residual("fin1", Unit(U_DN + 10), 1.0, None)
            root("fin1")
            for j in range(DC):
                ve.scalar_tensor_tensor(out=xT[:, j, :], in0=xT[:, j, :], scalar=pcol("fin1", j), in1=rb[:, :],
                                        op0=ALU.mult, op1=ALU.mult).then_inc(*ve_t.tick(("fin1", j)))
            own()

            with loop(book, "ve", "layer", ve, "layer", LAYERS) as l:
                at = {"layer": l}

                def p_(label):
                    return pe_t(label, layer=l)

                def s_(label):
                    return sc_t(label, layer=l)

                ve.tensor_copy(lv[:, :], pv[:, ds(l * LW + PV["layer"], LW)]).then_inc(*ve_t.tick("layer columns"))
                own(**at)
                for j in range(DC):
                    ve.memset(small[:, 80 + j:81 + j], 0.0).then_inc(*ve_t.tick(("x", "n1", j)))
                for j in range(DC):
                    low("n1", lambda j: lv[:, j:j + 1], j, **at)
                root("n1", wait=False, **at)
                gated(V_UP1, "f1", "n1", l)
                residual("nm", Unit(V_DN1 + 10, l), 0.5, lambda j: lv[:, 8 + j:9 + j], **at)
                root("nm", **at)

                def z_rows(a, b):
                    for n in range(a, b):
                        ve.wait_ge(consumed, Unit(V_WIN + n // 2, l).began + 4 * (n % 2) + 4)
                        ve.scalar_tensor_tensor(out=z2[:, n, :], in0=bank(n % 4), scalar=0.125 if 6 <= n < 9 else 1.0,
                                                in1=rb[:, :], op0=ALU.mult, op1=ALU.mult).then_inc(*ve_t.tick(("z", n)))

                def vf_rows(u, t):
                    c = slice(COLS * u, COLS if u == 0 else VF)
                    ve.wait_ge(consumed, Unit(V_WIN + 6 + u, l).began + 2 * t + 2)
                    ve.tensor_scalar(vf[:, t, c], ps[:, t, c], rcol[:, t:t + 1], None, ALU.mult)\
                      .then_inc(*ve_t.tick(("vf", u, t)))

                def pool(k):
                    z, src, d = z2[:, 4 + k, :], z2[:, 4 + k, :], 1
                    for n in range(2 + 2 * k):
                        dst = tmp[3 + n % 2][:, 0:T]
                        own(**at)
                        ve.tensor_copy(dst[:, 0:d], src[:, 0:d]).then_inc(*ve_t.tick(("pool", k, n, 0)))
                        mul(dst[:, d:T], src[:, d:T], src[:, 0:T - d], ("pool", k, n, 1), ALU.add)
                        src, d = dst, 2 * d
                    own(**at)
                    for g in range(2):
                        r = slice(64 * g, 64 * g + 64)
                        w = tmp[3 + g][r, 0:T]
                        mul(w, w, poolt[r, k, :], ("pool mean", k, g))
                        own(**at)
                        mul(z[r, :], w, z[r, :], "pooled" if k and g else ("pooled", k, g), ALU.subtract)

                def mla_rope(h):
                    ve.wait_ge(*p_(("mla q turned", h)))
                    own(**at)
                    mul(tmp[3][0:QD, 0:T], ps[0:QD, 5, :], ropet[0:QD, 1, :], ("mla sin", h))
                    mul(qf[0:QD, h, :], qf[0:QD, h, :], ropet[0:QD, 0, :], ("mla cos", h))
                    own(**at)
                    mul(qf[0:QD, h, :], qf[0:QD, h, :], tmp[3][0:QD, 0:T], ("mla q", h), ALU.add)

                z_rows(0, 4)
                root_column("nm", **at)
                for g in range(2):
                    ve.memset(poolw[HD * g:HD * g + HD, :, HD - HD * g:P - HD * g], 0.0).then_inc(*ve_t.tick(("pool zero", g)))
                z_rows(4, 6)
                ve.wait_ge(*p_("q_a mean"))
                ve.tensor_scalar(tmp[3][:, 0:T], bank(4), 1.0 / 256, EPS, ALU.mult, ALU.add).then_inc(*ve_t.tick("q_a mean"))
                ve.wait_ge(*p_("kv_a mean"))
                ve.tensor_scalar(tmp[4][:, 0:T], bank(5), 1.0 / 128, EPS, ALU.mult, ALU.add).then_inc(*ve_t.tick("mla means"))
                for n in range(2):
                    ve.wait_ge(*s_(("mla sqrt", n)))
                    ve.reciprocal(tmp[3 + n][:, 0:T], tmp[3 + n][:, 0:T]).then_inc(*ve_t.tick(("mla root", n)))
                own(**at)
                for n in range(3):
                    ve.scalar_tensor_tensor(out=z2[:, n, :], in0=z2[:, n, :], scalar=lv[:, 24 + n:25 + n],
                                            in1=tmp[3 + n // 2][:, 0:T], op0=ALU.mult, op1=ALU.mult)\
                      .then_inc(*ve_t.tick("kv_a" if n == 2 else ("q_a", n)))
                ve.wait_ge(layer_in, l * 128 + 128)
                z_rows(6, 8)
                pool(0)
                z_rows(8, 10)
                pool(1)
                z_rows(10, 12)
                ve.wait_ge(*p_("pool out"))
                for k in range(2):
                    ve.tensor_scalar(z2[:, 4 + k, :], bank(7 - 2 * k), lv[:, 27 + k:28 + k], None, ALU.mult)\
                      .then_inc(*ve_t.tick(("pool out", k)))
                for u in range(2):
                    for t in range(NT):
                        vf_rows(u, t)
                        if NT * u + t < HEADS:
                            mla_rope(NT * u + t)
                ve.wait_ge(*p_("k rope"))
                own(**at)
                kr = slice(HD, QD)
                mul(tmp[3][kr, 0:T], ps[kr, 7, :], ropet[kr, 1, :], "k sin")
                mul(z2[kr, 3, :], z2[kr, 3, :], ropet[kr, 0, :], "k cos")
                own(**at)
                mul(z2[kr, 3, :], z2[kr, 3, :], tmp[3][kr, 0:T], "k rope", ALU.add)
                x24 = small[:, 0:24].rearrange("p (t h) -> p t h", h=HEADS)
                mul(x24, vf[:, :, 384:390], small[:, 64:70].unsqueeze(1).to_broadcast([P, NT, HEADS]), "f x", ALU.add)
                own(**at)
                ve.scalar_tensor_tensor(out=small[:, 24:48], in0=small[:, 0:24], scalar=-1.0, in1=small[:, 0:24],
                                        op0=ALU.mult, op1=ALU.max).then_inc(*ve_t.tick("f size"))
                ve.tensor_copy(kf[kr, :, :], z2[kr, 3:4, :].to_broadcast([ROPE, HEADS, T])).then_inc(*ve_t.tick("kf"))
                for t in range(NT):
                    ve.wait_ge(*p_(("mla v", t)))
                    ve.tensor_copy(mv[:, t, :], ps[:, t, 0:HEADS * HD]).then_inc(*ve_t.tick(("mla v", t)))
                ve.wait_ge(*s_("f ln"))
                ve.scalar_tensor_tensor(out=small[:, 0:24], in0=small[:, 0:24], scalar=0.0, in1=small[:, 24:48],
                                        op0=ALU.min, op1=ALU.subtract).then_inc(*ve_t.tick("log f"))
                ve.wait_ge(*p_("fox sum"))
                ve.tensor_copy(small[:, 24:48], ps[:, 4, 0:24]).then_inc(*ve_t.tick("fox columns"))
                for k in range(2):
                    ve.wait_ge(*s_(("pool high", k)))
                    own(**at)
                    mul(xlo[:, 3 + k, :], z2[:, 4 + k, :], xhi[:, 3 + k, :].bitcast(F32), ("pool low", k), ALU.subtract)

                for slot_n in range(AN + 4):
                    n = slot_n
                    if n < AN:
                        t, s = n % NT, asc(n)
                        w = P * (t + 1)
                        ve.wait_ge(*p_(("scores", n)))
                        if n >= 4:
                            ve.wait_ge(*p_(("turned", n - 4)))
                        if n >= AN // 2:
                            h = n // NT - HEADS
                            ve.wait_ge(*s_(("fox row", h)))
                            c = 24 + HEADS * t + h
                            ve.scalar_tensor_tensor(out=s[:, 0:w], in0=ps[:, SB[n % 3], 0:w], scalar=small[:, c:c + 1],
                                                    in1=arow(h)[:, 0:w], op0=ALU.add, op1=ALU.subtract)\
                              .then_inc(*ve_t.tick(("shift", n)))
                            own(**at)
                            mul(s[:, P * t:w], s[:, P * t:w], causal, ("scores", n), ALU.add)
                        else:
                            scores(s, ps[:, SB[n % 3], :], t, ("scores", n))
                        own(**at)
                        ve.tensor_reduce(small[:, 70 + n % 2:71 + n % 2], s[:, 0:w], AX, ALU.max, negate=True)\
                          .then_inc(*ve_t.tick(("max", n)))
                    n = slot_n - 1
                    if 0 <= n < AN:
                        s, c = asc(n)[:, 0:P * (n % NT + 1)], 74 + n % 2
                        ve.wait_ge(*s_(("exp", n)))
                        ve.reciprocal(small[:, c:c + 1], small[:, c - 2:c - 1]).then_inc(*ve_t.tick(("inverse", n)))
                        own(**at)
                        ve.tensor_scalar(s, s, small[:, c:c + 1], None, ALU.mult).then_inc(*ve_t.tick(("weights", n)))
                    n = slot_n - 4
                    if n >= 0 and n % 8 == 7:
                        ve.wait_ge(*s_(("high", n // 8)))
                        ch = CHUNKS[n // 8]
                        mul(xlo[:, ch, :], tmp[3][:, 0:T], xhi[:, ch, :].bitcast(F32), ("low", n // 8), ALU.subtract)
                        own(**at)
                    n = slot_n - 3
                    if 0 <= n < AN:
                        o = slice(64 * (n // NT % 2), 64 * (n // NT % 2) + 64)
                        ve.wait_ge(*p_(("out", n)))
                        ve.tensor_copy(tmp[3][o, P * (n % NT):P * (n % NT) + P], ps[o, OB[n % 2], 0:P])\
                          .then_inc(*ve_t.tick(("out", n)))
                residual("n2", Unit(V_WO + 3, l), 1.0, lambda j: lv[:, 16 + j:17 + j], **at)
                root("n2", wait=False, **at)
                gated(V_UP2, "f2", "n2", l)
                residual("end", Unit(V_DN2 + 10, l), 0.5, None)
                own(**at)
            root("fin2")
            for j in range(DC):
                ve.scalar_tensor_tensor(out=xT[:, j, :], in0=xT[:, j, :], scalar=pcol("fin2", j), in1=rb[:, :],
                                        op0=ALU.mult, op1=ALU.mult).then_inc(*ve_t.tick(("y", j)))
            for t in range(NT):
                for k in range(2):
                    ve.wait_ge(*pe_t(("out half", t, k)))
                    ve.tensor_copy(raw_out(t)[:, T * k:T * k + T], bank(k)).then_inc(*ve_t.tick(("out half", t, k)))


def constants():
    i, j = np.arange(P)[:, None], np.arange(P)[None, :]
    cst = np.stack([i == j, i <= j, i < j, np.where(j > i, NEG, 0.0), np.ones((P, P))], 1).astype(np.float32)
    lev = np.stack([(i // (2 * s) == j // (2 * s)) & (j // s % 2 == 1) & (i // s % 2 == 0)
                    for s in (1, 2, 4, 8, 16, 32, 64)], 1).astype(np.float32)
    half = ROPE // 2
    inv = np.float32(10000.0) ** (-np.arange(0, ROPE, 2, dtype=np.float32) / np.float32(ROPE))
    ang = np.arange(T, dtype=np.float32)[None, :] * inv[:, None].astype(np.float32)
    rope = np.zeros((QD, 2, T), np.float32)
    rope[0:HD, 0] = 1.0
    rope[HD:QD, 0] = np.tile(np.cos(ang.astype(np.float64)), (2, 1))
    rope[HD:QD, 1] = np.tile(np.sin(ang.astype(np.float64)), (2, 1))
    turn = np.zeros((QD, QD), np.float32)
    for k in range(half):
        turn[HD + half + k, HD + k] = -1.0
        turn[HD + k, HD + half + k] = 1.0
    counts = np.zeros((P, 2, T), np.float32)
    for g, w in enumerate((2, 4, 8, 16)):
        counts[64 * (g % 2):64 * (g % 2) + 64, g // 2] = 1.0 / np.minimum(np.arange(1, T + 1), w)
    return {"constants": cst, "levels": lev, "rope": rope, "turn": turn, "counts": counts}


def kernel(**inputs):
    import concourse.bacc as bacc
    from concourse.bass_utils import run_bass_kernel_spmd

    def program(known):
        nc = bacc.Bacc("TRN2", target_bir_lowering=False, num_devices=1)
        dram = {n: nc.dram_tensor(f"in_{n}", a.shape, F32, kind="ExternalInput").ap() for n, a in arrays.items()}
        out = nc.dram_tensor("out", (1, T, D), F32, kind="ExternalOutput").ap()
        book = Book(known)
        build(nc, dram, out, book)
        return nc, book

    arrays = {n: np.ascontiguousarray(a) for n, a in inputs.items()} | constants()
    _, counts = program(None)
    nc, _ = program(counts)
    r = run_bass_kernel_spmd(nc, [{f"in_{n}": a for n, a in arrays.items()}], core_ids=[0])
    return r.results[0]["out"]
```
